# Optimizing a Trainium2 kernel written in Bass

```python
import jax
import jax.numpy as jnp
from jax import lax
import numpy as np
import math

D_MODEL = 1024
BATCH = 1
SEQ = 512
DEPTH = 2

RET_HEADS = 4
RET_HEAD_DIM = D_MODEL // 2 // RET_HEADS
RET_VALUE_DIM = D_MODEL // 2 // RET_HEADS
RET_CHUNK = 128
RET_WIDTH = RET_HEADS * RET_VALUE_DIM
WIN_Q_HEADS = 8
WIN_KV_HEADS = 2
WIN_HEAD_DIM = D_MODEL // 2 // WIN_Q_HEADS
WINDOW = 128
WIN_BLOCK = WINDOW
WIN_WIDTH = WIN_Q_HEADS * WIN_HEAD_DIM
FOURIER_GROUPS = 4
ROPE_THETA = 10000.0
N_GROUPS = 4
EXPERTS_PER_GROUP = 8
N_EXPERTS = N_GROUPS * EXPERTS_PER_GROUP
TOP_K = 2
EXPERT_HIDDEN = D_MODEL // 2
LN_EPS = 1e-5
GN_EPS = 1e-6
DEEPNORM_ALPHA = (2.0 * DEPTH) ** 0.25
DEEPNORM_BETA = (8.0 * DEPTH) ** -0.25
N_EVEN = (DEPTH + 1) // 2
N_ODD = DEPTH // 2
RET_QK = RET_HEADS * RET_HEAD_DIM
WIN_KV = WIN_KV_HEADS * WIN_HEAD_DIM
EVEN_SPLITS = tuple(np.cumsum([RET_QK, RET_QK, RET_WIDTH, RET_WIDTH, WIN_WIDTH, WIN_KV])[:].tolist())
IN_EVEN = 2 * RET_QK + 2 * RET_WIDTH + WIN_WIDTH + 2 * WIN_KV


def layer_norm(x, gain, bias):
    xf = x.astype(jnp.float32)
    mu = jnp.mean(xf, axis=-1, keepdims=True)
    var = jnp.mean(jnp.square(xf - mu), axis=-1, keepdims=True)
    y = (xf - mu) * lax.rsqrt(var + LN_EPS) * gain.astype(jnp.float32) + bias.astype(jnp.float32)
    return y.astype(x.dtype)

def rope(x, pos):
    d = x.shape[-1]
    half = d // 2
    inv = ROPE_THETA ** (-jnp.arange(half, dtype=jnp.float32) / half)
    ang = pos.astype(jnp.float32)[:, None] * inv[None, :]
    cos = jnp.cos(ang)[None, :, None, :]
    sin = jnp.sin(ang)[None, :, None, :]
    xf = x.astype(jnp.float32)
    x1, x2 = xf[..., :half], xf[..., half:]
    return jnp.concatenate([x1 * cos - x2 * sin, x1 * sin + x2 * cos], axis=-1).astype(x.dtype)

def retention_one_direction(q, k, v, log_gamma, include_diag):
    B, H, S, dk = q.shape
    dv = v.shape[-1]
    C = RET_CHUNK
    NC = S // C
    qc = q.reshape(B, H, NC, C, dk)
    kc = k.reshape(B, H, NC, C, dk)
    vc = v.reshape(B, H, NC, C, dv)
    pos = jnp.arange(C, dtype=jnp.float32)
    lg = log_gamma[:, None, None]
    diff = pos[:, None] - pos[None, :]
    mask = diff >= 0 if include_diag else diff > 0
    dmat = jnp.where(mask[None], jnp.exp(lg * jnp.maximum(diff, 0.0)[None]), 0.0)
    scores = jnp.einsum('bhncd,bhnmd->bhncm', qc, kc) * dmat[None, :, None]
    y_inner = jnp.einsum('bhncm,bhnmv->bhncv', scores, vc)
    zeta = jnp.exp(log_gamma[:, None] * (C - 1.0 - pos)[None])
    kv = jnp.einsum('bhnmd,bhnmv->nbhdv', kc * zeta[None, :, None, :, None], vc)
    chunk_decay = jnp.exp(log_gamma * C)[None, :, None, None]

    def step(state, kv_n):
        return state * chunk_decay + kv_n, state

    _, r_prev = lax.scan(step, jnp.zeros((B, H, dk, dv), jnp.float32), kv)
    xi = jnp.exp(log_gamma[:, None] * (pos + 1.0)[None])
    y_cross = jnp.einsum('bhncd,nbhdv->bhncv', qc * xi[None, :, None, :, None], r_prev)
    return (y_inner + y_cross).reshape(B, H, S, dv)

def bidirectional_retention(q, k, v, decay_logit):
    qf = jnp.transpose(q.astype(jnp.float32), (0, 2, 1, 3))
    kf = jnp.transpose(k.astype(jnp.float32), (0, 2, 1, 3))
    vf = jnp.transpose(v.astype(jnp.float32), (0, 2, 1, 3))
    log_gamma = jax.nn.log_sigmoid(decay_logit.astype(jnp.float32))
    fwd = retention_one_direction(qf, kf, vf, log_gamma[0], True)
    bwd = jnp.flip(retention_one_direction(jnp.flip(qf, 2), jnp.flip(kf, 2), jnp.flip(vf, 2),
                                           log_gamma[1], False), 2)
    return jnp.transpose(fwd + bwd, (0, 2, 1, 3))

def banded_keys(t):
    B, S, Hkv, d = t.shape
    NB = S // WIN_BLOCK
    tp = jnp.pad(t, ((0, 0), (WINDOW, WINDOW), (0, 0), (0, 0))).reshape(B, NB + 2, WIN_BLOCK, Hkv, d)
    return jnp.concatenate([tp[:, :-2], tp[:, 1:-1], tp[:, 2:]], axis=2)

def window_attention_with_sink(q, k, v, sink_logit):
    B, S, Hq, d = q.shape
    Hkv = k.shape[2]
    G = Hq // Hkv
    NB = S // WIN_BLOCK
    qb = q.reshape(B, NB, WIN_BLOCK, Hkv, G, d)
    kb = banded_keys(k)
    vb = banded_keys(v)
    s = jnp.einsum('bnqhgd,bnkhd->bnhgqk', qb, kb).astype(jnp.float32)
    i = jnp.arange(WIN_BLOCK)[:, None]
    j = jnp.arange(3 * WIN_BLOCK)[None, :]
    rel_ok = jnp.abs(i - j + WINDOW) <= WINDOW
    kpos = jnp.arange(NB)[:, None] * WIN_BLOCK + jnp.arange(3 * WIN_BLOCK)[None, :] - WINDOW
    in_ok = (kpos >= 0) & (kpos < S)
    mask = rel_ok[None] & in_ok[:, None, :]
    s = jnp.where(mask[None, :, None, None], s, -1e30)
    sink = jnp.broadcast_to(sink_logit.astype(jnp.float32).reshape(1, 1, Hkv, G, 1, 1), s.shape[:-1] + (1,))
    p = jax.nn.softmax(jnp.concatenate([s, sink], axis=-1), axis=-1)[..., :-1]
    o = jnp.einsum('bnhgqk,bnkhd->bnqhgd', p.astype(v.dtype), vb)
    return o.reshape(B, S, Hq * d)

def even_mixer(x, w_in, decay_logit, gn_gain, sink_logit, w_out, pos):
    B, S, _ = x.shape
    h = x @ w_in
    qa, ka, va, ga, qb, kb, vb = jnp.split(h, EVEN_SPLITS, axis=-1)
    qa = rope(qa.reshape(B, S, RET_HEADS, RET_HEAD_DIM), pos)
    ka = rope(ka.reshape(B, S, RET_HEADS, RET_HEAD_DIM), pos) * (RET_HEAD_DIM ** -0.5)
    va = va.reshape(B, S, RET_HEADS, RET_VALUE_DIM)
    ya = bidirectional_retention(qa, ka, va, decay_logit)
    mu = jnp.mean(ya, axis=-1, keepdims=True)
    var = jnp.mean(jnp.square(ya - mu), axis=-1, keepdims=True)
    ya = ((ya - mu) * lax.rsqrt(var + GN_EPS)).reshape(B, S, RET_WIDTH) * gn_gain.astype(jnp.float32)
    ya = jax.nn.silu(ga) * ya.astype(x.dtype)
    qb = rope(qb.reshape(B, S, WIN_Q_HEADS, WIN_HEAD_DIM), pos) * (WIN_HEAD_DIM ** -0.5)
    kb = rope(kb.reshape(B, S, WIN_KV_HEADS, WIN_HEAD_DIM), pos)
    vb = vb.reshape(B, S, WIN_KV_HEADS, WIN_HEAD_DIM)
    yb = window_attention_with_sink(qb, kb, vb, sink_logit)
    return jnp.concatenate([ya, yb], axis=-1) @ w_out

def fourier_mixer(x, w_out):
    B, S, D = x.shape
    xg = x.astype(jnp.float32).reshape(B, S, FOURIER_GROUPS, D // FOURIER_GROUPS)
    y = jnp.fft.fft2(xg, axes=(1, 3), norm='ortho').real.reshape(B, S, D)
    return y.astype(x.dtype) @ w_out

def hierarchical_moe(x, w_coarse, b_coarse, w_fine, b_fine, w_gate, w_up, w_down):
    B, S, D = x.shape
    xt = x.reshape(B * S, D)
    T = B * S
    coarse = (xt @ w_coarse + b_coarse).astype(jnp.float32)
    p_group, g_idx = lax.top_k(jax.nn.softmax(coarse, axis=-1), 1)
    fine = (xt @ w_fine + b_fine).astype(jnp.float32).reshape(T, N_GROUPS, EXPERTS_PER_GROUP)
    fine_g = jnp.take_along_axis(fine, g_idx[:, :, None], axis=1)[:, 0]
    top_val, top_idx = lax.top_k(fine_g, TOP_K)
    gate = jax.nn.softmax(top_val, axis=-1) * p_group
    expert_id = (g_idx * EXPERTS_PER_GROUP + top_idx).reshape(-1)
    order = jnp.argsort(expert_id)
    tok = order // TOP_K
    sizes = jnp.bincount(expert_id, length=N_EXPERTS).astype(jnp.int32)
    xs = xt[tok]
    hid = jax.nn.silu(lax.ragged_dot(xs, w_gate, sizes)) * lax.ragged_dot(xs, w_up, sizes)
    ys = lax.ragged_dot(hid, w_down, sizes) * gate.reshape(-1)[order][:, None].astype(x.dtype)
    out = jax.ops.segment_sum(ys, tok, num_segments=T)
    return out.reshape(B, S, D)

def first_inputs(seed: int = 0) -> dict:
    key = jax.random.key(seed)
    ks = jax.random.split(key, 20)
    f32 = jnp.float32
    nrm = lambda k, shape: jax.random.normal(k, shape, f32)
    base_logit = jnp.log(2.0 ** (5.0 + jnp.arange(RET_HEADS, dtype=f32)) - 1.0)
    return {
        "x": nrm(ks[0], (BATCH, SEQ, D_MODEL)),
        "w_in_even": nrm(ks[1], (N_EVEN, D_MODEL, IN_EVEN)) * D_MODEL ** -0.5,
        "ret_decay_logit": base_logit[None, None, :] + 0.1 * nrm(ks[2], (N_EVEN, 2, RET_HEADS)),
        "ret_gn_gain": 1.0 + 0.02 * nrm(ks[3], (N_EVEN, RET_WIDTH)),
        "sink_logit": 0.5 * nrm(ks[4], (N_EVEN, WIN_Q_HEADS)),
        "w_out_even": nrm(ks[5], (N_EVEN, D_MODEL, D_MODEL)) * D_MODEL ** -0.5 * DEEPNORM_BETA,
        "w_out_fourier": nrm(ks[6], (N_ODD, D_MODEL, D_MODEL)) * D_MODEL ** -0.5 * DEEPNORM_BETA,
        "ln1_gain": 1.0 + 0.02 * nrm(ks[7], (DEPTH, D_MODEL)),
        "ln1_bias": 0.02 * nrm(ks[8], (DEPTH, D_MODEL)),
        "ln2_gain": 1.0 + 0.02 * nrm(ks[9], (DEPTH, D_MODEL)),
        "ln2_bias": 0.02 * nrm(ks[10], (DEPTH, D_MODEL)),
        "router_coarse_w": nrm(ks[11], (DEPTH, D_MODEL, N_GROUPS)) * D_MODEL ** -0.5,
        "router_coarse_b": 0.01 * nrm(ks[12], (DEPTH, N_GROUPS)),
        "router_fine_w": nrm(ks[13], (DEPTH, D_MODEL, N_EXPERTS)) * D_MODEL ** -0.5,
        "router_fine_b": 0.01 * nrm(ks[14], (DEPTH, N_EXPERTS)),
        "expert_w_gate": nrm(ks[15], (DEPTH, N_EXPERTS, D_MODEL, EXPERT_HIDDEN)) * D_MODEL ** -0.5,
        "expert_w_up": nrm(ks[16], (DEPTH, N_EXPERTS, D_MODEL, EXPERT_HIDDEN)) * D_MODEL ** -0.5,
        "expert_w_down": nrm(ks[17], (DEPTH, N_EXPERTS, EXPERT_HIDDEN, D_MODEL)) * EXPERT_HIDDEN ** -0.5 * DEEPNORM_BETA,
    }

def first_block(x, w_in_even, ret_decay_logit, ret_gn_gain, sink_logit, w_out_even, w_out_fourier,
              ln1_gain, ln1_bias, ln2_gain, ln2_bias, router_coarse_w, router_coarse_b,
              router_fine_w, router_fine_b, expert_w_gate, expert_w_up, expert_w_down):
    pos = jnp.arange(x.shape[1], dtype=jnp.int32)
    for layer in range(DEPTH):
        if layer % 2 == 0:
            e = layer // 2
            mix = even_mixer(x, w_in_even[e], ret_decay_logit[e], ret_gn_gain[e], sink_logit[e],
                             w_out_even[e], pos)
        else:
            mix = fourier_mixer(x, w_out_fourier[layer // 2])
        x = layer_norm(DEEPNORM_ALPHA * x + mix, ln1_gain[layer], ln1_bias[layer])
        ffn = hierarchical_moe(x, router_coarse_w[layer], router_coarse_b[layer], router_fine_w[layer],
                               router_fine_b[layer], expert_w_gate[layer], expert_w_up[layer],
                               expert_w_down[layer])
        x = layer_norm(DEEPNORM_ALPHA * x + ffn, ln2_gain[layer], ln2_bias[layer])
    return x


DEPTH_2 = 1

HEAD_DIM = 64
GRID_W = 64
N_MEM = 256
NA_HEADS = 6
NA_WIN_ROWS = 8
NA_WIN_COLS = 16
ML_HEADS = 4
ML_CHUNK = 64
GDN_HEADS = 6
GDN_CHUNK = 64
CONV_K = 5
N_DIR = 2
XA_HEADS = 4
XA_HEAD_DIM = D_MODEL // XA_HEADS
D_FF = 4 * D_MODEL
NA_WIDTH = NA_HEADS * HEAD_DIM
ML_WIDTH = ML_HEADS * HEAD_DIM
GDN_WIDTH = GDN_HEADS * HEAD_DIM
D_MIX = NA_WIDTH + ML_WIDTH + GDN_WIDTH
EPS = 1e-6
IN_SIZES = (NA_WIDTH, NA_WIDTH, NA_WIDTH,
            ML_WIDTH, ML_WIDTH, ML_WIDTH, ML_WIDTH, N_DIR * ML_HEADS, N_DIR * ML_HEADS,
            GDN_WIDTH, GDN_WIDTH, GDN_WIDTH, GDN_WIDTH, N_DIR * GDN_HEADS, N_DIR * GDN_HEADS)
IN_OFFSETS = tuple(int(o) for o in np.cumsum(IN_SIZES)[:-1])
P_IN = int(sum(IN_SIZES))


def rmsnorm(x, w):
    xf = x.astype(jnp.float32)
    y = xf * lax.rsqrt(jnp.mean(xf * xf, axis=-1, keepdims=True) + EPS)
    return (y * w.astype(jnp.float32)).astype(x.dtype)

def head_rms(t):
    return t * lax.rsqrt(jnp.mean(t * t, axis=-1, keepdims=True) + EPS)

def l2norm(t):
    return t * lax.rsqrt(jnp.sum(t * t, axis=-1, keepdims=True) + EPS)

def neighbourhood_attention(q, k, v, rel_bias):
    b, s, h, dh = q.shape
    rows = s // GRID_W
    wr = min(NA_WIN_ROWS, rows)
    wc = NA_WIN_COLS
    qg = (q * dh ** -0.5).reshape(b, rows, GRID_W, h, dh)
    kg = k.reshape(b, rows, GRID_W, h, dh)
    vg = v.reshape(b, rows, GRID_W, h, dh)
    cols = jnp.arange(GRID_W)
    col_idx = jnp.clip(cols - wc // 2, 0, GRID_W - wc)[:, None] + jnp.arange(wc)[None, :]
    dc = col_idx - cols[:, None] + (NA_WIN_COLS - 1)

    def row_block(args):
        q_r, r = args
        r0 = jnp.clip(r - wr // 2, 0, rows - wr)
        k_win = lax.dynamic_slice_in_dim(kg, r0, wr, axis=1)[:, :, col_idx]
        v_win = lax.dynamic_slice_in_dim(vg, r0, wr, axis=1)[:, :, col_idx]
        dr = r0 + jnp.arange(wr) - r + (NA_WIN_ROWS - 1)
        bias = rel_bias[:, dr[None, :, None], dc[:, None, :]]
        logits = jnp.einsum('bqhd,brqchd->bhqrc', q_r, k_win).astype(jnp.float32) + bias.astype(jnp.float32)
        p = jax.nn.softmax(logits.reshape(b, h, GRID_W, wr * wc), axis=-1).reshape(logits.shape)
        return jnp.einsum('bhqrc,brqchd->bqhd', p.astype(v.dtype), v_win)

    out = lax.map(row_block, (jnp.moveaxis(qg, 1, 0), jnp.arange(rows)))
    return jnp.moveaxis(out, 0, 1).reshape(b, s, h * dh)

def mlstm_direction(q, k, v, ig, f_pre):
    b, h, s, d = q.shape
    L = ML_CHUNK
    nc = s // L
    q = q.reshape(b, h, nc, L, d)
    k = k.reshape(b, h, nc, L, d) * d ** -0.5
    v = v.reshape(b, h, nc, L, d)
    ig = ig.reshape(b, h, nc, L)
    bcum = jnp.cumsum(jax.nn.log_sigmoid(f_pre).reshape(b, h, nc, L), axis=-1)
    b_last = bcum[..., -1]
    w = b_last[..., None] - bcum + ig
    m_loc = jnp.max(w, axis=-1)
    wexp = jnp.exp(w - m_loc[..., None])
    c_loc = jnp.einsum('bhnl,bhnld,bhnle->nbhde', wexp, k, v)
    n_loc = jnp.einsum('bhnl,bhnld->nbhd', wexp, k)

    def step(carry, xs):
        c, n, m = carry
        c_l, n_l, m_l, bl = xs
        m_new = jnp.maximum(bl + m, m_l)
        a = jnp.exp(bl + m - m_new)
        g = jnp.exp(m_l - m_new)
        c_new = a[..., None, None] * c + g[..., None, None] * c_l
        n_new = a[..., None] * n + g[..., None] * n_l
        return (c_new, n_new, m_new), (c, n, m)

    init = (jnp.zeros((b, h, d, d), jnp.float32), jnp.zeros((b, h, d), jnp.float32), jnp.zeros((b, h), jnp.float32))
    _, (c_prev, n_prev, m_prev) = lax.scan(
        step, init, (c_loc, n_loc, jnp.moveaxis(m_loc, -1, 0), jnp.moveaxis(b_last, -1, 0)))
    c_prev = jnp.moveaxis(c_prev, 0, 2)
    n_prev = jnp.moveaxis(n_prev, 0, 2)
    m_prev = jnp.moveaxis(m_prev, 0, -1)
    causal = jnp.tril(jnp.ones((L, L), dtype=bool))
    dmat = jnp.where(causal, bcum[..., :, None] - bcum[..., None, :] + ig[..., None, :], -jnp.inf)
    inter = bcum + m_prev[..., None]
    m_t = jnp.maximum(jnp.max(dmat, axis=-1), inter)
    s_intra = jnp.einsum('bhnld,bhnsd->bhnls', q, k) * jnp.exp(dmat - m_t[..., None])
    a_inter = jnp.exp(inter - m_t)
    num = a_inter[..., None] * jnp.einsum('bhnld,bhnde->bhnle', q, c_prev) + jnp.einsum('bhnls,bhnse->bhnle', s_intra, v)
    den = a_inter * jnp.einsum('bhnld,bhnd->bhnl', q, n_prev) + jnp.sum(s_intra, axis=-1)
    out = num / jnp.maximum(jnp.abs(den), jnp.exp(-m_t))[..., None]
    return out.reshape(b, h, s, d)

def mlstm_mixer(q, k, v, o_pre, i_pre, f_pre, i_bias, f_bias, norm_w):
    b, s, _ = q.shape

    def heads(t):
        return t.reshape(b, s, ML_HEADS, HEAD_DIM).transpose(0, 2, 1, 3).astype(jnp.float32)

    qh, kh, vh = heads(q), heads(k), heads(v)
    ig = (i_pre.reshape(b, s, N_DIR, ML_HEADS).astype(jnp.float32) + i_bias.astype(jnp.float32)).transpose(2, 0, 3, 1)
    fg = (f_pre.reshape(b, s, N_DIR, ML_HEADS).astype(jnp.float32) + f_bias.astype(jnp.float32)).transpose(2, 0, 3, 1)
    h_fwd = mlstm_direction(qh, kh, vh, ig[0], fg[0])
    h_bwd = jnp.flip(mlstm_direction(jnp.flip(qh, 2), jnp.flip(kh, 2), jnp.flip(vh, 2),
                                     jnp.flip(ig[1], 2), jnp.flip(fg[1], 2)), 2)
    hs = head_rms((h_fwd + h_bwd).transpose(0, 2, 1, 3)).reshape(b, s, ML_WIDTH)
    out = hs * norm_w.astype(jnp.float32) * jax.nn.sigmoid(o_pre.astype(jnp.float32))
    return out.astype(q.dtype)

def centred_depthwise_conv(x, w):
    c = x.shape[-1]
    return lax.conv_general_dilated(
        x, w[:, None, :].astype(x.dtype), window_strides=(1,),
        padding=[(CONV_K // 2, CONV_K // 2)],
        dimension_numbers=('NWC', 'WIO', 'NWC'), feature_group_count=c)

def gdn_direction(q, k, v, g, beta):
    b, h, s, dk = q.shape
    dv = v.shape[-1]
    L = GDN_CHUNK
    nc = s // L
    q = (q * dk ** -0.5).reshape(b, h, nc, L, dk)
    k = k.reshape(b, h, nc, L, dk)
    v = v.reshape(b, h, nc, L, dv)
    beta = beta.reshape(b, h, nc, L)
    gc = jnp.cumsum(g.reshape(b, h, nc, L), axis=-1)
    incl = jnp.tril(jnp.ones((L, L), dtype=bool))
    strict = jnp.tril(jnp.ones((L, L), dtype=bool), -1)
    diff = gc[..., :, None] - gc[..., None, :]
    lmask = jnp.where(incl, jnp.exp(jnp.where(incl, diff, 0.0)), 0.0)
    kb = k * beta[..., None]
    a = jnp.where(strict, jnp.einsum('bhnld,bhnsd->bhnls', kb, k) * lmask, 0.0)
    eye = jnp.eye(L, dtype=jnp.float32)
    t = lax.linalg.triangular_solve(a + eye, jnp.broadcast_to(eye, a.shape),
                                    left_side=True, lower=True, unit_diagonal=True)
    u = jnp.einsum('bhnls,bhnse->bhnle', t, v * beta[..., None])
    wk = jnp.einsum('bhnls,bhnsd->bhnld', t, kb * jnp.exp(gc)[..., None])
    attn = jnp.where(incl, jnp.einsum('bhnld,bhnsd->bhnls', q, k) * lmask, 0.0)
    q_dec = q * jnp.exp(gc)[..., None]
    g_last = gc[..., -1]
    k_state = k * jnp.exp(g_last[..., None] - gc)[..., None]

    def step(state, xs):
        u_c, w_c, a_c, qd_c, ks_c, gl_c = xs
        v_new = u_c - jnp.einsum('bhld,bhde->bhle', w_c, state)
        o = jnp.einsum('bhld,bhde->bhle', qd_c, state) + jnp.einsum('bhls,bhse->bhle', a_c, v_new)
        state = state * jnp.exp(gl_c)[..., None, None] + jnp.einsum('bhld,bhle->bhde', ks_c, v_new)
        return state, o

    xs = tuple(jnp.moveaxis(t_, 2, 0) for t_ in (u, wk, attn, q_dec, k_state, g_last))
    _, o = lax.scan(step, jnp.zeros((b, h, dk, dv), jnp.float32), xs)
    return jnp.moveaxis(o, 0, 2).reshape(b, h, s, dv)

def gated_deltanet_mixer(q, k, v, z, beta_pre, alpha_pre, conv_w, a_log, dt_bias, norm_w):
    b, s, _ = q.shape
    qkv = jax.nn.silu(centred_depthwise_conv(jnp.concatenate([q, k, v], axis=-1), conv_w))
    qc, kc, vc = jnp.split(qkv, 3, axis=-1)

    def heads(t):
        return t.reshape(b, s, GDN_HEADS, HEAD_DIM).transpose(0, 2, 1, 3).astype(jnp.float32)

    qh, kh, vh = l2norm(heads(qc)), l2norm(heads(kc)), heads(vc)
    beta = jax.nn.sigmoid(beta_pre.reshape(b, s, N_DIR, GDN_HEADS).astype(jnp.float32)).transpose(2, 0, 3, 1)
    g = (-jnp.exp(a_log.astype(jnp.float32)) * jax.nn.softplus(
        alpha_pre.reshape(b, s, N_DIR, GDN_HEADS).astype(jnp.float32) + dt_bias.astype(jnp.float32))).transpose(2, 0, 3, 1)
    o_fwd = gdn_direction(qh, kh, vh, g[0], beta[0])
    o_bwd = jnp.flip(gdn_direction(jnp.flip(qh, 2), jnp.flip(kh, 2), jnp.flip(vh, 2),
                                   jnp.flip(g[1], 2), jnp.flip(beta[1], 2)), 2)
    o = head_rms((o_fwd + o_bwd).transpose(0, 2, 1, 3)).reshape(b, s, GDN_WIDTH)
    o = o * norm_w.astype(jnp.float32) * jax.nn.silu(z.astype(jnp.float32))
    return o.astype(z.dtype)

def memory_cross_attention(h, mem_n, w_q, w_kv, w_o):
    b, s, _ = h.shape
    m = mem_n.shape[1]
    q = (h @ w_q).reshape(b, s, XA_HEADS, XA_HEAD_DIM)
    kk, vv = jnp.split(mem_n @ w_kv, 2, axis=-1)
    kk = kk.reshape(b, m, XA_HEADS, XA_HEAD_DIM)
    vv = vv.reshape(b, m, XA_HEADS, XA_HEAD_DIM)
    logits = jnp.einsum('bshd,bmhd->bhsm', q, kk).astype(jnp.float32) * XA_HEAD_DIM ** -0.5
    p = jax.nn.softmax(logits, axis=-1)
    o = jnp.einsum('bhsm,bmhd->bshd', p.astype(vv.dtype), vv).reshape(b, s, XA_HEADS * XA_HEAD_DIM)
    return o @ w_o

def second_inputs(seed: int = 0) -> dict:
    key = jax.random.key(seed)
    ks = jax.random.split(key, 24)
    f32 = jnp.float32

    def nrm(k, shape, scale):
        return jax.random.normal(k, shape, f32) * scale

    def gain(k, shape):
        return 1.0 + 0.02 * jax.random.normal(k, shape, f32)

    dt = jnp.exp(jax.random.uniform(ks[12], (DEPTH_2, N_DIR, GDN_HEADS), f32, math.log(1e-3), math.log(1e-1)))
    return {
        'x': nrm(ks[0], (BATCH, SEQ, D_MODEL), 1.0),
        'mem': nrm(ks[1], (BATCH, N_MEM, D_MODEL), 1.0),
        'norm_mix_w': gain(ks[2], (DEPTH_2, D_MODEL)),
        'w_in': nrm(ks[3], (DEPTH_2, D_MODEL, P_IN), D_MODEL ** -0.5),
        'na_rel_bias': nrm(ks[4], (DEPTH_2, NA_HEADS, 2 * NA_WIN_ROWS - 1, 2 * NA_WIN_COLS - 1), 0.02),
        'ml_i_bias': nrm(ks[5], (DEPTH_2, N_DIR, ML_HEADS), 0.1),
        'ml_f_bias': 3.0 + 3.0 * jax.random.uniform(ks[6], (DEPTH_2, N_DIR, ML_HEADS), f32),
        'ml_norm_w': gain(ks[7], (DEPTH_2, ML_WIDTH)),
        'gdn_conv_w': nrm(ks[8], (DEPTH_2, CONV_K, 3 * GDN_WIDTH), CONV_K ** -0.5),
        'gdn_a_log': jnp.log(jax.random.uniform(ks[9], (DEPTH_2, N_DIR, GDN_HEADS), f32, 1.0, 16.0)),
        'gdn_dt_bias': dt + jnp.log(-jnp.expm1(-dt)),
        'gdn_norm_w': gain(ks[10], (DEPTH_2, GDN_WIDTH)),
        'w_out': nrm(ks[11], (DEPTH_2, D_MIX, D_MODEL), D_MIX ** -0.5),
        'norm_xa_w': gain(ks[13], (DEPTH_2, D_MODEL)),
        'norm_mem_w': gain(ks[14], (DEPTH_2, D_MODEL)),
        'w_xq': nrm(ks[15], (DEPTH_2, D_MODEL, XA_HEADS * XA_HEAD_DIM), D_MODEL ** -0.5),
        'w_xkv': nrm(ks[16], (DEPTH_2, D_MODEL, 2 * XA_HEADS * XA_HEAD_DIM), D_MODEL ** -0.5),
        'w_xo': nrm(ks[17], (DEPTH_2, XA_HEADS * XA_HEAD_DIM, D_MODEL), (XA_HEADS * XA_HEAD_DIM) ** -0.5),
        'norm_ffn_w': gain(ks[18], (DEPTH_2, D_MODEL)),
        'w_ff1': nrm(ks[19], (DEPTH_2, D_MODEL, D_FF), D_MODEL ** -0.5),
        'w_ff2': nrm(ks[20], (DEPTH_2, D_FF, D_MODEL), D_FF ** -0.5),
        'norm_out_w': gain(ks[21], (D_MODEL,)),
    }

def second_block(x, mem, norm_mix_w, w_in, na_rel_bias, ml_i_bias, ml_f_bias, ml_norm_w,
              gdn_conv_w, gdn_a_log, gdn_dt_bias, gdn_norm_w, w_out, norm_xa_w, norm_mem_w,
              w_xq, w_xkv, w_xo, norm_ffn_w, w_ff1, w_ff2, norm_out_w):
    b, s, _ = x.shape
    for l in range(DEPTH_2):
        h = rmsnorm(x, norm_mix_w[l])
        (na_q, na_k, na_v, ml_q, ml_k, ml_v, ml_o, ml_i, ml_f,
         gd_q, gd_k, gd_v, gd_z, gd_b, gd_a) = jnp.split(h @ w_in[l], IN_OFFSETS, axis=-1)
        y_na = neighbourhood_attention(na_q.reshape(b, s, NA_HEADS, HEAD_DIM),
                                       na_k.reshape(b, s, NA_HEADS, HEAD_DIM),
                                       na_v.reshape(b, s, NA_HEADS, HEAD_DIM), na_rel_bias[l])
        y_ml = mlstm_mixer(ml_q, ml_k, ml_v, ml_o, ml_i, ml_f, ml_i_bias[l], ml_f_bias[l], ml_norm_w[l])
        y_gd = gated_deltanet_mixer(gd_q, gd_k, gd_v, gd_z, gd_b, gd_a, gdn_conv_w[l],
                                    gdn_a_log[l], gdn_dt_bias[l], gdn_norm_w[l])
        x = x + jnp.concatenate([y_na, y_ml, y_gd], axis=-1) @ w_out[l]
        x = x + memory_cross_attention(rmsnorm(x, norm_xa_w[l]), rmsnorm(mem, norm_mem_w[l]),
                                       w_xq[l], w_xkv[l], w_xo[l])
        h = rmsnorm(x, norm_ffn_w[l])
        x = x + jnp.square(jax.nn.relu(h @ w_ff1[l])) @ w_ff2[l]
    return rmsnorm(x, norm_out_w)


def setup_inputs(seed=0):
    out = dict(first_inputs(seed))
    for name, value in second_inputs(seed + 1).items():
        if name != "x":
            out[name + "_2"] = value
    return out


def reference(
    x, w_in_even, ret_decay_logit, ret_gn_gain, sink_logit, w_out_even, w_out_fourier, ln1_gain,
    ln1_bias, ln2_gain, ln2_bias, router_coarse_w, router_coarse_b, router_fine_w,
    router_fine_b, expert_w_gate, expert_w_up, expert_w_down, mem_2, norm_mix_w_2, w_in_2,
    na_rel_bias_2, ml_i_bias_2, ml_f_bias_2, ml_norm_w_2, gdn_conv_w_2, gdn_a_log_2,
    gdn_dt_bias_2, gdn_norm_w_2, w_out_2, norm_xa_w_2, norm_mem_w_2, w_xq_2, w_xkv_2, w_xo_2,
    norm_ffn_w_2, w_ff1_2, w_ff2_2, norm_out_w_2,
):
    x = first_block(
        x, w_in_even, ret_decay_logit, ret_gn_gain, sink_logit, w_out_even, w_out_fourier,
        ln1_gain, ln1_bias, ln2_gain, ln2_bias, router_coarse_w, router_coarse_b, router_fine_w,
        router_fine_b, expert_w_gate, expert_w_up, expert_w_down,
    )
    return second_block(
        x, mem_2, norm_mix_w_2, w_in_2, na_rel_bias_2, ml_i_bias_2, ml_f_bias_2, ml_norm_w_2,
        gdn_conv_w_2, gdn_a_log_2, gdn_dt_bias_2, gdn_norm_w_2, w_out_2, norm_xa_w_2,
        norm_mem_w_2, w_xq_2, w_xkv_2, w_xo_2, norm_ffn_w_2, w_ff1_2, w_ff2_2, norm_out_w_2,
    )


_drawn_inputs = setup_inputs


def setup_inputs(seed=0):
    import zlib

    import numpy as np

    out = dict(_drawn_inputs(seed))
    spreads = {}
    factors = {'ret_gn_gain': 8.0,
     'sink_logit': 8.0,
     'router_coarse_b': 5.197,
     'router_fine_b': 7.029,
     'norm_mix_w_2': 2.908,
     'na_rel_bias_2': 8.0,
     'ml_i_bias_2': 8.0,
     'ml_norm_w_2': 8.0,
     'gdn_norm_w_2': 7.807,
     'norm_xa_w_2': 8.0,
     'norm_mem_w_2': 8.0,
     'norm_ffn_w_2': 10.978,
     'norm_out_w_2': 8.125}
    for name, (base, spread) in spreads.items():
        noise = np.random.default_rng([zlib.crc32(name.encode()), seed]).standard_normal(out[name].shape)
        drawn = base * np.exp(spread * noise) if base else spread * noise
        out[name] = jnp.asarray(drawn.astype(out[name].dtype))
    for name, factor in factors.items():
        out[name] = (out[name] * factor).astype(out[name].dtype)
    return out
```

```python
from contextlib import ExitStack

import numpy as np
import concourse.bass as bass
from concourse import mybir

ALU = mybir.AluOpType
ACT = mybir.ActivationFunctionType
F32 = mybir.dt.float32
I32 = mybir.dt.int32
U32 = mybir.dt.uint32
AX = mybir.AxisListType.X

P = 128
S = 512
T = S // P
D = 1024
KD = D // P
WT = 512
ALPHA = 4.0 ** 0.25
LN_EPS = 1e-5
EPS = 1e-6
NEG = -1e30

RH = 4
WQ, WKV, WD = 8, 2, 64
IN_EVEN = 2816
OFF_QA, OFF_KA, OFF_VA, OFF_GA, OFF_QB, OFF_KB, OFF_VB = 0, 512, 1024, 1536, 2048, 2560, 2688
TOEP = 7 * P

NE = 32
NG = 4
EH = 512
NOV = (2 * S) // (P + 1)
JOBS = NE + NOV

NAH, MLH, GDH = 6, 4, 6
HD = 64
C2_NAQ, C2_NAK, C2_NAV = 0, 384, 768
C2_MLQ, C2_MLK, C2_MLV, C2_MLO, C2_MLI, C2_MLF, C2_MLE = 0, 256, 512, 768, 1024, 1032, 1040
C2_Z, C2_B, C2_A, C2_ZE = 0, 384, 396, 408
W2_ML, W2_GD, W2_Z = 1152, 2192, 3344
GDC = 3 * GDH * HD
GCT = GDC // P
MEMN = 256
XH, XD = 4, 256
FF = 4096
FFT = FF // P
LEVELS = 7

RING = 3


class Names:
    pass


class Engine:

    def __init__(self, K, eng, name, step):
        self.K, self.eng, self.name, self.step = K, eng, name, step
        self.n = 0
        self.s = 0
        self.loop = None
        self.w = 0

    def gen(self, n):
        if self.loop is None or n < self.loop[3]:
            return n // 8
        return self.loop[0] * (self.loop[1] // 8) + n // 8

    def take(self):
        n, self.n = self.n, self.n + 1
        return n

    def bank(self, n):
        return self.K.ps[:, n % 8, :]

    def wait_filled(self, n):
        self.eng.wait_ge(self.K.bank_filled[n % 8], self.gen(n) + 1)

    def wait_evacuated(self, lo, hi):
        for n in range(max(lo, hi - 8), hi):
            self.eng.wait_ge(self.K.bank_evacuated[n % 8], self.gen(n) + 1)

    def wait_bank(self, n):
        if n >= 8:
            self.eng.wait_ge(self.K.bank_evacuated[n % 8], self.gen(n))

    def filled(self, ins, n):
        ins.then_inc(self.K.bank_filled[n % 8], 1)

    def evacuated(self, ins, n):
        ins.then_inc(self.K.bank_evacuated[n % 8], 1)

    def link(self, ins):
        self.s += 1
        ins.then_inc(self.step, 1)
        if self.loop is None:
            self.eng.wait_ge(self.step, self.s)
        else:
            self.eng.wait_ge(self.step, self.loop[0] * self.loop[2] + self.s)

    def phase(self):
        self.K.phases[self.name] += 1
        self.eng.drain().then_inc(self.K.phase_done, 1)
        self.eng.wait_ge(self.K.phase_done, 4 * self.K.phases[self.name])

    def begin_loop(self, reg, products, steps, start=0):
        assert products % 8 == 0
        self.loop = (reg, products, steps, self.n)
        self.at = (self.n, self.s)

    def end_loop(self, turns):
        _, products, steps, _ = self.loop
        assert self.n - self.at[0] == products, (self.name, self.n - self.at[0], products)
        assert self.s - self.at[1] == steps, (self.name, self.s - self.at[1], steps)
        self.n = self.at[0] + products * turns
        self.s = self.at[1] + steps * turns
        self.loop = None



def pe_transposes(E, tasks):
    for blocks in tasks:
        n = E.take()
        E.wait_bank(n)
        for i, src in enumerate(blocks):
            rows, cols = src.shape
            last = E.eng.transpose(E.bank(n)[0:cols, P * i:P * i + rows], src, E.K.ident[0:rows, 0:rows])
        E.filled(last, n)


def copy_out(E, tasks):
    for dst, view, who in tasks:
        n = E.take()
        if who != E.name:
            continue
        E.wait_filled(n)
        src = view(E.bank(n))
        if E.name == "act":
            ins = E.eng.activation(dst, src, ACT.Copy)
        else:
            ins = E.eng.tensor_copy(dst, src)
        E.evacuated(ins, n)


def turn(i):
    return ("act", "dve")[i % 2]


def xt_tasks(src):
    return [[src[:, t, P * k:P * k + P] for t in range(T)] for k in range(KD)]


def xt_out(dst):
    return [(dst[:, k, :], lambda b: b, turn(k)) for k in range(KD)]


def pe_weights(E):
    K = E.K
    w, E.w = E.w, E.w + 1
    E.eng.wait_ge(K.w_loaded[w % RING], 16 * (w // RING + 1))
    return K.ring[:, w % RING, :]


def pe_linear(E, xT, widths, tiles=T):
    for i, width in enumerate(widths):
        w = pe_weights(E).rearrange("p (k n) -> p k n", k=KD)
        for t in range(tiles):
            n = E.take()
            E.wait_bank(n)
            for k in range(KD):
                mm = E.eng.matmul(E.bank(n)[:, 0:width], xT[:, k, P * t:P * t + P], w[:, k, 0:width],
                                  start=(k == 0), stop=(k == KD - 1))
                if i and t == 0 and k == 0:
                    mm.then_inc(E.K.w_used, 1)
            E.filled(mm, n)
    E.eng.drain().then_inc(E.K.w_used, 1)


def linear_out(dst, widths):
    out, at = [], 0
    for width in widths:
        for t in range(T):
            out.append((dst[:, t, at:at + width], lambda b, w=width: b[:, 0:w], turn(len(out))))
        at += width
    return out


def residual_out(E, x, halves, scale):
    for h in range(halves):
        for t in range(T):
            n = E.take()
            if E.name == "dve":
                E.wait_filled(n)
                part = x[:, t, WT * h:WT * h + WT]
                E.evacuated(E.eng.scalar_tensor_tensor(part, part, scale, E.bank(n), ALU.mult, ALU.add), n)


def dve_rsqrt(E, y, x, t):
    v = E.eng
    E.link(v.tensor_scalar(y.bitcast(I32), x.bitcast(I32), -0.5, float(0x5F3759DF), ALU.mult, ALU.add))
    for _ in range(3):
        E.link(v.tensor_tensor(t, y, y, ALU.mult))
        E.link(v.scalar_tensor_tensor(t, t, -0.5, x, ALU.mult, ALU.mult))
        E.link(v.scalar_tensor_tensor(y, t, 1.5, y, ALU.add, ALU.mult))


def dve_layer_norm(E, x, gain, bias, st):
    v = E.eng
    for t in range(T):
        for h in range(2):
            ins = v.bn_stats(st[:, t, 6 * h:6 * h + 6], x[:, t, WT * h:WT * h + WT])
    E.link(ins)
    for t in range(T):
        ins = v.bn_aggr(st[:, t, 12:14], st[:, t, 0:12])
    E.link(ins)
    E.link(v.tensor_scalar(st[:, :, 13], st[:, :, 13], LN_EPS, None, ALU.add))
    dve_rsqrt(E, st[:, :, 14], st[:, :, 13], st[:, :, 15])
    for t in range(T):
        ins = v.tensor_scalar(x[:, t, :], x[:, t, :], st[:, t, 12:13], st[:, t, 14:15], ALU.subtract, ALU.mult)
    E.link(ins)
    for t in range(T):
        ins = v.tensor_tensor(x[:, t, :], x[:, t, :], gain, ALU.mult)
    E.link(ins)
    for t in range(T):
        ins = v.tensor_tensor(x[:, t, :], x[:, t, :], bias, ALU.add)
    E.link(ins)


def dve_rms_norm(E, dst, x, gain, st, tiles, tmp):
    v = E.eng
    for t in range(tiles):
        E.link(v.tensor_tensor(tmp, x[:, t, :], x[:, t, :], ALU.mult))
        E.link(v.reduce_sum(st[:, t, 0:1], tmp, AX))
    E.link(v.tensor_scalar(st[:, 0:tiles, 1], st[:, 0:tiles, 0], 1.0 / D, EPS, ALU.mult, ALU.add))
    dve_rsqrt(E, st[:, 0:tiles, 2], st[:, 0:tiles, 1], st[:, 0:tiles, 3])
    for t in range(tiles):
        ins = v.scalar_tensor_tensor(dst[:, t, :], x[:, t, :], st[:, t, 2:3], gain, ALU.mult, ALU.mult)
    E.link(ins)


def dve_rope(E, x, heads, half, cos, sin, ta, tb):
    v = E.eng
    w = heads * 2 * half
    x4 = x.rearrange("p t (h a d) -> p t h a d", h=heads, a=2)
    a4 = ta[:, :, 0:w].rearrange("p t (h a d) -> p t h a d", h=heads, a=2)
    b4 = tb[:, :, 0:w].rearrange("p t (h a d) -> p t h a d", h=heads, a=2)
    shape = [P, heads, half]
    for t in range(T):
        c = cos[:, t, :].unsqueeze(1).to_broadcast(shape)
        s = sin[:, t, :].unsqueeze(1).to_broadcast(shape)
        for a in range(2):
            v.tensor_tensor(a4[:, t, :, a, :], x4[:, t, :, a, :], c, ALU.mult)
            ins = v.tensor_tensor(b4[:, t, :, a, :], x4[:, t, :, 1 - a, :], s, ALU.mult)
    E.link(ins)
    for t in range(T):
        v.tensor_tensor(x4[:, t, :, 0, :], a4[:, t, :, 0, :], b4[:, t, :, 0, :], ALU.subtract)
        ins = v.tensor_tensor(x4[:, t, :, 1, :], a4[:, t, :, 1, :], b4[:, t, :, 1, :], ALU.add)
    return ins



def att_plan(a):
    a.pairs = [(n, i) for n in range(T) for i in range(len(a.blocks[n]))]
    a.turns = [a.pairs[i:i + 4] for i in range(0, len(a.pairs), 4)]
    a.npv = WT // a.dv if WT // a.dv < T else T
    a.pvs = T // a.npv
    a.per = T + len(a.turns) + a.pvs
    return a


def att_order(a):
    yield "scores", 0
    for h in range(a.heads):
        if h + 1 < a.heads:
            yield "scores", h + 1
        yield "rest", h


def pe_attention(E, a):
    pe, K = E.eng, E.K
    for what, h in att_order(a):
        if what == "scores":
            for n in range(T):
                m = E.take()
                E.wait_bank(m)
                lo, hi = a.cols(n)
                parts = a.scores(h, n)
                for i, (lhsT, rhs) in enumerate(parts):
                    mm = pe.matmul(E.bank(m)[:, 0:hi - lo], lhsT, rhs, start=(i == 0), stop=(i == len(parts) - 1))
                E.filled(mm, m)
            continue
        pe.wait_ge(K.probs_ready, K.probs_base[a.name] + h + 1)
        t0 = E.n
        pe_transposes(E, [[a.s[:, h % 2, n, a.cols(n)[0] + P * i:a.cols(n)[0] + P * i + P] for n, i in g] for g in a.turns])
        E.wait_evacuated(t0, t0 + len(a.turns))
        for g in range(a.pvs):
            m = E.take()
            E.wait_bank(m)
            for n in range(g * a.npv, (g + 1) * a.npv):
                at = [i for i, (nn, _) in enumerate(a.pairs) if nn == n]
                for j, i in enumerate(at):
                    c = (n - g * a.npv) * a.dv
                    mm = pe.matmul(E.bank(m)[:, c:c + a.dv], a.pT[:, h % 2, i, :], a.value(h, a.blocks[n][j]),
                                   start=(j == 0), stop=(j == len(at) - 1))
            E.filled(mm, m)


def dve_attention(E, a):
    v, K = E.eng, E.K
    base = K.probs_base[a.name]
    for what, h in att_order(a):
        b = h % 2
        if what == "scores":
            for n in range(T):
                m = E.take()
                lo, hi = a.cols(n)
                dst, src = a.s[:, b, n, lo:hi], E.bank(m)[:, 0:hi - lo]
                E.wait_filled(m)
                add = a.addend(h, n)
                if add is None:
                    ins = v.tensor_scalar(dst, src, a.scale, None, ALU.mult)
                else:
                    ins = v.scalar_tensor_tensor(dst, src, a.scale, add, ALU.mult, ALU.add)
                E.evacuated(ins, m)
            E.wait_evacuated(E.n - T, E.n)
            E.link(v.reduce_max(a.st[:, b, 0, :], a.s[:, b, :, :], AX))
            sink = a.sink(h)
            if sink is None:
                ins = v.tensor_scalar(a.st[:, b, 1, :], a.st[:, b, 0, :], -1.0, None, ALU.mult)
            else:
                ins = v.tensor_scalar(a.st[:, b, 1, :], a.st[:, b, 0, :], sink, -1.0, ALU.max, ALU.mult)
            ins.then_inc(K.scores_ready, 1)
            continue
        v.wait_ge(K.probs_ready, base + h + 1)
        if a.sink(h) is not None:
            E.link(v.tensor_tensor(a.st[:, b, 2, :], a.st[:, b, 2, :], a.st[:, b, 3, :], ALU.add))
        E.link(v.reciprocal(a.st[:, b, 4, :], a.st[:, b, 2, :]))
        E.n += len(a.turns)
        for g in range(a.pvs):
            m = E.take()
            E.wait_filled(m)
            lo, hi = g * a.npv, (g + 1) * a.npv
            src = E.bank(m)[:, 0:a.npv * a.dv].rearrange("p (n d) -> p n d", d=a.dv)
            den = a.st[:, b, 4, lo:hi].unsqueeze(2).to_broadcast([P, hi - lo, a.dv])
            E.evacuated(v.tensor_tensor(a.out(h, lo, hi), src, den, ALU.mult), m)


def act_attention(E, a):
    s, K = E.eng, E.K
    base = K.probs_base[a.name]
    pv = {}
    for what, h in att_order(a):
        b = h % 2
        if what == "scores":
            E.n += T
            s.wait_ge(K.scores_ready, base + h + 1)
            for n in range(T):
                row = a.s[:, b, n, a.cols(n)[0]:a.cols(n)[1]]
                ins = s.activation(row, row, ACT.Exp, bias=a.st[:, b, 1, n:n + 1], accum_out=a.st[:, b, 2, n:n + 1])
            if a.sink(h) is not None:
                ins = s.activation(a.st[:, b, 3, :], a.st[:, b, 1, :], ACT.Exp, bias=a.sink(h))
            ins.then_inc(K.probs_ready, 1)
            continue
        if h >= 2:
            for m in pv[h - 2]:
                E.wait_filled(m)
        for g in a.turns:
            m = E.take()
            i = a.pairs.index(g[0])
            E.wait_filled(m)
            dst = a.pT[:, b, i:i + len(g), :].rearrange("p i q -> p (i q)")
            E.evacuated(s.activation(dst, E.bank(m)[:, 0:P * len(g)], ACT.Copy), m)
        pv[h] = list(range(E.n, E.n + a.pvs))
        E.n += a.pvs



def even_views(K):
    A = K.carve(0)
    m = Names()
    m.h = A(T, IN_EVEN)
    m.mix = A(T, D)
    m.cos128, m.sin128, m.cos64, m.sin64 = A(T, 64), A(T, 64), A(T, 32), A(T, 32)
    here = A.at
    m.qaT, m.kaT = A(RH, S), A(RH, S)
    A.at = here
    m.qbT, m.kbT = A(WQ, S)[0:WD], A(WKV, S)[0:WD]
    m.dpos, m.dneg = A(TOEP), A(TOEP)
    m.gn = A(RH * P)
    m.lg = A(32)
    m.sink = A(WQ)
    m.gst = A(3, T * RH)
    m.st = A(2, 5, T)
    here = A.at
    m.ta, m.tb = A(T, 512), A(T, 512)
    A.at = here
    m.G, m.sq = A(RH, TOEP), A(T * RH, P)
    A.at = here
    m.s, m.pT, m.mask = A(2, T, 3 * P), A(2, 10, P), A(3 * P)
    m.W = [m.h[:, :, 0:512], m.h[:, :, 512:1024]]
    m.ga = m.h[:, :, OFF_GA:OFF_QB]
    return m


def even_attention(K):
    m = K.even
    a = Names()
    a.name = "window"
    a.heads = WQ
    a.scale = WD ** -0.5
    a.dv = WD
    a.s = m.s
    a.pT = m.pT
    a.st = m.st
    a.blocks = [[j for j in (n - 1, n, n + 1) if 0 <= j < T] for n in range(T)]
    a.cols = lambda n: (P if n == 0 else 0, 2 * P if n == T - 1 else 3 * P)
    a.scores = lambda h, n: [(m.qbT[:, h, P * n:P * n + P],
                              m.kbT[:, h // (WQ // WKV), P * a.blocks[n][0]:P * a.blocks[n][-1] + P])]
    a.addend = lambda h, n: m.mask[:, a.cols(n)[0]:a.cols(n)[1]]
    a.sink = lambda h: m.sink[:, h:h + 1]
    a.value = lambda h, j: m.h[:, j, OFF_VB + WD * (h // (WQ // WKV)):OFF_VB + WD * (h // (WQ // WKV)) + WD]
    a.out = lambda h, lo, hi: m.mix[:, lo:hi, 512 + WD * h:512 + WD * h + WD]
    return att_plan(a)


EVEN_WIDTHS = [512] * 5 + [256]


def rope_tasks(m):
    tasks = [[m.h[:, t, OFF_QA + P * h:OFF_QA + P * h + P] for t in range(T)] for h in range(RH)]
    tasks += [[m.h[:, t, OFF_KA + P * h:OFF_KA + P * h + P] for t in range(T)] for h in range(RH)]
    tasks += [[m.h[:, t, OFF_QB + WD * h:OFF_QB + WD * h + WD] for t in range(T)] for h in range(WQ)]
    tasks += [[m.h[:, t, OFF_KB + WD * h:OFF_KB + WD * h + WD] for t in range(T)] for h in range(WKV)]
    return tasks


def rope_out(m):
    out = [(m.qaT[:, h, :], lambda b: b) for h in range(RH)] + [(m.kaT[:, h, :], lambda b: b) for h in range(RH)]
    out += [(m.qbT[:, h, :], lambda b: b[0:WD]) for h in range(WQ)] + [(m.kbT[:, h, :], lambda b: b[0:WD]) for h in range(WKV)]
    return [(d, f, "act") for d, f in out]


def pe_even(E):
    K, m, pe = E.K, E.K.even, E.eng
    pe.wait_ge(K.x_loaded, 16)
    pe.wait_ge(K.consts_loaded, 16 * K.CONSTS)
    n0 = E.n
    pe_transposes(E, xt_tasks(K.x))
    E.wait_evacuated(n0, E.n)
    pe_linear(E, K.xT, EVEN_WIDTHS)
    E.phase()
    tasks = rope_tasks(m)
    for i in range(2):
        pe.wait_ge(K.rope_done, i + 1)
        pe_transposes(E, tasks[RH * i:RH * i + RH])
    E.phase()
    for h in range(RH + 1):
        if h < RH:
            for i in range(T):
                n = E.take()
                E.wait_bank(n)
                E.filled(pe.matmul(E.bank(n), m.kaT[:, h, P * i:P * i + P], m.qaT[:, h, :], start=True, stop=True), n)
        if h >= 1:
            g = h - 1
            E.wait_evacuated(K.ret_scores[g], K.ret_scores[g] + T)
            n = E.take()
            E.wait_bank(n)
            for t in range(T):
                for i in range(T):
                    mm = pe.matmul(E.bank(n)[:, P * t:P * t + P], m.W[g % 2][:, i, P * t:P * t + P],
                                   m.h[:, i, OFF_VA + P * g:OFF_VA + P * g + P], start=(i == 0), stop=(i == T - 1))
            E.filled(mm, n)
    E.phase()
    n0 = E.n
    pe_transposes(E, tasks[2 * RH:])
    E.wait_evacuated(n0, E.n)
    pe_attention(E, K.window)
    E.phase()
    mixer_end_pe(E, m.mix, 1)


def mixer_end_pe(E, mix, norm):
    K = E.K
    n0 = E.n
    if mix is not None:
        pe_transposes(E, xt_tasks(mix))
        E.wait_evacuated(n0, E.n)
    pe_linear(E, K.xT, [512] * 2)
    turn_x_pe(E, norm)
    E.phase()


def turn_x_pe(E, norm):
    E.eng.wait_ge(E.K.norm_done, norm)
    n0 = E.n
    pe_transposes(E, xt_tasks(E.K.x))
    E.wait_evacuated(n0, E.n)


def act_even(E):
    K, m, s = E.K, E.K.even, E.eng
    copy_out(E, xt_out(K.xT))
    n0 = E.n
    copy_out(E, linear_out(m.h, EVEN_WIDTHS))
    E.wait_evacuated(n0, E.n)
    E.phase()
    s.activation(m.mix[:, :, 0:512], m.ga, ACT.Exp, scale=-1.0)
    s.wait_ge(K.small_dve, 1)
    s.activation(m.lg[:, 8:16], m.lg[:, 8:16], ACT.Exp, scale=-1.0).then_inc(K.small_act, 1)
    s.wait_ge(K.small_dve, 2)
    s.activation(m.lg[:, 24:32], m.lg[:, 16:24], ACT.Ln).then_inc(K.small_act, 1)
    copy_out(E, rope_out(m)[0:2 * RH])
    E.phase()
    for h in range(RH):
        s.wait_ge(K.decay_exponents, h + 1)
        s.activation(m.G[:, h, :], m.G[:, h, :], ACT.Exp).then_inc(K.decays_ready, 1)
    E.n += (T + 1) * RH
    E.phase()
    copy_out(E, rope_out(m)[2 * RH:])
    act_attention(E, K.window)
    E.phase()
    mixer_end_act(E, m.mix)


def mixer_end_act(E, mix):
    K = E.K
    if mix is not None:
        copy_out(E, xt_out(K.xT))
    residual_out(E, K.x, 2, ALPHA)
    copy_out(E, xt_out(K.xT))
    E.phase()


def dve_log1p_end(E, out, ln, u, e, t):
    v = E.eng
    E.link(v.scalar_tensor_tensor(t, u, -1.0, e, ALU.add, ALU.subtract))
    E.link(v.tensor_tensor(out, ln, t, ALU.subtract))


def dve_even(E):
    K, m, v = E.K, E.K.even, E.eng
    copy_out(E, xt_out(K.xT))
    n0 = E.n
    copy_out(E, linear_out(m.h, EVEN_WIDTHS))
    E.wait_evacuated(n0, E.n)
    E.phase()
    v.wait_ge(K.even_loaded, 16 * K.EVEN_DMAS)
    lg, e, u, ln = m.lg[:, 0:8], m.lg[:, 8:16], m.lg[:, 16:24], m.lg[:, 24:32]
    v.scalar_tensor_tensor(e, lg, -1.0, lg, ALU.mult, ALU.max).then_inc(K.small_dve, 1)
    for x, heads, half, cos, sin in ((m.h[:, :, OFF_QA:OFF_KA], RH, 64, m.cos128, m.sin128),
                                     (m.h[:, :, OFF_KA:OFF_VA], RH, 64, m.cos128, m.sin128),
                                     (m.h[:, :, OFF_QB:OFF_KB], WQ, 32, m.cos64, m.sin64),
                                     (m.h[:, :, OFF_KB:OFF_VB], WKV, 32, m.cos64, m.sin64)):
        K.rope_count += 1
        dve_rope(E, x, heads, half, cos, sin, m.ta, m.tb).then_inc(K.rope_done, 1)
        v.wait_ge(K.rope_done, K.rope_count)
    v.wait_ge(K.small_act, 1)
    v.tensor_scalar(u, e, 1.0, None, ALU.add).then_inc(K.small_dve, 1)
    v.wait_ge(K.small_dve, 2)
    v.wait_ge(K.small_act, 2)
    dve_log1p_end(E, ln, ln, u, e, e)
    E.link(v.scalar_tensor_tensor(lg, lg, 0.0, ln, ALU.min, ALU.subtract))
    copy_out(E, rope_out(m)[0:2 * RH])
    E.phase()
    for h in range(RH):
        E.link(v.tensor_scalar(m.G[:, h, :], m.dneg, lg[:, RH + h:RH + h + 1], None, ALU.mult))
        v.scalar_tensor_tensor(m.G[:, h, :], m.dpos, lg[:, h:h + 1], m.G[:, h, :], ALU.mult, ALU.add).then_inc(K.decay_exponents, 1)
    E.link(v.tensor_scalar(m.mix[:, :, 0:512], m.mix[:, :, 0:512], 1.0, None, ALU.add))
    E.link(v.reciprocal(m.mix[:, :, 0:512], m.mix[:, :, 0:512]))
    E.link(v.tensor_tensor(m.ga, m.ga, m.mix[:, :, 0:512], ALU.mult))
    for h in range(RH + 1):
        if h < RH:
            v.wait_ge(K.decays_ready, h + 1)
            for i in range(T):
                n = E.take()
                E.wait_filled(n)
                E.evacuated(v.scalar_tensor_tensor(m.W[h % 2][:, i, :], E.bank(n), P ** -0.5,
                                                   m.G[:, h, P * (T - 1 - i):P * (T - 1 - i) + S], ALU.mult, ALU.mult), n)
        if h >= 1:
            n = E.take()
            E.wait_filled(n)
            E.evacuated(v.tensor_copy(m.mix[:, :, P * (h - 1):P * h], E.bank(n).rearrange("p (t d) -> p t d", t=T)), n)
    E.wait_evacuated(E.n - 8, E.n)
    ya = m.mix[:, :, 0:512].rearrange("p t (h d) -> p t h d", h=RH)
    sq = m.sq.rearrange("p (t h) d -> p t h d", t=T)
    mu, var, rs = (m.gst[:, i, :].rearrange("p (t h) -> p t h", t=T) for i in range(3))
    E.link(v.reduce_sum(mu, ya, AX))
    E.link(v.tensor_scalar(mu, mu, 1.0 / P, None, ALU.mult))
    for t in range(T):
        ins = v.tensor_tensor(ya[:, t], ya[:, t], mu[:, t].unsqueeze(2).to_broadcast([P, RH, P]), ALU.subtract)
    E.link(ins)
    for t in range(T):
        ins = v.tensor_tensor(sq[:, t], ya[:, t], ya[:, t], ALU.mult)
    E.link(ins)
    E.link(v.reduce_sum(var, sq, AX))
    E.link(v.tensor_scalar(var, var, 1.0 / P, EPS, ALU.mult, ALU.add))
    dve_rsqrt(E, rs, var, mu)
    for t in range(T):
        ins = v.tensor_tensor(ya[:, t], ya[:, t], rs[:, t].unsqueeze(2).to_broadcast([P, RH, P]), ALU.mult)
    E.link(ins)
    for t in range(T):
        ins = v.tensor_tensor(m.mix[:, t, 0:512], m.mix[:, t, 0:512], m.gn, ALU.mult)
    E.link(ins)
    E.link(v.tensor_tensor(m.mix[:, :, 0:512], m.mix[:, :, 0:512], m.ga, ALU.mult))
    E.phase()
    for b in range(2):
        v.memset(m.s[:, b, 0, 0:P], NEG)
        ins = v.memset(m.s[:, b, T - 1, 2 * P:3 * P], NEG)
    E.link(ins)
    v.wait_ge(K.mask_loaded, 16)
    copy_out(E, rope_out(m)[2 * RH:])
    dve_attention(E, K.window)
    E.phase()
    mixer_end_dve(E, m.mix, 0)


def mixer_end_dve(E, mix, layer):
    K = E.K
    if mix is not None:
        copy_out(E, xt_out(K.xT))
    n0 = E.n
    residual_out(E, K.x, 2, ALPHA)
    E.wait_evacuated(n0, E.n)
    E.eng.wait_ge(K.gains_loaded, 16 * 2 * (2 * layer + 1))
    dve_layer_norm(E, K.x, K.gains[:, 0, :], K.gains[:, 1, :], K.lnst)
    E.eng.drain().then_inc(K.norm_done, 1)
    copy_out(E, xt_out(K.xT))
    E.phase()



def fourier_views(K):
    A = K.carve(0)
    m = Names()
    m.feat = A(2, 512)
    m.cs, m.sn = A(T, S), A(T, S)
    m.z = A(T, 4, 512)
    return m


def pe_fourier(E):
    K, m, pe = E.K, E.K.fourier, E.eng
    pe.wait_ge(K.fourier_loaded, 16 * 3)
    n0 = E.n
    for t in range(T):
        for g in range(4):
            n = E.take()
            E.wait_bank(n)
            for k in range(2):
                mm = pe.matmul(E.bank(n), K.xT[:, 2 * g + k, P * t:P * t + P], m.feat[:, k, :], start=(k == 0), stop=(k == 1))
            E.filled(mm, n)
    E.wait_evacuated(n0, E.n)
    n0 = E.n
    for k in range(KD):
        g, c = k // 2, P * (k % 2)
        n = E.take()
        E.wait_bank(n)
        for t in range(T):
            pe.matmul(E.bank(n), m.z[:, t, g, c:c + P], m.cs[:, t, :], start=(t == 0), stop=False)
        for t in range(T):
            mm = pe.matmul(E.bank(n), m.z[:, t, g, 256 + c:256 + c + P], m.sn[:, t, :], start=False, stop=(t == T - 1))
        E.filled(mm, n)
    E.wait_evacuated(n0, E.n)
    mixer_end_pe(E, None, 3)


def fourier_out(E):
    K, m = E.K, E.K.fourier
    copy_out(E, [(m.z[:, t, g, :], lambda b: b, turn(g)) for t in range(T) for g in range(4)])
    copy_out(E, xt_out(K.xT))
    (mixer_end_act if E.name == "act" else lambda E, x: mixer_end_dve(E, x, 1))(E, None)



def moe_views(K):
    A = K.carve(0)
    m = Names()
    m.wr, m.br = A(KD, NG + NE), A(NG + NE)
    m.iota, m.iotag, m.iotaj = A(NE), A(NE), A(NOV, NE)
    m.tok = A(T)
    m.lg, m.cp, m.mx, m.fm = A(T, NG + NE), A(T, 8), A(T, 8), A(T, NE)
    m.ix, m.mk = A(T, 8), A(T, NE)
    m.one = A(2, T, NE)
    m.A, m.rk, m.tmp = A(T, NE), A(5, NE), A(T, NE)
    m.ov, m.ovend, m.extra, m.zero = A(NE), A(NE), A(NE), A(NE)
    m.c = A(16, T)
    m.slot = A(2, T)
    m.jt, m.jx, m.ja = A(8), A(NOV, NE), A(NOV, NE)
    m.idx, m.scr = A(1), A(1)
    m.zt = A(JOBS + 1)
    m.xs, m.xsT = A(D), A(KD, P)
    m.sg, m.hid, m.hidT, m.y = A(EH), A(EH), A(EH // P, P), A(D)
    m.g = A(2, T, D)
    return m


MOE_T = [(0, 3), (3, 6), (6, 8)]


def pe_skip(E, count):
    for _ in range(count):
        n = E.take()
        E.wait_bank(n)
        E.filled(E.eng.nop(), n)


def dve_skip(E, count):
    for _ in range(count):
        n = E.take()
        E.wait_filled(n)
        E.evacuated(E.eng.nop(), n)


def pe_moe(E, layer):
    K, m, pe = E.K, E.K.moe, E.eng
    pe.wait_ge(K.moe_loaded, 16 * K.MOE_DMAS * (layer + 1))
    n = E.take()
    E.wait_bank(n)
    for t in range(T):
        for k in range(KD):
            mm = pe.matmul(E.bank(n)[:, 36 * t:36 * t + 36], K.xT[:, k, P * t:P * t + P], m.wr[:, k, :],
                           start=(k == 0), stop=(k == KD - 1))
    E.filled(mm, n)
    pe.wait_ge(K.choices_ready, layer + 1)
    n = E.take()
    E.wait_bank(n)
    for t in range(T):
        for u in range(t + 1):
            pe.matmul(E.bank(n)[:, NE * t:NE * t + NE], K.before if u == t else K.ones, m.A[:, u, :],
                      start=(u == 0), stop=(u == t))
    for u in range(T):
        mm = pe.matmul(E.bank(n)[:, NE * T:NE * T + NE], K.ones, m.A[:, u, :], start=(u == 0), stop=(u == T - 1))
    E.filled(mm, n)

    def turn_rows():
        for lo, hi in MOE_T:
            n = E.take()
            E.wait_bank(n)
            for k in range(lo, hi):
                tr = pe.transpose(E.bank(n)[:, P * (k - lo):P * (k - lo) + P], m.xs[:, P * k:P * k + P], K.ident)
                if k == 0 and E.loop:
                    tr.then_inc(K.w_used, 1)
            E.filled(tr, n)

    xs0 = 16 * (JOBS + 1) * layer
    pe.wait_ge(K.xs_gathered, xs0 + 16)
    turn_rows()
    pe_skip(E, 3)
    w0 = E.w
    with pe.Fori(0, JOBS) as j:
        E.begin_loop(j, 8, 0)

        def weights(i):
            w = w0 + i
            pe.wait_ge(K.w_loaded[w % RING], j * 16 * (3 // RING) + 16 * (w // RING + 1))
            return K.ring[:, w % RING, :]

        for i in (2, 3, 4):
            E.wait_bank(E.n + i)
        for i in range(2):
            w = weights(i).rearrange("p (k n) -> p k n", k=KD)
            n = E.take()
            E.wait_bank(n)
            for k in range(KD):
                mm = pe.matmul(E.bank(n), m.xsT[:, k, :], w[:, k, :], start=(k == 0), stop=(k == KD - 1))
                if i == 1 and k == 0:
                    mm.then_inc(K.w_used, 1)
            E.filled(mm, n)
        pe.wait_ge(K.xs_gathered, j * 16 + (xs0 + 32))
        turn_rows()
        n = E.take()
        E.wait_evacuated(n - 4, n - 3)
        E.wait_bank(n)
        for i in range(EH // P):
            tr = pe.transpose(E.bank(n)[:, P * i:P * i + P], m.hid[:, P * i:P * i + P], K.ident)
        E.filled(tr, n)
        E.wait_evacuated(n, n + 1)
        w = weights(2).rearrange("p (k n) -> p k n", k=EH // P)
        for half in range(2):
            n = E.take()
            E.wait_bank(n)
            for k in range(EH // P):
                mm = pe.matmul(E.bank(n), m.hidT[:, k, :], w[:, k, WT * half:WT * half + WT],
                               start=(k == 0), stop=(k == EH // P - 1))
            E.filled(mm, n)
        pe.drain().then_inc(K.w_used, 1)
        E.end_loop(JOBS)
    E.w = w0 + 3 * JOBS


def act_moe(E, layer):
    K, m, s = E.K, E.K.moe, E.eng
    s.wait_ge(K.norm_done, 2 * layer + 1)
    s.dma_start(K.xg_dram.rearrange("(t p) d -> p t d", p=P), K.x).then_inc(K.rows_stored, 16)
    E.n += 1
    s.wait_ge(K.router_dve, 2 * layer + 1)
    s.activation(m.cp[:, :, 0:4], m.cp[:, :, 0:4], ACT.Exp).then_inc(K.router_act, 1)
    s.wait_ge(K.router_dve, 2 * layer + 2)
    s.activation(m.c[:, 3, :], m.c[:, 3, :], ACT.Exp).then_inc(K.router_act, 1)
    E.n += 1

    def rows_out():
        for (lo, hi), who in zip(MOE_T, ("act", "dve", "act")):
            copy_out(E, [(m.xsT[:, lo:hi, :].rearrange("p k t -> p (k t)"), lambda b, c=hi - lo: b[:, 0:P * c], who)])

    rows_out()
    E.n += 3
    st0 = 16 * (JOBS + 1) * layer + 16
    with s.Fori(0, JOBS) as j:
        E.begin_loop(j, 8, 0)
        n = E.take()
        E.wait_filled(n)
        E.wait_bank(E.n)
        E.evacuated(s.activation(m.sg, E.bank(n), ACT.Silu), n)
        E.n += 1
        rows_out()
        E.n += 1
        s.wait_ge(K.rows_stored, j * 16 + st0)
        n = E.take()
        E.wait_filled(n)
        E.evacuated(s.activation(m.y[:, 0:WT], E.bank(n), ACT.Copy), n)
        n = E.take()
        E.wait_evacuated(n - 1, n + 1)
        s.dma_start(K.ys_dram[bass.ds(j * P, P), :], m.y).then_inc(K.rows_stored, 16)
        E.end_loop(JOBS)


def dve_moe(E, layer):
    K, m, v = E.K, E.K.moe, E.eng
    L = E.link
    c = lambda i: m.c[:, i, :]
    v.wait_ge(K.moe_loaded, 16 * K.MOE_DMAS * (layer + 1))
    v.memset(m.cp, NEG)
    L(v.memset(m.zero, 0.0))
    n = E.take()
    E.wait_filled(n)
    E.evacuated(v.tensor_tensor(m.lg, E.bank(n)[:, 0:T * 36].rearrange("p (t e) -> p t e", t=T),
                                m.br.unsqueeze(1).to_broadcast([P, T, 36]), ALU.add), n)
    E.wait_evacuated(n, n + 1)
    L(v.tensor_copy(m.cp[:, :, 0:NG], m.lg[:, :, 0:NG]))
    for t in range(T):
        ins = v.max(m.mx[:, t, :], m.cp[:, t, :])
    L(ins)
    for t in range(T):
        ins = v.max_index(m.ix.bitcast(U32)[:, t, :], m.mx[:, t, :], m.cp[:, t, :])
    L(ins)
    L(v.tensor_copy(c(0), m.ix.bitcast(U32)[:, :, 0]))
    v.tensor_tensor(m.cp[:, :, 0:NG], m.lg[:, :, 0:NG], m.mx[:, :, 0:1].to_broadcast([P, T, NG]),
                    ALU.subtract).then_inc(K.router_dve, 1)
    for t in range(T):
        ins = v.tensor_scalar(m.mk[:, t, :], m.iotag, m.c[:, 0, t:t + 1], None, ALU.is_equal)
    L(ins)
    v.wait_ge(K.router_act, 2 * layer + 1)
    L(v.reduce_sum(c(1), m.cp[:, :, 0:NG], AX))
    L(v.reciprocal(c(1), c(1)))
    L(v.tensor_tensor(m.fm, m.lg[:, :, NG:], m.mk, ALU.mult))
    L(v.tensor_scalar(m.mk, m.mk, -NEG, NEG, ALU.mult, ALU.add))
    L(v.tensor_tensor(m.fm, m.fm, m.mk, ALU.add))
    for t in range(T):
        ins = v.max(m.mx[:, t, :], m.fm[:, t, :])
    L(ins)
    for t in range(T):
        ins = v.max_index(m.ix.bitcast(U32)[:, t, :], m.mx[:, t, :], m.fm[:, t, :])
    L(ins)
    v.tensor_tensor(c(3), m.mx[:, :, 1], m.mx[:, :, 0], ALU.subtract).then_inc(K.router_dve, 1)
    for k in range(2):
        ins = v.tensor_copy(c(4 + k), m.ix.bitcast(U32)[:, :, k])
    L(ins)
    for k in range(2):
        for t in range(T):
            ins = v.tensor_scalar(m.one[:, k, t, :], m.iota, m.c[:, 4 + k, t:t + 1], None, ALU.is_equal)
    L(ins)
    v.tensor_tensor(m.A, m.one[:, 0], m.one[:, 1], ALU.add).then_inc(K.choices_ready, 1)
    v.wait_ge(K.router_act, 2 * layer + 2)
    L(v.tensor_scalar(c(6), c(3), 1.0, None, ALU.add))
    L(v.reciprocal(c(6), c(6)))
    L(v.tensor_tensor(c(6), c(6), c(1), ALU.mult))
    L(v.tensor_tensor(c(7), c(6), c(3), ALU.mult))
    n = E.take()
    E.wait_filled(n)
    E.evacuated(v.tensor_copy(m.rk, E.bank(n)[:, 0:5 * NE].rearrange("p (a e) -> p a e", a=5)), n)
    E.wait_evacuated(n, n + 1)
    cnt = m.rk[:, T, :]
    L(v.tensor_scalar(m.extra, cnt, P + 0.5, None, ALU.is_gt))
    for q in (2, 3):
        L(v.scalar_tensor_tensor(m.extra, cnt, P * q + 0.5, m.extra, ALU.is_gt, ALU.add))
    L(v.tensor_tensor_scan(m.ovend, m.extra, m.zero, 0.0, ALU.add, ALU.add))
    L(v.tensor_tensor(m.ov, m.ovend, m.extra, ALU.subtract))
    for k in range(2):
        r, o, ch, nz, e = c(8), c(9), c(10), c(11), c(4 + k)
        L(v.tensor_tensor(m.tmp, m.rk[:, 0:T, :], m.one[:, k], ALU.mult))
        L(v.reduce_sum(r, m.tmp, AX))
        L(v.tensor_tensor(m.tmp, m.ov.unsqueeze(1).to_broadcast([P, T, NE]), m.one[:, k], ALU.mult))
        L(v.reduce_sum(o, m.tmp, AX))
        L(v.tensor_scalar(nz, r, P - 0.5, None, ALU.is_gt))
        L(v.scalar_tensor_tensor(ch, r, 2 * P - 0.5, nz, ALU.is_gt, ALU.add))
        L(v.scalar_tensor_tensor(ch, r, 3 * P - 0.5, ch, ALU.is_gt, ALU.add))
        L(v.tensor_tensor(o, o, ch, ALU.add))
        L(v.tensor_tensor(o, o, e, ALU.subtract))
        L(v.scalar_tensor_tensor(o, o, NE - 1.0, nz, ALU.add, ALU.mult))
        L(v.tensor_tensor(o, o, e, ALU.add))
        L(v.tensor_tensor(o, o, ch, ALU.subtract))
        L(v.scalar_tensor_tensor(o, o, float(P), r, ALU.mult, ALU.add))
        L(v.tensor_copy(m.slot.bitcast(I32)[:, k, :], o))
    ovb = m.ov.unsqueeze(1).to_broadcast([P, NOV, NE])
    oveb = m.ovend.unsqueeze(1).to_broadcast([P, NOV, NE])
    v.tensor_tensor(m.jx, m.iotaj, ovb, ALU.is_ge)
    L(v.tensor_tensor(m.ja, m.iotaj, oveb, ALU.is_lt))
    L(v.tensor_tensor(m.jx, m.jx, m.ja, ALU.mult))
    L(v.tensor_tensor(m.jx, m.jx, m.iota.unsqueeze(1).to_broadcast([P, NOV, NE]), ALU.mult))
    L(v.reduce_sum(m.ja[:, 0, 0:NOV], m.jx, AX))
    L(v.tensor_copy(m.jt.bitcast(I32)[:, 0:NOV], m.ja[:, 0, 0:NOV]))
    v.drain().then_inc(K.slots_ready, 1)

    def rows_out():
        for (lo, hi), who in zip(MOE_T, ("act", "dve", "act")):
            copy_out(E, [(m.xsT[:, lo:hi, :].rearrange("p k t -> p (k t)"), lambda b, cc=hi - lo: b[:, 0:P * cc], who)])

    rows_out()
    dve_skip(E, 3)
    st0 = 16 * (JOBS + 1) * layer + 16
    with v.Fori(0, JOBS) as j:
        E.begin_loop(j, 8, 0)
        gate, up = E.take(), E.take()
        E.wait_evacuated(gate, gate + 1)
        E.wait_filled(up)
        E.evacuated(v.tensor_tensor(m.hid, m.sg, E.bank(up), ALU.mult), up)
        rows_out()
        copy_out(E, [(m.hidT.rearrange("p k t -> p (k t)"), lambda b: b, "dve")])
        E.n += 1
        v.wait_ge(K.rows_stored, j * 16 + st0)
        copy_out(E, [(m.y[:, WT:D], lambda b: b, "dve")])
        E.end_loop(JOBS)
    L(v.tensor_scalar(K.x, K.x, ALPHA, None, ALU.mult))
    v.wait_ge(K.y_gathered, 16 * 2 * T * (layer + 1))
    for k in range(2):
        for t in range(T):
            ins = v.scalar_tensor_tensor(K.x[:, t, :], m.g[:, k, t, :], m.c[:, 6 + k, t:t + 1], K.x[:, t, :], ALU.mult, ALU.add)
        L(ins)
    v.wait_ge(K.gains_loaded, 16 * 2 * (2 * layer + 2))
    dve_layer_norm(E, K.x, K.gains[:, 0, :], K.gains[:, 1, :], K.lnst)
    v.drain().then_inc(K.norm_done, 1)


def pool_moe(E, layer):
    K, m, g = E.K, E.K.moe, E.eng
    g.dma_start(m.wr[:, :, NG:], K.d.router_fine_w[layer].rearrange("(k p) e -> p k e", p=P)).then_inc(K.moe_loaded, 16)
    g.dma_start(m.wr[:, :, 0:NG], K.d.router_coarse_w[layer].rearrange("(k p) e -> p k e", p=P)).then_inc(K.moe_loaded, 16)
    g.dma_start(m.br[:, 0:NG], K.d.router_coarse_b[layer:layer + 1, :].to_broadcast([P, NG])).then_inc(K.moe_loaded, 16)
    g.dma_start(m.br[:, NG:], K.d.router_fine_b[layer:layer + 1, :].to_broadcast([P, NE])).then_inc(K.moe_loaded, 16)
    g.dma_start(m.iota, K.d.c_iota).then_inc(K.moe_loaded, 16)
    g.dma_start(m.iotag, K.d.c_iotag).then_inc(K.moe_loaded, 16)
    g.dma_start(m.iotaj, K.d.c_iotaj).then_inc(K.moe_loaded, 16)
    g.dma_start(m.tok.bitcast(I32), K.d.c_tok).then_inc(K.moe_loaded, 16)
    g.memset(m.zt, 0.0).then_inc(K.table_zero, 1)
    g.wait_ge(K.table_zero, layer + 1)
    g.dma_start(K.slot_dram.rearrange("(p j) o -> p (j o)", p=P), m.zt.bitcast(I32)).then_inc(K.table_cleared, 16)
    g.wait_ge(K.norm_done, 2 * layer + 1)
    load_gains(E, K.d.ln2_gain[layer:layer + 1, :], K.d.ln2_bias[layer:layer + 1, :])
    g.wait_ge(K.table_cleared, 16 * (layer + 1))
    g.wait_ge(K.moe_loaded, 16 * K.MOE_DMAS * (layer + 1))
    g.wait_ge(K.slots_ready, layer + 1)
    for k in range(2):
        for t in range(T):
            i = (2 * layer + k) * T + t
            g.indirect_dma_start(out=K.slot_dram, out_offset=bass.IndirectOffsetOnAxis(ap=m.slot.bitcast(U32)[:, k, t:t + 1], axis=0),
                                 in_=m.tok.bitcast(I32)[:, t:t + 1], in_offset=None).then_inc(K.slots_stored, 16)
    g.wait_ge(K.slots_stored, 16 * 2 * T * (layer + 1))
    base = 16 * (JOBS + 1) * layer
    g.wait_ge(K.rows_stored, base + 16)

    def gather(src, idx_done, passed):
        g.dma_start(m.idx.bitcast(I32), src).then_inc(K.idx_loaded, 16)
        g.wait_ge(K.idx_loaded, idx_done)
        if passed is not None:
            g.wait_ge(K.idx_passed, passed)
        g.tensor_tensor(m.scr, m.zt[:, 0:1], m.zt[:, 0:1], ALU.add).then_inc(K.idx_passed, 1)
        g.indirect_dma_start(out=m.xs, out_offset=None, in_=K.xg_dram,
                             in_offset=bass.IndirectOffsetOnAxis(ap=m.idx.bitcast(U32), axis=0)).then_inc(K.xs_gathered, 16)

    E.n += 2
    gather(K.slot_dram[0:P, :], base + 16, (JOBS + 1) * layer or None)
    E.n += 6
    with g.Fori(0, JOBS) as j:
        E.begin_loop(j, 8, 0)
        E.eng.wait_ge(K.bank_filled[(E.n + 4) % 8], E.gen(E.n + 4))
        g.wait_ge(K.xs_gathered, j * 16 + (base + 16))
        gather(K.slot_dram[bass.ds(j * P + P, P), :], j * 16 + (base + 32),
               j + ((JOBS + 1) * layer + 1))
        E.n += 8
        E.end_loop(JOBS)
    g.wait_ge(K.rows_stored, base + 16 * (JOBS + 1))
    for k in range(2):
        for t in range(T):
            g.indirect_dma_start(out=m.g[:, k, t, :], out_offset=None, in_=K.ys_dram,
                                 in_offset=bass.IndirectOffsetOnAxis(ap=m.slot.bitcast(U32)[:, k, t:t + 1], axis=0)).then_inc(K.y_gathered, 16)


def load_gains(E, *rows):
    for i, row in enumerate(rows):
        E.eng.dma_start(E.K.gains[:, i, :], row.to_broadcast([P, D])).then_inc(E.K.gains_loaded, 16)


def pool_even(E):
    K, m, g, d = E.K, E.K.even, E.eng, E.K.d
    g.dma_start(K.x, d.x[0].rearrange("(t p) d -> p t d", p=P)).then_inc(K.x_loaded, 16)
    for dst, src in ((K.ident, d.c_ident), (K.ones, d.c_ones), (K.before, d.c_before), (K.upto, d.c_upto), (K.since, d.c_since)):
        g.dma_start(dst, src).then_inc(K.consts_loaded, 16)
    loads = [(m.cos128, d.c_cos128), (m.sin128, d.c_sin128), (m.cos64, d.c_cos64), (m.sin64, d.c_sin64),
             (m.dpos, d.c_dpos), (m.dneg, d.c_dneg),
             (m.gn, d.ret_gn_gain.to_broadcast([P, RH * P])),
             (m.lg[:, 0:8], d.ret_decay_logit.rearrange("a b h -> a (b h)").to_broadcast([P, 8])),
             (m.sink, d.sink_logit.to_broadcast([P, WQ]))]
    assert len(loads) == K.EVEN_DMAS
    for dst, src in loads:
        g.dma_start(dst, src).then_inc(K.even_loaded, 16)
    load_gains(E, d.ln1_gain[0:1, :], d.ln1_bias[0:1, :])
    for _ in range(3):
        E.phase()
    g.dma_start(m.mask, d.c_mask).then_inc(K.mask_loaded, 16)
    E.phase()
    E.phase()
    E.n = K.after_even


def pool_fourier(E):
    K, m, g, d = E.K, E.K.fourier, E.eng, E.K.d
    g.dma_start(m.feat, d.c_feat).then_inc(K.fourier_loaded, 16)
    g.dma_start(m.cs, d.c_cs).then_inc(K.fourier_loaded, 16)
    g.dma_start(m.sn, d.c_sn).then_inc(K.fourier_loaded, 16)
    load_gains(E, d.ln1_gain[1:2, :], d.ln1_bias[1:2, :])
    E.phase()
    E.n += 16 + KD + 2 * T + KD



def second_views(K):
    A = K.carve(0)
    m = Names()
    m.mix = A(T, D)
    m.gates = A(36, T)
    m.small = A(13, T, 12)
    m.par = A(2 * MLH * 2 + 2 * GDH * 2)
    m.nw = K.gains[:, 1, 512:512 + GDH * HD]
    base = A.at
    m.h = A(T, W2_ML)
    m.bias, m.near, m.far = A(NAH, 14, HD), A(HD), A(HD)
    m.nqT, m.nkT = A(NAH, S)[0:HD], A(NAH, S)[0:HD]
    m.s, m.pT, m.st = A(2, T, S), A(2, 16, P), A(2, 5, T)
    A.at = base
    m.hm = A(T, C2_MLE)
    m.mqT, m.mkT = A(MLH, S)[0:HD], A(MLH, S)[0:HD]
    m.ST, m.W, m.Dm = A(T, S), A(2, T, S), A(2, T, S)
    m.v1 = A(T, MLH, HD + 1)
    m.hs, m.ex = A(T, 256), A(T, 256)
    m.hsq = m.Dm[:, 0].rearrange("p a c -> p (a c)")[:, 0:T * 256].rearrange("p (t c) -> p t c", t=T)
    m.rows, m.zrow = A(2, S), A(S)
    m.norm = A(2, T, HD + 1)
    A.at = base
    m.hz = A(T, C2_ZE)
    m.tm = A(T, GDC)
    m.levels = A(2, LEVELS, P)
    base = A.at
    m.cin, m.cout = A(GCT, S + 4), A(GCT, S)
    m.cw = A(GCT, 5)
    m.gtmp = A(T, 2 * GDH * HD)
    A.at = base
    m.gqT, m.gkT = A(GDH, S)[0:HD], A(GDH, S)[0:HD]
    U = (4, 3, P)
    V = (4, 3, HD)
    m.E, m.AT, m.X = A(*U), A(*U), A(*U)
    m.at = m.E
    m.qd, m.nw_T = A(*U)[0:HD], A(*U)[0:HD]
    m.vb, m.kbe, m.ks, m.vn = A(*V), A(*V), A(*V), A(*V)
    spare = K.xT.rearrange("p k s -> p (k s)")
    size = 12 * P
    m.Ti, m.TiT = (spare[:, size * i:size * i + size].rearrange("p (g u l) -> p g u l", g=4, u=3) for i in range(2))
    m.state = spare[0:HD, 2 * size:2 * size + 2 * GDH * HD].rearrange("p (h d) -> p h d", h=2 * GDH)
    m.o = K.gains.rearrange("p a d -> p (a d)")[:, 0:T * GDH * HD].rearrange("p (t c) -> p t c", t=T)
    flat = lambda ap: ap.rearrange("p g u l -> p (g u l)").rearrange("p (t c) -> p t c", t=T)
    m.osq, m.ez = flat(m.AT), flat(m.Ti)
    return m


def cross_views(K):
    A = K.carve(0)
    m = Names()
    m.hn, m.mem = A(T, D), A(2, D)
    m.memT = A(KD, MEMN)
    m.qT, m.kT, m.v = A(KD, S), A(KD, MEMN), A(2, D)
    m.s, m.pT, m.st = A(2, T, MEMN), A(2, 8, P), A(2, 5, T)
    m.mix = m.hn
    m.tmp, m.nst = A(D), A(T, 4)
    m.gain = A(D)
    return m


def ffn_views(K):
    A = K.carve(0)
    m = Names()
    m.hT = A(FFT, S)
    m.hn = A(T, D)
    m.tmp, m.nst = A(D), A(T, 4)
    m.r = A(2, S)
    return m


NEAR_WIDTHS = [512, 512, W2_ML - 1024]
ML_WIDTHS = [512, 512, C2_MLE - 1024]


def near_attention(K):
    m = K.second
    a = Names()
    a.name = "near"
    a.heads = NAH
    a.scale = HD ** -0.5
    a.dv = HD
    a.s = m.s
    a.pT = m.pT
    a.st = m.st
    a.blocks = [list(range(T))] * T
    a.cols = lambda n: (0, S)
    a.scores = lambda h, n: [(m.nqT[:, h, P * n:P * n + P], m.nkT[:, h, :])]
    a.addend = lambda h, n: m.bias[:, h, 6 - 2 * n:14 - 2 * n, :].rearrange("p r c -> p (r c)")
    a.sink = lambda h: None
    a.value = lambda h, j: m.h[:, j, C2_NAV + HD * h:C2_NAV + HD * h + HD]
    a.out = lambda h, lo, hi: m.mix[:, lo:hi, HD * h:HD * h + HD]
    return att_plan(a)


def cross_attention(K):
    m = K.cross
    a = Names()
    a.name = "memory"
    a.heads = XH
    a.scale = XD ** -0.5
    a.dv = XD
    a.s = m.s
    a.pT = m.pT
    a.st = m.st
    a.blocks = [[0, 1]] * T
    a.cols = lambda n: (0, MEMN)
    a.scores = lambda h, n: [(m.qT[:, 2 * h + i, P * n:P * n + P], m.kT[:, 2 * h + i, :]) for i in range(2)]
    a.addend = lambda h, n: None
    a.sink = lambda h: None
    a.value = lambda h, j: m.v[:, j, XD * h:XD * h + XD]
    a.out = lambda h, lo, hi: m.mix[:, lo:hi, XD * h:XD * h + XD]
    return att_plan(a)


def head_tasks(src, heads, dst, who=None):
    tasks = [[src[:, t, HD * h:HD * h + HD] for t in range(T)] for h in range(heads)]
    return tasks, [(dst[:, h, :], lambda b: b[0:HD], who or turn(h)) for h in range(heads)]


def second_head_tasks(m):
    a = head_tasks(m.h[:, :, C2_NAQ:C2_NAK], NAH, m.nqT)
    b = head_tasks(m.h[:, :, C2_NAK:C2_NAV], NAH, m.nkT)
    return a[0] + b[0], a[1] + b[1]


def ml_head_tasks(m):
    a = head_tasks(m.hm[:, :, C2_MLQ:C2_MLK], MLH, m.mqT)
    b = head_tasks(m.hm[:, :, C2_MLK:C2_MLV], MLH, m.mkT)
    return a[0] + b[0], a[1] + b[1]


def ml_tiles(dir, i):
    return (i, T) if dir == 0 else (0, i + 1)


def pe_mlstm(E):
    K, m, pe = E.K, E.K.second, E.eng
    n0 = E.n
    pe_transposes(E, ml_head_tasks(m)[0])
    pe.wait_ge(K.ml_gates, 1)
    n = E.take()
    E.wait_bank(n)
    lf = m.small[:, 0]
    for t in range(T):
        for dir in range(2):
            others = [u for u in range(T) if (u < t if dir == 0 else u > t)]
            for i, u in enumerate([t] + others):
                mm = pe.matmul(E.bank(n)[:, 8 * t + 4 * dir:8 * t + 4 * dir + 4], (K.upto, K.since)[dir] if u == t else K.ones,
                               lf[:, u, 4 * dir:4 * dir + 4], start=(i == 0), stop=(i == len(others)))
    E.filled(mm, n)
    pe.wait_ge(K.ml_gates, 2)
    a = m.small[:, 3]
    pe_transposes(E, [[a[:, t, 4 * dir:4 * dir + 4] for t in range(T)] for dir in range(2)])
    pe.wait_ge(K.ml_gates, 3)
    n = E.take()
    E.wait_bank(n)
    for dir in range(2):
        for t in range(T):
            tr = pe.transpose(E.bank(n)[:, 16 * dir + 4 * t:16 * dir + 4 * t + 4], m.rows[0:4, dir, P * t:P * t + P], K.ident[0:4, 0:4])
    E.filled(tr, n)
    E.wait_evacuated(n0, n0 + 2 * MLH)
    for h in range(MLH):
        for i in range(T):
            n = E.take()
            E.wait_bank(n)
            E.filled(pe.matmul(E.bank(n), m.mkT[:, h, P * i:P * i + P], m.mqT[:, h, :], start=True, stop=True), n)
        for dir in range(2):
            n = E.take()
            E.wait_bank(n)
            E.filled(pe.matmul(E.bank(n), K.ident[0:4, h:h + 1].to_broadcast([4, P]), m.rows[0:4, dir, :],
                               start=True, stop=True), n)
        for dir in range(2):
            pe.wait_ge(K.ml_weights, 2 * h + dir + 1)
            n = E.take()
            E.wait_bank(n)
            for t in range(T):
                keys = [i for i in range(T) if ml_tiles(dir, i)[0] <= t < ml_tiles(dir, i)[1]]
                for i in keys:
                    mm = pe.matmul(E.bank(n)[:, (HD + 1) * t:(HD + 1) * (t + 1)], m.W[:, dir, i, P * t:P * t + P], m.v1[:, i, h, :],
                                   start=(i == keys[0]), stop=(i == keys[-1]))
            E.filled(mm, n)


def act_mlstm(E):
    K, m, s = E.K, E.K.second, E.eng
    copy_out(E, ml_head_tasks(m)[1])
    sm = lambda i: m.small[:, i, :, 0:8]
    s.wait_ge(K.ml_dve, 1)
    s.activation(sm(1), sm(1), ACT.Exp, scale=-1.0).then_inc(K.ml_act, 1)
    s.wait_ge(K.ml_dve, 2)
    s.activation(sm(5), sm(2), ACT.Ln).then_inc(K.ml_act, 1)
    s.wait_ge(K.ml_dve, 3)
    s.activation(sm(6), sm(6), ACT.Exp, scale=-1.0).then_inc(K.ml_act, 1)
    s.activation(m.ex, m.hm[:, :, C2_MLO:C2_MLI], ACT.Exp, scale=-1.0).then_inc(K.ml_act, 1)
    E.n += 4
    for h in range(MLH):
        if h:
            E.wait_filled(E.n - 1)
        for i in range(T):
            n = E.take()
            E.wait_filled(n)
            if h and i == 0:
                s.wait_ge(K.ml_weights, 2 * h)
            E.evacuated(s.activation(m.ST[:, i, :], E.bank(n), ACT.Copy, scale=HD ** -0.5), n)
        E.n += 2
        for dir in range(2):
            s.wait_ge(K.ml_exponents, 2 * h + dir + 1)
            for i in range(T):
                lo, hi = ml_tiles(dir, i)
                ins = s.activation(m.W[:, dir, i, P * lo:P * hi], m.Dm[:, dir, i, P * lo:P * hi], ACT.Exp, scale=-1.0)
            ins.then_inc(K.ml_exps, 1)
        E.n += 2


def dve_mlstm(E):
    K, m, v = E.K, E.K.second, E.eng
    L = E.link
    copy_out(E, ml_head_tasks(m)[1])
    sm = lambda i: m.small[:, i, :, 0:8]
    pi, pf = m.par[:, 0:8], m.par[:, 8:16]
    lf, e, u, a, F, ln, fl, igc = (sm(i) for i in range(8))
    for t in range(T):
        v.tensor_tensor(igc[:, t], m.hm[:, t, C2_MLI:C2_MLF], pi, ALU.add)
        ins = v.tensor_tensor(lf[:, t], m.hm[:, t, C2_MLF:C2_MLE], pf, ALU.add)
    L(ins)
    v.scalar_tensor_tensor(e, lf, -1.0, lf, ALU.mult, ALU.max).then_inc(K.ml_dve, 1)
    v.wait_ge(K.ml_act, 1)
    v.tensor_scalar(u, e, 1.0, None, ALU.add).then_inc(K.ml_dve, 1)
    v.wait_ge(K.ml_dve, 2)
    v.wait_ge(K.ml_act, 2)
    dve_log1p_end(E, ln, ln, u, e, e)
    v.scalar_tensor_tensor(lf, lf, 0.0, ln, ALU.min, ALU.subtract).then_inc(K.ml_gates, 1)
    L(v.memset(m.v1, 1.0))
    for h in range(MLH):
        v.tensor_copy(m.v1[:, :, h, 0:HD], m.hm[:, :, C2_MLV + HD * h:C2_MLV + HD * h + HD])
    L(v.memset(m.zrow, 0.0))
    n = E.take()
    E.wait_filled(n)
    E.evacuated(v.tensor_copy(F, E.bank(n)[:, 0:32].rearrange("p (t c) -> p t c", t=T)), n)
    E.wait_evacuated(n, n + 1)
    v.tensor_tensor(a, igc, F, ALU.subtract).then_inc(K.ml_gates, 1)
    v.wait_ge(K.ml_gates, 2)
    for dir in range(2):
        n = E.take()
        E.wait_filled(n)
        E.evacuated(v.tensor_copy(m.rows[0:4, dir, :], E.bank(n)[0:4, :]), n)
    E.wait_evacuated(n - 1, n + 1)
    L(v.tensor_tensor_scan(m.rows[0:4, 0, :], m.rows[0:4, 0, :], m.zrow[0:4, :], 0.0, ALU.max, ALU.max))
    v.tensor_tensor_scan(m.rows[0:4, 1, ::-1], m.rows[0:4, 1, ::-1], m.zrow[0:4, :], 0.0, ALU.max, ALU.max).then_inc(K.ml_gates, 1)
    n = E.take()
    E.wait_filled(n)
    for dir in range(2):
        ins = v.tensor_tensor(fl[:, :, 4 * dir:4 * dir + 4], F[:, :, 4 * dir:4 * dir + 4],
                              E.bank(n)[:, 16 * dir:16 * dir + 16].rearrange("p (t c) -> p t c", t=T), ALU.add)
    E.evacuated(ins, n)
    E.wait_evacuated(n, n + 1)
    v.nop().then_inc(K.ml_dve, 1)
    for h in range(MLH):
        n0 = E.n
        E.n += T
        for dir in range(2):
            n = E.take()
            E.wait_filled(n)
            for i in range(T):
                lo, hi = ml_tiles(dir, i)
                ins = v.tensor_scalar(m.Dm[:, dir, i, P * lo:P * hi], E.bank(n)[:, P * lo:P * hi],
                                      m.small[:, 3, i, 4 * dir + h:4 * dir + h + 1], 0.0, ALU.subtract, ALU.max)
                if i == T - 1:
                    E.evacuated(ins, n)
            E.wait_evacuated(n, n + 1)
            v.nop().then_inc(K.ml_exponents, 1)
        E.wait_evacuated(n0, n0 + T)
        for dir in range(2):
            v.wait_ge(K.ml_exps, 2 * h + dir + 1)
            for i in range(T):
                d = m.W[:, dir, i, P * i:P * i + P]
                ins = v.tensor_tensor(d, d, (K.upto, K.since)[dir], ALU.mult)
            L(ins)
            for i in range(T):
                lo, hi = ml_tiles(dir, i)
                w = m.W[:, dir, i, P * lo:P * hi]
                ins = v.tensor_tensor(w, w, m.ST[:, i, P * lo:P * hi], ALU.mult)
            ins.then_inc(K.ml_weights, 1)
        if h == 0:
            v.wait_ge(K.ml_act, 4)
        for dir in range(2):
            n = E.take()
            E.wait_filled(n)
            b = E.bank(n)[:, 0:T * (HD + 1)].rearrange("p (t d) -> p t d", t=T)
            dn = m.gates[:, 2 * dir, :]
            rn = m.gates[:, 2 * dir + 1, :]
            L(v.tensor_copy(dn, b[:, :, HD]))
            L(v.scalar_tensor_tensor(dn, dn, -1.0, dn, ALU.mult, ALU.max))
            L(v.tensor_tensor(dn, dn, m.small[:, 6, :, 4 * dir + h], ALU.max))
            L(v.reciprocal(rn, dn))
            out = m.hs[:, :, HD * h:HD * h + HD] if dir == 0 else m.norm[:, 0, :, 0:HD]
            E.evacuated(v.tensor_tensor(out, b[:, :, 0:HD], rn.unsqueeze(2).to_broadcast([P, T, HD]), ALU.mult), n)
        E.wait_evacuated(n - 1, n + 1)
        L(v.tensor_tensor(m.hs[:, :, HD * h:HD * h + HD], m.hs[:, :, HD * h:HD * h + HD], m.norm[:, 0, :, 0:HD], ALU.add))
    dve_head_norm(E, m.hs, m.hsq, m.gates, MLH)
    v.wait_ge(K.nw_loaded, 16)
    L(v.tensor_scalar(m.ex, m.ex, 1.0, None, ALU.add))
    L(v.reciprocal(m.ex, m.ex))
    for t in range(T):
        ins = v.tensor_tensor(m.hs[:, t], m.hs[:, t], m.nw[:, 0:256], ALU.mult)
    L(ins)
    L(v.tensor_tensor(m.mix[:, :, NAH * HD:NAH * HD + 256], m.hs, m.ex, ALU.mult))


def dve_head_norm(E, x, sq, cols, heads):
    v = E.eng
    x4 = x.rearrange("p t (h d) -> p t h d", h=heads)
    c = cols[:, 4:4 + heads, :].rearrange("p h t -> p t h")
    E.link(v.tensor_tensor(sq, x, x, ALU.mult))
    for h in range(heads):
        ins = v.reduce_sum(cols[:, 4 + h, :], sq[:, :, HD * h:HD * h + HD], AX)
    E.link(ins)
    E.link(v.tensor_scalar(cols[:, 10:10 + heads, :], cols[:, 4:4 + heads, :], 1.0 / HD, EPS, ALU.mult, ALU.add))
    dve_rsqrt(E, cols[:, 4:4 + heads, :], cols[:, 10:10 + heads, :], cols[:, 16:16 + heads, :])
    for t in range(T):
        ins = v.tensor_tensor(x4[:, t], x4[:, t], c[:, t].unsqueeze(2).to_broadcast([P, heads, HD]), ALU.mult)
    E.link(ins)



GROUPS = [(dir, half) for dir in range(2) for half in range(2)]


def chunk(dir, step):
    return step if dir == 0 else T - 1 - step


def pe_gdn(E):
    K, m, pe = E.K, E.K.second, E.eng
    pe_linear(E, K.xT, [C2_ZE])
    for width in (512, 512, 128):
        w = pe_weights(E).rearrange("p (k n) -> p k n", k=KD)
        for c in range(width // P):
            n = E.take()
            E.wait_bank(n)
            for k in range(KD):
                mm = pe.matmul(E.bank(n), w[:, k, P * c:P * c + P], K.xT[:, k, :], start=(k == 0), stop=(k == KD - 1))
            E.filled(mm, n)
        pe.drain().then_inc(K.w_used, 1)
    pe.wait_ge(K.conv_done, 1)
    pe_transposes(E, [[m.cout[:, c, P * t:P * t + P] for t in range(T)] for c in range(GCT)])
    pe.wait_ge(K.gd_gates, 1)
    n = E.take()
    E.wait_bank(n)
    g = m.small[:, 0]
    for dir in range(2):
        for t in range(T):
            pe.matmul(E.bank(n)[:, 12 * t + 6 * dir:12 * t + 6 * dir + 6], (K.upto, K.since)[dir], g[:, t, 6 * dir:6 * dir + 6],
                      start=True, stop=True)
    for t in range(T):
        mm = pe.matmul(E.bank(n)[:, 48 + 12 * t:60 + 12 * t], K.ones, g[:, t, :], start=True, stop=True)
    E.filled(mm, n)
    E.phase()
    n0 = E.n
    pe.wait_ge(K.gd_normed, 1)
    pe_transposes(E, head_tasks(m.tm[:, :, 0:384], GDH, m.gqT)[0])
    pe_transposes(E, head_tasks(m.tm[:, :, 384:768], GDH, m.gkT)[0])
    E.wait_evacuated(n0, E.n)

    def each(body):
        for gi, (dir, half) in enumerate(GROUPS):
            n = E.take()
            E.wait_bank(n)
            for u in range(3):
                mm = body(E.bank(n), gi, dir, 3 * half + u, u)
            E.filled(mm, n)

    cols = lambda u: slice(P * u, P * u + P)
    for step in range(T):
        tk = lambda dir: slice(P * chunk(dir, step), P * chunk(dir, step) + P)
        g = lambda dir, h: m.small[:, 0, chunk(dir, step), 6 * dir + h:6 * dir + h + 1].to_broadcast([P, P])
        b = lambda dir, h: m.small[:, 1, chunk(dir, step), 6 * dir + h:6 * dir + h + 1].to_broadcast([P, P])
        each(lambda ps, gi, dir, h, u: pe.matmul(ps[:, cols(u)], g(dir, h), (K.upto, K.since)[dir], start=True, stop=True))
        each(lambda ps, gi, dir, h, u: pe.matmul(ps[:, cols(u)], m.gkT[:, h, tk(dir)], m.gkT[:, h, tk(dir)], start=True, stop=True))
        each(lambda ps, gi, dir, h, u: pe.matmul(ps[:, cols(u)], b(dir, h), K.ident, start=True, stop=True))
        each(lambda ps, gi, dir, h, u: pe.matmul(ps[:, cols(u)], m.gkT[:, h, tk(dir)], m.gqT[:, h, tk(dir)], start=True, stop=True))
        for level in range(LEVELS):
            for gi in range(4):
                n = E.take()
                E.wait_bank(n)
                pe.wait_ge(K.level_masked, (step * LEVELS + level) * 4 + gi + 1)
                for u in range(3):
                    if level == 0:
                        mm = pe.transpose(E.bank(n)[:, cols(u)], m.X[:, gi, u, :], K.ident)
                    else:
                        mm = pe.matmul(E.bank(n)[:, cols(u)], m.X[:, gi, u, :], m.Ti[:, gi, u, :], start=True, stop=True)
                E.filled(mm, n)
            if level == 0:
                E.wait_evacuated(E.n - 4, E.n)
                continue
            for gi in range(4):
                E.wait_evacuated(E.n - 4 - gi * (1 if level == LEVELS - 1 else 2) + gi, E.n - 3 - gi * (1 if level == LEVELS - 1 else 2) + gi)
                for turned in ((True,) if level == LEVELS - 1 else (True, False)):
                    n = E.take()
                    E.wait_bank(n)
                    for u in range(3):
                        if turned:
                            mm = pe.matmul(E.bank(n)[:, cols(u)], m.X[:, gi, u, :], m.TiT[:, gi, u, :], start=True, stop=True)
                        else:
                            mm = pe.matmul(E.bank(n)[:, cols(u)], m.TiT[:, gi, u, :], m.X[:, gi, u, :], start=True, stop=True)
                    E.filled(mm, n)
            E.wait_evacuated(E.n - (4 if level == LEVELS - 1 else 8), E.n)
        pe.wait_ge(K.gd_operands, step + 1)
        each(lambda ps, gi, dir, h, u: pe.matmul(ps[0:HD, cols(u)], m.kbe[:, gi, u, :], m.TiT[:, gi, u, :], start=True, stop=True))
        E.wait_evacuated(E.n - 4, E.n)

        def new_values(ps, gi, dir, h, u):
            mm = pe.matmul(ps[:, HD * u:HD * u + HD], m.TiT[:, gi, u, :], m.vb[:, gi, u, :], start=True, stop=(step == 0))
            if step:
                mm = pe.matmul(ps[:, HD * u:HD * u + HD], m.nw_T[:, gi, u, :], m.state[:, 6 * dir + h, :], start=False, stop=True)
            return mm
        each(new_values)
        E.wait_evacuated(E.n - 4, E.n)

        def outputs(ps, gi, dir, h, u):
            mm = pe.matmul(ps[:, HD * u:HD * u + HD], m.at[:, gi, u, :], m.vn[:, gi, u, :], start=True, stop=(step == 0))
            if step:
                mm = pe.matmul(ps[:, HD * u:HD * u + HD], m.qd[:, gi, u, :], m.state[:, 6 * dir + h, :], start=False, stop=True)
            return mm
        each(outputs)
        if step < T - 1:
            each(lambda ps, gi, dir, h, u: pe.matmul(ps[0:HD, HD * u:HD * u + HD], m.ks[:, gi, u, :], m.vn[:, gi, u, :], start=True, stop=True))
            E.wait_evacuated(E.n - 8, E.n)


def act_gdn(E):
    K, m, s = E.K, E.K.second, E.eng
    n0 = E.n
    copy_out(E, linear_out(m.hz, [C2_ZE]))
    E.wait_evacuated(n0, E.n)
    for c in range(GCT):
        copy_out(E, [(m.cin[:, c, 2:S + 2], lambda b: b, "act")])
    s.wait_ge(K.conv_sums, 1)
    s.activation(m.cin[:, :, 0:S], m.cout, ACT.Exp, scale=-1.0).then_inc(K.gd_act, 1)
    sm = lambda i: m.small[:, i]
    s.wait_ge(K.gd_dve, 1)
    s.activation(sm(2), sm(2), ACT.Exp, scale=-1.0)
    s.activation(sm(1), m.hz[:, :, C2_B:C2_A], ACT.Exp, scale=-1.0)
    s.activation(m.par[:, 16:28], m.par[:, 16:28], ACT.Exp).then_inc(K.gd_act, 1)
    s.wait_ge(K.gd_dve, 2)
    s.activation(sm(4), sm(3), ACT.Ln).then_inc(K.gd_act, 1)
    copy_out(E, [(m.tm[:, :, P * c:P * c + P], lambda b: b.rearrange("p (t c) -> p t c", t=T), turn(c)) for c in range(GCT)])
    E.n += 1
    s.wait_ge(K.gd_dve, 3)
    s.activation(sm(6), sm(5), ACT.Exp)
    s.activation(sm(8), sm(7), ACT.Exp)
    s.activation(sm(10), sm(9), ACT.Exp).then_inc(K.gd_act, 1)
    E.phase()
    copy_out(E, head_tasks(m.tm[:, :, 0:384], GDH, m.gqT)[1])
    copy_out(E, head_tasks(m.tm[:, :, 384:768], GDH, m.gkT)[1])
    for step in range(T):
        for gi in range(4):
            n = E.take()
            s.wait_ge(K.gd_exponents, 4 * step + gi + 1)
            s.activation(m.qd[:, gi].rearrange("p u l -> p (u l)"), E.bank(n)[0:HD, 0:3 * P], ACT.Exp)
            E.evacuated(s.activation(m.E[:, gi], m.E[:, gi], ACT.Exp), n)
        E.n += 12
        for level in range(LEVELS):
            if level == 0:
                E.n += 4
                continue
            for gi in range(4):
                n = E.take()
                E.wait_filled(n)
                E.evacuated(s.activation(m.X[:, gi].rearrange("p u l -> p (u l)"), E.bank(n)[:, 0:3 * P], ACT.Copy), n)
            E.n += 4 if level == LEVELS - 1 else 8
        for gi in range(4):
            n = E.take()
            E.wait_filled(n)
            E.evacuated(s.activation(m.nw_T[:, gi].rearrange("p u l -> p (u l)"), E.bank(n)[0:HD, 0:3 * P], ACT.Copy, scale=-1.0), n)
        E.n += 8 if step == T - 1 else 12
    E.wait_evacuated(E.n - 4, E.n)
    s.activation(m.ez, m.hz[:, :, 0:384], ACT.Exp, scale=-1.0).then_inc(K.z_exp, 1)


def dve_gdn(E):
    K, m, v = E.K, E.K.second, E.eng
    L = E.link
    n0 = E.n
    copy_out(E, linear_out(m.hz, [C2_ZE]))
    E.wait_evacuated(n0, E.n)
    v.wait_ge(K.gd_loaded, 16 * K.GD_DMAS)
    v.memset(m.cin[:, :, 0:2], 0.0)
    L(v.memset(m.cin[:, :, S + 2:S + 4], 0.0))
    n0 = E.n
    E.n += GCT
    sm = lambda i: m.small[:, i]
    al = m.hz[:, :, C2_A:C2_ZE]
    for t in range(T):
        ins = v.tensor_tensor(sm(11)[:, t], al[:, t], m.par[:, 28:40], ALU.add)
    L(ins)
    v.scalar_tensor_tensor(sm(2), sm(11), -1.0, sm(11), ALU.mult, ALU.max).then_inc(K.gd_dve, 1)
    for c in range(GCT):
        E.wait_evacuated(n0 + c, n0 + c + 1)
        L(v.tensor_scalar(m.cout[:, c, :], m.cin[:, c, 0:S], m.cw[:, c, 0:1], None, ALU.mult))
        for k in range(1, 5):
            L(v.scalar_tensor_tensor(m.cout[:, c, :], m.cin[:, c, k:S + k], m.cw[:, c, k:k + 1], m.cout[:, c, :], ALU.mult, ALU.add))
    v.nop().then_inc(K.conv_sums, 1)
    v.wait_ge(K.gd_act, 1)
    x = m.cin[:, :, 0:S]
    L(v.tensor_scalar(x, x, 1.0, None, ALU.add))
    L(v.reciprocal(x, x))
    L(v.tensor_tensor(m.cout, m.cout, x, ALU.mult))
    v.nop().then_inc(K.conv_done, 1)
    v.wait_ge(K.gd_act, 2)
    L(v.tensor_scalar(sm(1), sm(1), 1.0, None, ALU.add))
    L(v.reciprocal(sm(1), sm(1)))
    v.tensor_scalar(sm(3), sm(2), 1.0, None, ALU.add).then_inc(K.gd_dve, 1)
    v.wait_ge(K.gd_dve, 2)
    v.wait_ge(K.gd_act, 3)
    dve_log1p_end(E, sm(4), sm(4), sm(3), sm(2), sm(2))
    L(v.scalar_tensor_tensor(sm(4), sm(11), 0.0, sm(4), ALU.max, ALU.add))
    for t in range(T):
        ins = v.scalar_tensor_tensor(sm(0)[:, t], sm(4)[:, t], -1.0, m.par[:, 16:28], ALU.mult, ALU.mult)
    L(ins)
    v.nop().then_inc(K.gd_gates, 1)
    n1 = E.n
    copy_out(E, [(m.tm[:, :, P * c:P * c + P], lambda b: b.rearrange("p (t c) -> p t c", t=T), turn(c)) for c in range(GCT)])
    n = E.take()
    E.wait_filled(n)
    v.tensor_copy(sm(9), E.bank(n)[:, 48:96].rearrange("p (t c) -> p t c", t=T))
    E.evacuated(v.tensor_copy(sm(5), E.bank(n)[:, 0:48].rearrange("p (t c) -> p t c", t=T)), n)
    E.wait_evacuated(n, n + 1)
    L(v.tensor_tensor(sm(7), sm(9), sm(5), ALU.subtract))
    v.nop().then_inc(K.gd_dve, 1)
    E.wait_evacuated(n1, E.n)
    L(v.tensor_tensor(m.gtmp[:, :, 0:768], m.tm[:, :, 0:768], m.tm[:, :, 0:768], ALU.mult))
    for i in range(12):
        ins = v.reduce_sum(m.gates[:, i, :], m.gtmp[:, :, HD * i:HD * i + HD], AX)
    L(ins)
    L(v.tensor_scalar(m.gates[:, 12:24, :], m.gates[:, 0:12, :], EPS, None, ALU.add))
    dve_rsqrt(E, m.gates[:, 0:12, :], m.gates[:, 12:24, :], m.gates[:, 24:36, :])
    L(v.tensor_scalar(m.gates[:, 0:6, :], m.gates[:, 0:6, :], HD ** -0.5, None, ALU.mult))
    c = m.gates[:, 0:12, :].rearrange("p h t -> p t h")
    for t in range(T):
        x4 = m.tm[:, t, 0:768].rearrange("p (h d) -> p h d", h=12)
        ins = v.tensor_tensor(x4, x4, c[:, t].unsqueeze(2).to_broadcast([P, 12, HD]), ALU.mult)
    L(ins)
    v.wait_ge(K.gd_act, 4)
    L(v.tensor_tensor(sm(12), sm(1), sm(6), ALU.mult))
    E.phase()
    v.nop().then_inc(K.gd_normed, 1)
    L(v.memset(m.o, 0.0))
    copy_out(E, head_tasks(m.tm[:, :, 0:384], GDH, m.gqT)[1])
    copy_out(E, head_tasks(m.tm[:, :, 384:768], GDH, m.gkT)[1])
    E.wait_evacuated(E.n - 12, E.n)
    incl = (K.upto, K.since)
    bc3 = lambda ap: ap.unsqueeze(1).to_broadcast([P, 3, P])
    v3 = lambda b: b[:, 0:3 * P].rearrange("p (u l) -> p u l", u=3)
    for step in range(T):
        rows = E.n
        for gi, (dir, half) in enumerate(GROUPS):
            n = E.take()
            E.wait_filled(n)
            for u in range(3):
                col = m.small[:, 5, chunk(dir, step), 6 * dir + 3 * half + u:6 * dir + 3 * half + u + 1]
                ins = v.tensor_scalar(m.E[:, gi, u, :], E.bank(n)[:, P * u:P * u + P], col, 0.0, ALU.subtract, ALU.min)
            ins.then_inc(K.gd_exponents, 1)
        for gi, (dir, half) in enumerate(GROUPS):
            E.wait_evacuated(rows + gi, rows + gi + 1)
            c = chunk(dir, step)
            h0 = 3 * half
            wide = lambda i: m.small[:, i, c, 6 * dir + h0:6 * dir + h0 + 3].unsqueeze(2).to_broadcast([P, 3, HD])
            k3 = m.tm[:, c, 384 + HD * h0:384 + HD * h0 + 192].rearrange("p (u d) -> p u d", u=3)
            x3 = m.tm[:, c, 768 + HD * h0:768 + HD * h0 + 192].rearrange("p (u d) -> p u d", u=3)
            v.tensor_tensor(m.vb[:, gi], x3, wide(1), ALU.mult)
            v.tensor_tensor(m.kbe[:, gi], k3, wide(12), ALU.mult)
            v.tensor_tensor(m.ks[:, gi], k3, wide(8), ALU.mult)
            q3 = m.gqT[:, h0:h0 + 3, P * c:P * c + P]
            v.tensor_tensor(m.qd[:, gi], m.qd[:, gi], q3, ALU.mult)
            ins = v.tensor_tensor(m.E[:, gi], m.E[:, gi], bc3(incl[dir]), ALU.mult)
        L(ins)
        v.nop().then_inc(K.gd_operands, 1)
        n0 = E.n
        for gi in range(4):
            n = E.take()
            E.wait_filled(n)
            E.evacuated(v.tensor_tensor(m.AT[:, gi], v3(E.bank(n)), m.E[:, gi], ALU.mult), n)
        E.wait_evacuated(n0, E.n)
        n0 = E.n
        for gi in range(4):
            n = E.take()
            E.wait_filled(n)
            E.evacuated(v.tensor_tensor(m.AT[:, gi], v3(E.bank(n)), m.AT[:, gi], ALU.mult), n)
        E.wait_evacuated(n0, E.n)
        for gi in range(4):
            n = E.take()
            E.wait_filled(n)
            E.evacuated(v.tensor_tensor(m.at[:, gi], v3(E.bank(n)), m.E[:, gi], ALU.mult), n)
        for level in range(LEVELS):
            for gi, (dir, half) in enumerate(GROUPS):
                v.tensor_tensor(m.X[:, gi], m.AT[:, gi], bc3(m.levels[:, dir, level, :]), ALU.mult).then_inc(K.level_masked, 1)
            if level == 0:
                v.wait_ge(K.level_masked, (step * LEVELS + level) * 4 + 4)
                for gi in range(4):
                    ins = v.scalar_tensor_tensor(m.TiT[:, gi], m.X[:, gi], -1.0, bc3(K.ident), ALU.mult, ALU.add)
                L(ins)
                for gi in range(4):
                    n = E.take()
                    E.wait_filled(n)
                    E.evacuated(v.scalar_tensor_tensor(m.Ti[:, gi], v3(E.bank(n)), -1.0, bc3(K.ident), ALU.mult, ALU.add), n)
                E.wait_evacuated(E.n - 4, E.n)
                continue
            E.n += 4
            last = level == LEVELS - 1
            n0 = E.n
            for gi in range(4):
                n = E.take()
                if not last:
                    E.wait_filled(n + 1)
                else:
                    E.wait_filled(n)
                E.evacuated(v.tensor_tensor(m.TiT[:, gi], m.TiT[:, gi], v3(E.bank(n)), ALU.subtract), n)
                if not last:
                    n = E.take()
                    E.evacuated(v.tensor_tensor(m.Ti[:, gi], m.Ti[:, gi], v3(E.bank(n)), ALU.subtract), n)
            E.wait_evacuated(n0, E.n)
        E.n += 4
        w3 = lambda b: b[:, 0:3 * HD].rearrange("p (u d) -> p u d", u=3)
        for gi in range(4):
            n = E.take()
            E.wait_filled(n)
            E.evacuated(v.tensor_copy(m.vn[:, gi], w3(E.bank(n))), n)
        for gi, (dir, half) in enumerate(GROUPS):
            n = E.take()
            E.wait_filled(n)
            o3 = m.o[:, chunk(dir, step), 192 * half:192 * half + 192].rearrange("p (u d) -> p u d", u=3)
            E.evacuated(v.tensor_tensor(o3, o3, w3(E.bank(n)), ALU.add), n)
        E.wait_evacuated(E.n - 4, E.n)
        if step < T - 1:
            for gi, (dir, half) in enumerate(GROUPS):
                n = E.take()
                E.wait_filled(n)
                for u in range(3):
                    h = 6 * dir + 3 * half + u
                    src, st = E.bank(n)[0:HD, HD * u:HD * u + HD], m.state[:, h, :]
                    if step == 0:
                        ins = v.tensor_copy(st, src)
                    else:
                        ins = v.scalar_tensor_tensor(st, st, m.small[0:HD, 10, chunk(dir, step), h:h + 1], src, ALU.mult, ALU.add)
                E.evacuated(ins, n)
            E.wait_evacuated(E.n - 4, E.n)
    dve_head_norm(E, m.o, m.osq, m.gates, GDH)
    v.wait_ge(K.nw_loaded, 32)
    for t in range(T):
        ins = v.tensor_tensor(m.o[:, t], m.o[:, t], m.nw, ALU.mult)
    L(ins)
    v.wait_ge(K.z_exp, 1)
    z, ez = m.hz[:, :, 0:384], m.ez
    L(v.tensor_scalar(ez, ez, 1.0, None, ALU.add))
    L(v.reciprocal(ez, ez))
    L(v.tensor_tensor(ez, ez, z, ALU.mult))
    L(v.tensor_tensor(m.mix[:, :, 640:1024], m.o, ez, ALU.mult))


def dve_norm_to_xt(E, hn, x, gain, st, tiles, tmp, norm):
    dve_rms_norm(E, hn, x, gain, st, tiles, tmp)
    E.eng.drain().then_inc(E.K.norm_done, 1)


def pe_second(E):
    K, m, pe = E.K, E.K.second, E.eng
    pe.wait_ge(K.norm_done, 5)
    n0 = E.n
    pe_transposes(E, xt_tasks(m.mix))
    E.wait_evacuated(n0, E.n)
    pe_linear(E, K.xT, NEAR_WIDTHS)
    E.phase()
    n0 = E.n
    pe_transposes(E, second_head_tasks(m)[0])
    E.wait_evacuated(n0, E.n)
    pe_attention(E, K.near)
    E.phase()
    pe_linear(E, K.xT, ML_WIDTHS)
    E.phase()
    pe_mlstm(E)
    E.phase()
    pe_gdn(E)
    E.phase()
    n0 = E.n
    pe_transposes(E, xt_tasks(m.mix))
    E.wait_evacuated(n0, E.n)
    pe_linear(E, K.xT, [512] * 2)
    E.phase()


def act_second(E):
    K, m = E.K, E.K.second
    copy_out(E, xt_out(K.xT))
    copy_out(E, linear_out(m.h, NEAR_WIDTHS))
    E.wait_evacuated(E.n - 8, E.n)
    E.phase()
    copy_out(E, second_head_tasks(m)[1])
    act_attention(E, K.near)
    E.phase()
    copy_out(E, linear_out(m.hm, ML_WIDTHS))
    E.wait_evacuated(E.n - 8, E.n)
    E.phase()
    act_mlstm(E)
    E.phase()
    act_gdn(E)
    E.phase()
    copy_out(E, xt_out(K.xT))
    residual_out(E, K.x, 2, 1.0)
    E.phase()


def dve_second(E):
    K, m, v = E.K, E.K.second, E.eng
    v.wait_ge(K.gains_loaded, 16 * 9)
    dve_rms_norm(E, m.mix, K.x, K.gains[:, 0, :], m.st.rearrange("p a b c -> p (a b c)")[:, 0:16].rearrange("p (t c) -> p t c", t=T),
                 T, m.h.rearrange("p t c -> p (t c)")[:, 0:D])
    v.drain().then_inc(K.norm_done, 1)
    copy_out(E, xt_out(K.xT))
    v.wait_ge(K.bias_loaded, 16 * (2 * NAH + 1))
    E.link(v.tensor_scalar(m.far, m.near, -NEG, NEG, ALU.mult, ALU.add))
    b = m.bias.rearrange("p h r c -> p (h r) c")
    wide = lambda ap: ap.unsqueeze(1).to_broadcast([P, NAH * 14, HD])
    E.link(v.tensor_tensor(b, b, wide(m.near), ALU.mult))
    E.link(v.tensor_tensor(b, b, wide(m.far), ALU.add))
    copy_out(E, linear_out(m.h, NEAR_WIDTHS))
    E.wait_evacuated(E.n - 8, E.n)
    E.phase()
    copy_out(E, second_head_tasks(m)[1])
    dve_attention(E, K.near)
    E.phase()
    copy_out(E, linear_out(m.hm, ML_WIDTHS))
    E.wait_evacuated(E.n - 8, E.n)
    E.phase()
    dve_mlstm(E)
    E.phase()
    dve_gdn(E)
    E.phase()
    copy_out(E, xt_out(K.xT))
    residual_out(E, K.x, 2, 1.0)
    E.wait_evacuated(E.n - 8, E.n)
    E.phase()


def pool_second(E):
    K, m, g, d = E.K, E.K.second, E.eng, E.K.d
    load_gains(E, d.norm_mix_w_2)
    g.dma_start(m.near, d.c_near).then_inc(K.bias_loaded, 16)
    for lo, src in ((0, d.ml_i_bias_2), (8, d.ml_f_bias_2), (16, d.gdn_a_log_2), (28, d.gdn_dt_bias_2)):
        n = src.shape[1] * src.shape[2]
        g.dma_start(m.par[:, lo:lo + n], src.rearrange("a b h -> a (b h)").to_broadcast([P, n])).then_inc(K.par_loaded, 16)
    rows, pad = NAH * 15, 2 * HD - 1
    stage = m.s.rearrange("p a t c -> p (a t c)")[0:rows, 0:pad]
    g.memset(stage, 0.0).then_inc(K.stage_zero, 1)
    g.wait_ge(K.stage_zero, 1)
    g.dma_start(stage[:, HD - 16:HD + 15], d.na_rel_bias_2.rearrange("a h r c -> (a h r) c")).then_inc(K.stage_filled, 16)
    g.wait_ge(K.stage_filled, 16)
    g.dma_start(K.bias_dram, stage.unsqueeze(1).to_broadcast([rows, HD, pad])).then_inc(K.stage_stored, 16)
    g.wait_ge(K.stage_stored, 16)
    for h in range(NAH):
        for a in range(2):
            src = bass.AP(tensor=K.bias_dram.tensor, offset=(15 * h + 1 - a) * HD * pad + HD - 1,
                          ap=[[pad - 1, HD], [HD * pad, 14], [1, HD]])
            g.dma_start(m.bias[HD * a:HD * a + HD, h], src).then_inc(K.bias_loaded, 16)
    g.wait_ge(K.par_loaded, 16 * 4)
    E.phase()
    E.phase()
    E.phase()
    g.dma_start(m.nw[:, 0:MLH * HD], d.ml_norm_w_2.to_broadcast([P, MLH * HD])).then_inc(K.nw_loaded, 16)
    E.phase()
    g.dma_start(m.nw, d.gdn_norm_w_2.to_broadcast([P, GDH * HD])).then_inc(K.nw_loaded, 16)
    for dir in range(2):
        g.dma_start(m.levels[:, dir], (d.c_levels_up, d.c_levels_down)[dir]).then_inc(K.gd_loaded, 16)
    for c in range(GCT):
        g.dma_start(m.cw[:, c, :], d.gdn_conv_w_2[0, :, P * c:P * c + P].rearrange("k p -> p k"),
                    allow_slow_non_contiguous=True).then_inc(K.gd_loaded, 16)
    E.phase()
    E.phase()
    E.phase()


def pe_feature_major(E, xT, tokens, tiles):
    for _ in range(tiles):
        w = pe_weights(E).rearrange("p (k n) -> p k n", k=KD)
        for c in range(WT // P):
            n = E.take()
            E.wait_bank(n)
            for k in range(KD):
                mm = E.eng.matmul(E.bank(n)[:, 0:tokens], w[:, k, P * c:P * c + P], xT[:, k, :], start=(k == 0), stop=(k == KD - 1))
            E.filled(mm, n)
        E.eng.drain().then_inc(E.K.w_used, 1)


def cross_copies(m):
    kT = [(m.kT[:, c, :], lambda b: b[:, 0:MEMN], turn(c)) for c in range(KD)]
    v = [(m.v[:, t, WT * h:WT * h + WT], lambda b: b, turn(t)) for h in range(2) for t in range(2)]
    qT = [(m.qT[:, c, :], lambda b: b, turn(c)) for c in range(KD)]
    return kT, v, qT


def mem_tasks(m):
    return [[m.mem[:, t, P * k:P * k + P] for t in range(2)] for k in range(KD)]


def mem_out(m):
    return [(m.memT[:, k, :], lambda b: b[:, 0:MEMN], turn(k)) for k in range(KD)]


def pe_cross(E):
    K, m, pe = E.K, E.K.cross, E.eng
    pe.wait_ge(K.norm_done, 6)
    n0 = E.n
    pe_transposes(E, mem_tasks(m))
    E.wait_evacuated(n0, E.n)
    pe_feature_major(E, m.memT, MEMN, 2)
    pe_linear(E, m.memT, [512] * 2, tiles=2)
    pe.wait_ge(K.norm_done, 7)
    n0 = E.n
    pe_transposes(E, xt_tasks(m.hn))
    E.wait_evacuated(n0, E.n)
    pe_feature_major(E, K.xT, S, 2)
    E.wait_evacuated(E.n - 8, E.n)
    pe_attention(E, K.memory)
    E.phase()
    n0 = E.n
    pe_transposes(E, xt_tasks(m.mix))
    E.wait_evacuated(n0, E.n)
    pe_linear(E, K.xT, [512] * 2)
    E.phase()


def act_cross(E):
    K, m = E.K, E.K.cross
    kT, v, qT = cross_copies(m)
    copy_out(E, mem_out(m))
    copy_out(E, kT)
    copy_out(E, v)
    copy_out(E, xt_out(K.xT))
    copy_out(E, qT)
    act_attention(E, K.memory)
    E.phase()
    copy_out(E, xt_out(K.xT))
    residual_out(E, K.x, 2, 1.0)
    E.phase()


def dve_cross(E):
    K, m, v = E.K, E.K.cross, E.eng
    kT, vv, qT = cross_copies(m)
    v.wait_ge(K.mem_loaded, 32)
    dve_rms_norm(E, m.mem, m.mem, m.gain, m.nst, 2, m.tmp)
    v.drain().then_inc(K.norm_done, 1)
    v.wait_ge(K.gains_loaded, 16 * 10)
    dve_rms_norm(E, m.hn, K.x, K.gains[:, 1, :], m.nst, T, m.tmp)
    v.drain().then_inc(K.norm_done, 1)
    copy_out(E, mem_out(m))
    copy_out(E, kT)
    copy_out(E, vv)
    copy_out(E, xt_out(K.xT))
    copy_out(E, qT)
    E.wait_evacuated(E.n - 8, E.n)
    dve_attention(E, K.memory)
    E.phase()
    copy_out(E, xt_out(K.xT))
    residual_out(E, K.x, 2, 1.0)
    E.wait_evacuated(E.n - 8, E.n)
    E.phase()


def pool_cross(E):
    K, m, g, d = E.K, E.K.cross, E.eng, E.K.d
    g.dma_start(m.mem, d.mem_2[0].rearrange("(t p) d -> p t d", p=P)).then_inc(K.mem_loaded, 16)
    g.dma_start(m.gain, d.norm_mem_w_2.to_broadcast([P, D])).then_inc(K.mem_loaded, 16)
    g.dma_start(K.gains[:, 1, :], d.norm_xa_w_2.to_broadcast([P, D])).then_inc(K.gains_loaded, 16)
    E.phase()
    E.phase()


def pe_ffn(E):
    K, m, pe = E.K, E.K.ffn, E.eng
    pe.wait_ge(K.norm_done, 8)
    n0 = E.n
    pe_transposes(E, xt_tasks(m.hn))
    E.wait_evacuated(n0, E.n)
    pe_feature_major(E, K.xT, S, FF // WT)
    E.wait_evacuated(E.n - 8, E.n)
    n0 = E.n
    for i in range(8):
        E.wait_bank(E.take())
    for f in range(FF // WT):
        w = pe_weights(E).rearrange("p (k n) -> p k n", k=WT // P)
        for t in range(T):
            for half in range(2):
                for k in range(WT // P):
                    mm = pe.matmul(E.bank(n0 + 4 * half + t), m.hT[:, 4 * f + k, P * t:P * t + P], w[:, k, WT * half:WT * half + WT],
                                   start=(f == 0 and k == 0), stop=(f == FF // WT - 1 and k == WT // P - 1))
                if f == FF // WT - 1:
                    E.filled(mm, n0 + 4 * half + t)
        pe.drain().then_inc(K.w_used, 1)
    E.phase()


def act_ffn(E):
    K, m, s = E.K, E.K.ffn, E.eng
    copy_out(E, xt_out(K.xT))
    for f in range(FFT):
        n = E.take()
        if f % 2 == 0:
            E.wait_filled(n)
            E.link(s.activation(m.r[:, 0, :], E.bank(n), ACT.Relu))
            E.evacuated(s.activation(m.hT[:, f, :], m.r[:, 0, :], ACT.Square), n)
            E.wait_evacuated(n, n + 1)
    residual_out(E, K.x, 2, 1.0)
    E.phase()


def dve_ffn(E):
    K, m, v = E.K, E.K.ffn, E.eng
    v.wait_ge(K.gains_loaded, 16 * 12)
    dve_rms_norm(E, m.hn, K.x, K.gains[:, 0, :], m.nst, T, m.tmp)
    v.drain().then_inc(K.norm_done, 1)
    copy_out(E, xt_out(K.xT))
    for f in range(FFT):
        n = E.take()
        if f % 2 == 1:
            E.wait_filled(n)
            E.link(v.tensor_scalar(m.r[:, 1, :], E.bank(n), 0.0, None, ALU.max))
            E.evacuated(v.tensor_tensor(m.hT[:, f, :], m.r[:, 1, :], m.r[:, 1, :], ALU.mult), n)
            E.wait_evacuated(n, n + 1)
    n0 = E.n
    residual_out(E, K.x, 2, 1.0)
    E.wait_evacuated(n0, E.n)
    E.phase()
    dve_rms_norm(E, m.hn, K.x, K.gains[:, 1, :], m.nst, T, m.tmp)
    v.drain().then_inc(K.norm_done, 1)


def pool_ffn(E):
    K, m, g, d = E.K, E.K.ffn, E.eng, E.K.d
    load_gains(E, d.norm_ffn_w_2, d.norm_out_w_2.rearrange("(a n) -> a n", a=1))
    E.phase()
    g.wait_ge(K.norm_done, 9)
    g.dma_start(K.out[0].rearrange("(t p) d -> p t d", p=P), m.hn).then_inc(K.out_stored, 16)
    g.wait_ge(K.out_stored, 16)



def sp_weights(E):
    K, sp, d = E.K, E.eng, E.K.d

    def load(src, rows, w=None, gen=None):
        w = E.w
        E.w += 1
        if w >= RING:
            sp.wait_ge(K.w_used, w - RING + 1)
        cols = src.shape[1]
        wide = WT if rows == KD else D
        dst = K.ring[:, w % RING, :].rearrange("p (k n) -> p k n", n=wide)[:, :, 0:cols]
        sp.dma_start(dst, src.rearrange("(k p) n -> p k n", p=P)).then_inc(K.w_loaded[w % RING], 16)

    def load_wide(mat, lo, hi):
        for c in range(lo, hi, WT):
            load(mat[:, c:min(c + WT, hi)], KD)

    def experts(layer, count, expert):
        w0 = E.w
        with sp.Fori(0, count) as j:
            e = expert(j)
            mats = [K.gate_rows[layer], K.up_rows[layer], K.down_rows[layer]]
            for i, mat in enumerate(mats):
                w = w0 + i
                sp.wait_ge(K.w_used, j * 3 + (w - RING + 1))
                rows = D if i < 2 else EH
                src = mat[bass.ds(e * rows, rows), :]
                dst = K.ring[:, w % RING, :].rearrange("p (k n) -> p k n", k=rows // P)
                sp.dma_start(dst, src.rearrange("(k p) n -> p k n", p=P)).then_inc(K.w_loaded[w % RING], 16)
        E.w = w0 + 3 * count

    load_wide(d.w_in_even[0], 0, IN_EVEN)
    load_wide(d.w_out_even[0], 0, D)
    for layer in range(2):
        if layer == 1:
            load_wide(d.w_out_fourier[0], 0, D)
        experts(layer, NE, lambda j: j)
        sp.wait_ge(K.slots_ready, layer + 1)
        jt = K.moe.jt.bitcast(I32)
        experts(layer, NOV, lambda j: sp.value_load(jt[0:1, bass.ds(j, 1)], min_val=0, max_val=NE - 1))
    w = d.w_in_2[0]
    load_wide(w, 0, W2_ML)
    load_wide(w, W2_ML, W2_GD)
    load(w[:, W2_Z:], KD)
    load_wide(w, W2_GD, W2_Z)
    load_wide(d.w_out_2[0], 0, D)
    load_wide(d.w_xkv_2[0], 0, 2 * D)
    load_wide(d.w_xq_2[0], 0, D)
    load_wide(d.w_xo_2[0], 0, D)
    load_wide(d.w_ff1_2[0], 0, FF)
    for f in range(FF // WT):
        load(d.w_ff2_2[0][WT * f:WT * f + WT, :], WT // P)


def bass_two_block_kernel(nc, args, out):
    d = Names()
    (d.x, d.w_in_even, d.ret_decay_logit, d.ret_gn_gain, d.sink_logit, d.w_out_even, d.w_out_fourier, d.ln1_gain,
     d.ln1_bias, d.ln2_gain, d.ln2_bias, d.router_coarse_w, d.router_coarse_b, d.router_fine_w, d.router_fine_b,
     d.expert_w_gate, d.expert_w_up, d.expert_w_down, d.mem_2, d.norm_mix_w_2, d.w_in_2, d.na_rel_bias_2,
     d.ml_i_bias_2, d.ml_f_bias_2, d.ml_norm_w_2, d.gdn_conv_w_2, d.gdn_a_log_2, d.gdn_dt_bias_2, d.gdn_norm_w_2,
     d.w_out_2, d.norm_xa_w_2, d.norm_mem_w_2, d.w_xq_2, d.w_xkv_2, d.w_xo_2, d.norm_ffn_w_2, d.w_ff1_2, d.w_ff2_2,
     d.norm_out_w_2, d.c_ident, d.c_ones, d.c_before, d.c_upto, d.c_since, d.c_cos128, d.c_sin128, d.c_cos64,
     d.c_sin64, d.c_dpos, d.c_dneg, d.c_mask, d.c_feat, d.c_cs, d.c_sn, d.c_iota, d.c_iotag, d.c_iotaj, d.c_tok,
     d.c_near, d.c_levels_up, d.c_levels_down) = args
    K = Names()
    K.d, K.out, K.rope_count = d, out, 0
    K.CONSTS, K.EVEN_DMAS, K.MOE_DMAS, K.GD_DMAS = 5, 9, 8, 2 + GCT
    K.phases = dict(pe=0, act=0, dve=0, pool=0)
    with ExitStack() as ctx:
        ring = ctx.enter_context(nc.sbuf_tensor("ring", [P, RING, KD * WT], F32))
        K.ring = ring[:, :, :]
        K.x = ctx.enter_context(nc.sbuf_tensor("x", [P, T, D], F32))[:, :, :]
        K.xT = ctx.enter_context(nc.sbuf_tensor("xT", [P, KD, S], F32))[:, :, :]
        K.gains = ctx.enter_context(nc.sbuf_tensor("gains", [P, 2, D], F32))[:, :, :]
        K.ident, K.ones, K.before, K.upto, K.since = (
            ctx.enter_context(nc.sbuf_tensor(name, [P, P], F32))[:, :] for name in ("ident", "ones", "before", "upto", "since"))
        K.lnst = ctx.enter_context(nc.sbuf_tensor("lnst", [P, T, 16], F32))[:, :, :]
        words = ARENA
        arena = ctx.enter_context(nc.sbuf_tensor("arena", [P, words], F32))
        K.ps = ctx.enter_context(nc.psum_tensor("products", [P, 8, WT], F32))[:, :, :]
        K.slot_dram = nc.dram_tensor("slot_tokens", ((JOBS + 1) * P, 1), I32).ap()
        K.xg_dram = nc.dram_tensor("token_rows", (S, D), F32).ap()
        K.ys_dram = nc.dram_tensor("expert_rows", (JOBS * P, D), F32).ap()
        K.bias_dram = nc.dram_tensor("bias_rows", (NAH * 15, HD, 2 * HD - 1), F32).ap()
        K.gate_rows = [d.expert_w_gate[l].rearrange("e k n -> (e k) n") for l in range(2)]
        K.up_rows = [d.expert_w_up[l].rearrange("e k n -> (e k) n") for l in range(2)]
        K.down_rows = [d.expert_w_down[l].rearrange("e k n -> (e k) n") for l in range(2)]

        def carve(at):
            def take(*shape):
                size = int(np.prod(shape))
                ap = arena[:, c.at:c.at + size]
                c.at += size
                assert c.at <= words, (c.at, words)
                names = "abcd"[:len(shape)]
                if len(shape) > 1:
                    ap = ap.rearrange(f"p ({' '.join(names)}) -> p {' '.join(names)}", **dict(zip(names[1:], shape[1:])))
                return ap
            c = take
            c.at = at
            return take
        K.carve = carve
        K.even, K.fourier, K.moe = even_views(K), fourier_views(K), moe_views(K)
        K.second, K.cross, K.ffn = second_views(K), cross_views(K), ffn_views(K)
        K.window, K.near, K.memory = even_attention(K), near_attention(K), cross_attention(K)
        K.probs_base = dict(window=0, near=WQ, memory=WQ + NAH)

        sem = lambda name: ctx.enter_context(nc.semaphore(name))
        K.bank_filled = [sem(f"bank_filled_{i}") for i in range(8)]
        K.bank_evacuated = [sem(f"bank_evacuated_{i}") for i in range(8)]
        K.w_loaded = [sem(f"w_loaded_{i}") for i in range(RING)]
        K.vector_step = sem("vector_step")
        K.scalar_step = sem("scalar_step")
        K.phase_done = sem("phase_done")
        K.w_used = sem("w_used")
        K.x_loaded = sem("x_loaded")
        K.consts_loaded = sem("consts_loaded")
        K.even_loaded = sem("even_loaded")
        K.mask_loaded = sem("mask_loaded")
        K.gains_loaded = sem("gains_loaded")
        K.norm_done = sem("norm_done")
        K.rope_done = sem("rope_done")
        K.small_dve = sem("small_dve")
        K.small_act = sem("small_act")
        K.decay_exponents = sem("decay_exponents")
        K.decays_ready = sem("decays_ready")
        K.scores_ready = sem("scores_ready")
        K.probs_ready = sem("probs_ready")
        K.fourier_loaded = sem("fourier_loaded")
        K.moe_loaded = sem("moe_loaded")
        K.router_dve = sem("router_dve")
        K.router_act = sem("router_act")
        K.choices_ready = sem("choices_ready")
        K.slots_ready = sem("slots_ready")
        K.table_zero = sem("table_zero")
        K.table_cleared = sem("table_cleared")
        K.slots_stored = sem("slots_stored")
        K.rows_stored = sem("rows_stored")
        K.idx_loaded = sem("idx_loaded")
        K.idx_passed = sem("idx_passed")
        K.xs_gathered = sem("xs_gathered")
        K.y_gathered = sem("y_gathered")
        K.bias_loaded = sem("bias_loaded")
        K.par_loaded = sem("par_loaded")
        K.stage_zero = sem("stage_zero")
        K.stage_filled = sem("stage_filled")
        K.stage_stored = sem("stage_stored")
        K.nw_loaded = sem("nw_loaded")
        K.ml_gates = sem("ml_gates")
        K.ml_dve = sem("ml_dve")
        K.ml_act = sem("ml_act")
        K.ml_exponents = sem("ml_exponents")
        K.ml_exps = sem("ml_exps")
        K.ml_weights = sem("ml_weights")
        K.gd_loaded = sem("gd_loaded")
        K.conv_sums = sem("conv_sums")
        K.conv_done = sem("conv_done")
        K.gd_gates = sem("gd_gates")
        K.gd_dve = sem("gd_dve")
        K.gd_act = sem("gd_act")
        K.gd_normed = sem("gd_normed")
        K.gd_exponents = sem("gd_exponents")
        K.gd_operands = sem("gd_operands")
        K.level_masked = sem("level_masked")
        K.z_exp = sem("z_exp")
        K.mem_loaded = sem("mem_loaded")
        K.out_stored = sem("out_stored")

        n = KD + T * len(EVEN_WIDTHS) + 2 * RH
        K.ret_scores = {}
        for h in range(RH + 1):
            if h < RH:
                K.ret_scores[h] = n
                n += T
            if h >= 1:
                n += 1
        K.after_even = n + WQ + WKV + WQ * K.window.per + KD + 2 * T + KD

        block = ctx.enter_context(nc.Block())

        @block.sync
        def _(eng):
            sp_weights(Engine(K, eng, "sp", None))

        @block.tensor
        def _(eng):
            E = Engine(K, eng, "pe", None)
            pe_even(E)
            pe_moe(E, 0)
            E.phase()
            turn_x_pe(E, 2)
            pe_fourier(E)
            pe_moe(E, 1)
            E.phase()
            pe_second(E)
            pe_cross(E)
            pe_ffn(E)

        @block.scalar
        def _(eng):
            E = Engine(K, eng, "act", K.scalar_step)
            act_even(E)
            act_moe(E, 0)
            E.phase()
            copy_out(E, xt_out(K.xT))
            fourier_out(E)
            act_moe(E, 1)
            E.phase()
            act_second(E)
            act_cross(E)
            act_ffn(E)

        @block.vector
        def _(eng):
            E = Engine(K, eng, "dve", K.vector_step)
            dve_even(E)
            dve_moe(E, 0)
            E.phase()
            copy_out(E, xt_out(K.xT))
            fourier_out(E)
            dve_moe(E, 1)
            E.phase()
            dve_second(E)
            dve_cross(E)
            dve_ffn(E)

        @block.gpsimd
        def _(eng):
            E = Engine(K, eng, "pool", None)
            pool_even(E)
            pool_moe(E, 0)
            E.phase()
            E.n += KD
            pool_fourier(E)
            pool_moe(E, 1)
            E.phase()
            pool_second(E)
            pool_cross(E)
            pool_ffn(E)


ARENA = 29976

def shape_tables():
    f = np.float32
    r = np.arange(P)
    c = {}
    c["ident"] = np.eye(P, dtype=f)
    c["ones"] = np.ones((P, P), f)
    c["before"] = (r[:, None] < r[None, :]).astype(f)
    c["upto"] = (r[:, None] <= r[None, :]).astype(f)
    c["since"] = (r[:, None] >= r[None, :]).astype(f)
    for half in (64, 32):
        inv = (f(10000.0) ** (-np.arange(half, dtype=f) / f(half))).astype(f)
        ang = (np.arange(S, dtype=f)[:, None] * inv[None, :]).astype(f).astype(np.float64)
        rows = lambda a: np.ascontiguousarray(a.reshape(T, P, half).transpose(1, 0, 2)).astype(f)
        c[f"cos{2 * half}"], c[f"sin{2 * half}"] = rows(np.cos(ang)), rows(np.sin(ang))
    diff = np.arange(TOEP)[None, :] - (T - 1) * P - r[:, None]
    c["dpos"], c["dneg"] = np.maximum(diff, 0).astype(f), np.maximum(-diff, 0).astype(f)
    rel = np.arange(3 * P)[None, :] - P - r[:, None]
    c["mask"] = np.where(np.abs(rel) <= P, 0.0, NEG).astype(f)
    a = 2 * np.pi * np.outer(np.arange(256), np.arange(256)) / 256
    feat = np.concatenate([np.cos(a), np.sin(a)], 1)
    c["feat"] = feat.reshape(2, P, 512).transpose(1, 0, 2).astype(f)
    a = 2 * np.pi * np.outer(np.arange(S), np.arange(S)) / S
    norm = 1.0 / np.sqrt(S * 256.0)
    c["cs"] = (np.cos(a) * norm).reshape(T, P, S).transpose(1, 0, 2).astype(f)
    c["sn"] = (-np.sin(a) * norm).reshape(T, P, S).transpose(1, 0, 2).astype(f)
    c["iota"] = np.tile(np.arange(NE, dtype=f), (P, 1))
    c["iotag"] = np.tile((np.arange(NE) // (NE // NG)).astype(f), (P, 1))
    c["iotaj"] = np.tile(np.arange(NOV, dtype=f)[None, :, None], (P, 1, NE))
    c["tok"] = (np.arange(T, dtype=np.int32)[None, :] * P + r[:, None].astype(np.int32)).astype(np.int32)
    col = np.arange(HD)
    start = np.clip(col - 8, 0, HD - 16)
    ok = (col[None, :] >= start[:, None]) & (col[None, :] < start[:, None] + 16)
    c["near"] = np.tile(ok.astype(f), (2, 1))
    up = np.zeros((P, LEVELS, P), f)
    for l in range(LEVELS):
        b = 1 << l
        up[:, l, :] = (r[:, None] // (2 * b) == r[None, :] // (2 * b)) & (r[:, None] // b % 2 == 0) & (r[None, :] // b % 2 == 1)
    c["levels_up"] = up
    c["levels_down"] = np.ascontiguousarray(up.transpose(2, 1, 0))
    return {"c_" + k: np.ascontiguousarray(v) for k, v in c.items()}


_INS = ['x', 'w_in_even', 'ret_decay_logit', 'ret_gn_gain', 'sink_logit', 'w_out_even', 'w_out_fourier', 'ln1_gain',
        'ln1_bias', 'ln2_gain', 'ln2_bias', 'router_coarse_w', 'router_coarse_b', 'router_fine_w', 'router_fine_b',
        'expert_w_gate', 'expert_w_up', 'expert_w_down', 'mem_2', 'norm_mix_w_2', 'w_in_2', 'na_rel_bias_2',
        'ml_i_bias_2', 'ml_f_bias_2', 'ml_norm_w_2', 'gdn_conv_w_2', 'gdn_a_log_2', 'gdn_dt_bias_2', 'gdn_norm_w_2',
        'w_out_2', 'norm_xa_w_2', 'norm_mem_w_2', 'w_xq_2', 'w_xkv_2', 'w_xo_2', 'norm_ffn_w_2', 'w_ff1_2', 'w_ff2_2',
        'norm_out_w_2']


def kernel(**inputs):
    import concourse.bacc as _bacc
    from concourse.bass_utils import run_bass_kernel_spmd as _run

    nc = _bacc.Bacc("TRN2", target_bir_lowering=False, num_devices=1)
    arrays, args = {}, []
    for name, a in [(name, inputs[name]) for name in _INS] + list(shape_tables().items()):
        a = np.ascontiguousarray(a)
        arrays[f"in_{name}_dram"] = a
        args.append(nc.dram_tensor(f"in_{name}_dram", a.shape, mybir.dt.from_np(a.dtype), kind="ExternalInput").ap())
    out = nc.dram_tensor("out_0_dram", (1, S, D), F32, kind="ExternalOutput").ap()
    bass_two_block_kernel(nc, args, out)
    r = _run(nc, [arrays], core_ids=[0])
    return r.results[0]["out_0_dram"]
```

```python
from contextlib import ExitStack

import numpy as np
import concourse.bass as bass
from concourse import mybir

ALU = mybir.AluOpType
ACT = mybir.ActivationFunctionType
F32 = mybir.dt.float32
I32 = mybir.dt.int32
U32 = mybir.dt.uint32
AX = mybir.AxisListType.X

P = 128
S = 512
T = S // P
D = 1024
KD = D // P
WT = 512
ALPHA = 4.0 ** 0.25
LN_EPS = 1e-5
EPS = 1e-6
NEG = -1e30

RH = 4
WQ, WKV, WD = 8, 2, 64
IN_EVEN = 2816
OFF_QA, OFF_KA, OFF_VA, OFF_GA, OFF_QB, OFF_KB, OFF_VB = 0, 512, 1024, 1536, 2048, 2560, 2688
TOEP = 7 * P

NE = 32
NG = 4
EH = 512
SB = 64
NOV = (2 * S) // (SB + 1)
JOBS = NE + NOV

NAH, MLH, GDH = 6, 4, 6
HD = 64
C2_NAQ, C2_NAK, C2_NAV = 0, 384, 768
C2_MLQ, C2_MLK, C2_MLV, C2_MLO, C2_MLI, C2_MLF, C2_MLE = 0, 256, 512, 768, 1024, 1032, 1040
C2_Z, C2_B, C2_A, C2_ZE = 0, 384, 396, 408
W2_ML, W2_GD, W2_Z = 1152, 2192, 3344
GDC = 3 * GDH * HD
GCT = GDC // P
MEMN = 256
XH, XD = 4, 256
FF = 4096
FFT = FF // P
LEVELS = 7

RING = 3


class Names:
    pass


class Engine:

    def __init__(self, K, eng, name, step):
        self.K, self.eng, self.name, self.step = K, eng, name, step
        self.n = 0
        self.s = 0
        self.loop = None
        self.w = 0

    def gen(self, n):
        if self.loop is None or n < self.loop[3]:
            return n // 8
        return self.loop[0] * (self.loop[1] // 8) + n // 8

    def take(self):
        n, self.n = self.n, self.n + 1
        return n

    def bank(self, n):
        return self.K.ps[:, n % 8, :]

    def wait_filled(self, n):
        self.eng.wait_ge(self.K.bank_filled[n % 8], self.gen(n) + 1)

    def wait_evacuated(self, lo, hi):
        for n in range(max(lo, hi - 8), hi):
            self.eng.wait_ge(self.K.bank_evacuated[n % 8], self.gen(n) + 1)

    def wait_bank(self, n):
        if n >= 8:
            self.eng.wait_ge(self.K.bank_evacuated[n % 8], self.gen(n))

    def skip(self):
        n = self.take()
        if self.name == "pe":
            self.wait_bank(n)
            self.filled(self.eng.nop(), n)

    def filled(self, ins, n):
        ins.then_inc(self.K.bank_filled[n % 8], 1)

    def evacuated(self, ins, n):
        ins.then_inc(self.K.bank_evacuated[n % 8], 1)

    def link(self, ins):
        self.s += 1
        ins.then_inc(self.step, 1)
        if self.loop is None:
            self.eng.wait_ge(self.step, self.s)
        else:
            self.eng.wait_ge(self.step, self.loop[0] * self.loop[2] + self.s)

    def phase(self):
        self.K.phases[self.name] += 1
        self.eng.drain().then_inc(self.K.phase_done, 1)
        self.eng.wait_ge(self.K.phase_done, 4 * self.K.phases[self.name])

    def begin_loop(self, reg, products, steps, start=0):
        assert products % 8 == 0
        self.loop = (reg, products, steps, self.n)
        self.at = (self.n, self.s)

    def end_loop(self, turns):
        _, products, steps, _ = self.loop
        assert self.n - self.at[0] == products, (self.name, self.n - self.at[0], products)
        assert self.s - self.at[1] == steps, (self.name, self.s - self.at[1], steps)
        self.n = self.at[0] + products * turns
        self.s = self.at[1] + steps * turns
        self.loop = None



def pe_transposes(E, tasks):
    for blocks in tasks:
        n = E.take()
        E.wait_bank(n)
        for i, src in enumerate(blocks):
            rows, cols = src.shape
            last = E.eng.transpose(E.bank(n)[0:cols, P * i:P * i + rows], src, E.K.ident[0:rows, 0:rows])
        E.filled(last, n)


def copy_out(E, tasks):
    for dst, view, who in tasks:
        n = E.take()
        if who != E.name:
            continue
        E.wait_filled(n)
        src = view(E.bank(n))
        if E.name == "act":
            ins = E.eng.activation(dst, src, ACT.Copy)
        else:
            ins = E.eng.tensor_copy(dst, src)
        E.evacuated(ins, n)


def turn(i):
    return ("act", "dve")[i % 2]


def xt_tasks(src):
    return [[src[:, t, P * k:P * k + P] for t in range(T)] for k in range(KD)]


def xt_out(dst):
    return [(dst[:, k, :], lambda b: b, turn(k)) for k in range(KD)]


def pe_weights(E):
    K = E.K
    w, E.w = E.w, E.w + 1
    E.eng.wait_ge(K.w_loaded[w % RING], 16 * (w // RING + 1))
    return K.ring[:, w % RING, :]


def pe_linear(E, xT, widths, tiles=T):
    for i, width in enumerate(widths):
        w = pe_weights(E).rearrange("p (k n) -> p k n", k=KD)
        for t in range(tiles):
            n = E.take()
            E.wait_bank(n)
            for k in range(KD):
                mm = E.eng.matmul(E.bank(n)[:, 0:width], xT[:, k, P * t:P * t + P], w[:, k, 0:width],
                                  start=(k == 0), stop=(k == KD - 1))
                if i and t == 0 and k == 0:
                    mm.then_inc(E.K.w_used, 1)
            E.filled(mm, n)
    E.eng.drain().then_inc(E.K.w_used, 1)


def linear_out(dst, widths):
    out, at = [], 0
    for width in widths:
        for t in range(T):
            out.append((dst[:, t, at:at + width], lambda b, w=width: b[:, 0:w], turn(len(out))))
        at += width
    return out


def residual_out(E, x, halves, scale):
    for h in range(halves):
        for t in range(T):
            n = E.take()
            if E.name == "dve":
                E.wait_filled(n)
                part = x[:, t, WT * h:WT * h + WT]
                E.evacuated(E.eng.scalar_tensor_tensor(part, part, scale, E.bank(n), ALU.mult, ALU.add), n)


def dve_rsqrt(E, y, x, t):
    v = E.eng
    E.link(v.tensor_scalar(y.bitcast(I32), x.bitcast(I32), -0.5, float(0x5F3759DF), ALU.mult, ALU.add))
    for _ in range(3):
        E.link(v.tensor_tensor(t, y, y, ALU.mult))
        E.link(v.scalar_tensor_tensor(t, t, -0.5, x, ALU.mult, ALU.mult))
        E.link(v.scalar_tensor_tensor(y, t, 1.5, y, ALU.add, ALU.mult))


def dve_layer_norm(E, x, gain, bias, st):
    v = E.eng
    for t in range(T):
        for h in range(2):
            ins = v.bn_stats(st[:, t, 6 * h:6 * h + 6], x[:, t, WT * h:WT * h + WT])
    E.link(ins)
    for t in range(T):
        ins = v.bn_aggr(st[:, t, 12:14], st[:, t, 0:12])
    E.link(ins)
    E.link(v.tensor_scalar(st[:, :, 13], st[:, :, 13], LN_EPS, None, ALU.add))
    dve_rsqrt(E, st[:, :, 14], st[:, :, 13], st[:, :, 15])
    for t in range(T):
        ins = v.scalar_tensor_tensor(x[:, t, :], x[:, t, :], st[:, t, 12:13], gain, ALU.subtract, ALU.mult)
    E.link(ins)
    for t in range(T):
        ins = v.scalar_tensor_tensor(x[:, t, :], x[:, t, :], st[:, t, 14:15], bias, ALU.mult, ALU.add)
    E.link(ins)


def dve_rms_norm(E, dst, x, gain, tiles):
    v, st = E.eng, E.K.lnst
    for t in range(tiles):
        for h in range(2):
            ins = v.bn_stats(st[:, t, 6 * h:6 * h + 6], x[:, t, WT * h:WT * h + WT])
    E.link(ins)
    for t in range(tiles):
        ins = v.bn_aggr(st[:, t, 12:14], st[:, t, 0:12])
    E.link(ins)
    mean, square = st[:, 0:tiles, 12], st[:, 0:tiles, 13]
    E.link(v.tensor_tensor(mean, mean, mean, ALU.mult))
    E.link(v.scalar_tensor_tensor(square, square, EPS, mean, ALU.add, ALU.add))
    dve_rsqrt(E, st[:, 0:tiles, 14], square, st[:, 0:tiles, 15])
    for t in range(tiles):
        ins = v.scalar_tensor_tensor(dst[:, t, :], x[:, t, :], st[:, t, 14:15], gain, ALU.mult, ALU.mult)
    E.link(ins)


def dve_rope(E, x, heads, half, cos, sin, ta, tb):
    v = E.eng
    w = heads * 2 * half
    x4 = x.rearrange("p t (h a d) -> p t h a d", h=heads, a=2)
    a4 = ta[:, :, 0:w].rearrange("p t (h a d) -> p t h a d", h=heads, a=2)
    b4 = tb[:, :, 0:w].rearrange("p t (h a d) -> p t h a d", h=heads, a=2)
    shape = [P, heads, half]
    for t in range(T):
        c = cos[:, t, :].unsqueeze(1).to_broadcast(shape)
        s = sin[:, t, :].unsqueeze(1).to_broadcast(shape)
        for a in range(2):
            v.tensor_tensor(a4[:, t, :, a, :], x4[:, t, :, a, :], c, ALU.mult)
            ins = v.tensor_tensor(b4[:, t, :, a, :], x4[:, t, :, 1 - a, :], s, ALU.mult)
    E.link(ins)
    for t in range(T):
        v.tensor_tensor(x4[:, t, :, 0, :], a4[:, t, :, 0, :], b4[:, t, :, 0, :], ALU.subtract)
        ins = v.tensor_tensor(x4[:, t, :, 1, :], a4[:, t, :, 1, :], b4[:, t, :, 1, :], ALU.add)
    return ins



def att_plan(a):
    a.pairs = [(n, i) for n in range(T) for i in range(len(a.blocks[n]))]
    a.turns = [a.pairs[i:i + 4] for i in range(0, len(a.pairs), 4)]
    a.npv = WT // a.dv if WT // a.dv < T else T
    a.pvs = T // a.npv
    a.per = T + len(a.turns) + a.pvs
    return a


def att_order(a):
    yield "scores", 0
    for h in range(a.heads):
        if h + 1 < a.heads:
            yield "scores", h + 1
        yield "rest", h


def pe_attention(E, a):
    pe, K = E.eng, E.K
    for what, h in att_order(a):
        if what == "scores":
            for n in range(T):
                m = E.take()
                E.wait_bank(m)
                lo, hi = a.cols(n)
                parts = a.scores(h, n)
                for i, (lhsT, rhs) in enumerate(parts):
                    mm = pe.matmul(E.bank(m)[:, 0:hi - lo], lhsT, rhs, start=(i == 0), stop=(i == len(parts) - 1))
                E.filled(mm, m)
            continue
        pe.wait_ge(K.probs_ready, K.probs_base[a.name] + h + 1)
        t0 = E.n
        pe_transposes(E, [[a.s[:, h % 2, n, a.cols(n)[0] + P * i:a.cols(n)[0] + P * i + P] for n, i in g] for g in a.turns])
        E.wait_evacuated(t0, t0 + len(a.turns))
        for g in range(a.pvs):
            m = E.take()
            E.wait_bank(m)
            for n in range(g * a.npv, (g + 1) * a.npv):
                at = [i for i, (nn, _) in enumerate(a.pairs) if nn == n]
                for j, i in enumerate(at):
                    c = (n - g * a.npv) * a.dv
                    mm = pe.matmul(E.bank(m)[:, c:c + a.dv], a.pT[:, h % 2, i, :], a.value(h, a.blocks[n][j]),
                                   start=(j == 0), stop=(j == len(at) - 1))
            E.filled(mm, m)


def dve_attention(E, a):
    v, K = E.eng, E.K
    base = K.probs_base[a.name]
    for what, h in att_order(a):
        b = h % 2
        if what == "scores":
            for n in range(T):
                m = E.take()
                lo, hi = a.cols(n)
                dst, src = a.s[:, b, n, lo:hi], E.bank(m)[:, 0:hi - lo]
                E.wait_filled(m)
                add = a.addend(h, n)
                if add is None:
                    ins = v.tensor_scalar(dst, src, a.scale, None, ALU.mult)
                else:
                    ins = v.scalar_tensor_tensor(dst, src, a.scale, add, ALU.mult, ALU.add)
                E.evacuated(ins, m)
            E.wait_evacuated(E.n - T, E.n)
            E.link(v.reduce_max(a.st[:, b, 0, :], a.s[:, b, :, :], AX))
            sink = a.sink(h)
            if sink is None:
                ins = v.tensor_scalar(a.st[:, b, 1, :], a.st[:, b, 0, :], -1.0, None, ALU.mult)
            else:
                ins = v.tensor_scalar(a.st[:, b, 1, :], a.st[:, b, 0, :], sink, -1.0, ALU.max, ALU.mult)
            ins.then_inc(K.scores_ready, 1)
            continue
        v.wait_ge(K.probs_ready, base + h + 1)
        if a.sink(h) is not None:
            E.link(v.tensor_tensor(a.st[:, b, 2, :], a.st[:, b, 2, :], a.st[:, b, 3, :], ALU.add))
        E.link(v.reciprocal(a.st[:, b, 4, :], a.st[:, b, 2, :]))
        E.n += len(a.turns)
        for g in range(a.pvs):
            m = E.take()
            E.wait_filled(m)
            lo, hi = g * a.npv, (g + 1) * a.npv
            src = E.bank(m)[:, 0:a.npv * a.dv].rearrange("p (n d) -> p n d", d=a.dv)
            den = a.st[:, b, 4, lo:hi].unsqueeze(2).to_broadcast([P, hi - lo, a.dv])
            E.evacuated(v.tensor_tensor(a.out(h, lo, hi), src, den, ALU.mult), m)


def act_attention(E, a):
    s, K = E.eng, E.K
    base = K.probs_base[a.name]
    pv = {}
    for what, h in att_order(a):
        b = h % 2
        if what == "scores":
            E.n += T
            s.wait_ge(K.scores_ready, base + h + 1)
            for n in range(T):
                row = a.s[:, b, n, a.cols(n)[0]:a.cols(n)[1]]
                ins = s.activation(row, row, ACT.Exp, bias=a.st[:, b, 1, n:n + 1], accum_out=a.st[:, b, 2, n:n + 1])
            if a.sink(h) is not None:
                ins = s.activation(a.st[:, b, 3, :], a.st[:, b, 1, :], ACT.Exp, bias=a.sink(h))
            ins.then_inc(K.probs_ready, 1)
            continue
        if h >= 2:
            for m in pv[h - 2]:
                E.wait_filled(m)
        for g in a.turns:
            m = E.take()
            i = a.pairs.index(g[0])
            E.wait_filled(m)
            dst = a.pT[:, b, i:i + len(g), :].rearrange("p i q -> p (i q)")
            E.evacuated(s.activation(dst, E.bank(m)[:, 0:P * len(g)], ACT.Copy), m)
        pv[h] = list(range(E.n, E.n + a.pvs))
        E.n += a.pvs



def even_views(K):
    A = K.carve(0)
    m = Names()
    m.h = A(T, IN_EVEN)
    m.mix = A(T, D)
    m.cos128, m.sin128, m.cos64, m.sin64 = A(T, 64), A(T, 64), A(T, 32), A(T, 32)
    here = A.at
    m.qaT, m.kaT = A(RH, S), A(RH, S)
    A.at = here
    m.qbT, m.kbT = A(WQ, S)[0:WD], A(WKV, S)[0:WD]
    m.dpos, m.dneg = A(TOEP), A(TOEP)
    m.gn = A(RH * P)
    m.lg = A(32)
    m.sink = A(WQ)
    m.gst = A(3, T * RH)
    m.st = A(2, 5, T)
    here = A.at
    m.ta, m.tb = A(T, 512), A(T, 512)
    A.at = here
    m.G, m.sq = A(RH, TOEP), A(T * RH, P)
    A.at = here
    m.s, m.pT, m.mask = A(2, T, 3 * P), A(2, 10, P), A(3 * P)
    m.zero = m.ta.rearrange("p t c -> p (t c)")[:, 0:D]
    m.W = [m.h[:, :, 0:512], m.h[:, :, 512:1024]]
    m.ga = m.h[:, :, OFF_GA:OFF_QB]
    return m


def even_attention(K):
    m = K.even
    a = Names()
    a.name = "window"
    a.heads = WQ
    a.scale = WD ** -0.5
    a.dv = WD
    a.s = m.s
    a.pT = m.pT
    a.st = m.st
    a.blocks = [[j for j in (n - 1, n, n + 1) if 0 <= j < T] for n in range(T)]
    a.cols = lambda n: (P if n == 0 else 0, 2 * P if n == T - 1 else 3 * P)
    a.scores = lambda h, n: [(m.qbT[:, h, P * n:P * n + P],
                              m.kbT[:, h // (WQ // WKV), P * a.blocks[n][0]:P * a.blocks[n][-1] + P])]
    a.addend = lambda h, n: m.mask[:, a.cols(n)[0]:a.cols(n)[1]]
    a.sink = lambda h: m.sink[:, h:h + 1]
    a.value = lambda h, j: m.h[:, j, OFF_VB + WD * (h // (WQ // WKV)):OFF_VB + WD * (h // (WQ // WKV)) + WD]
    a.out = lambda h, lo, hi: m.mix[:, lo:hi, 512 + WD * h:512 + WD * h + WD]
    return att_plan(a)


EVEN_WIDTHS = [512] * 5 + [256]


def rope_tasks(m):
    tasks = [[m.h[:, t, OFF_QA + P * h:OFF_QA + P * h + P] for t in range(T)] for h in range(RH)]
    tasks += [[m.h[:, t, OFF_KA + P * h:OFF_KA + P * h + P] for t in range(T)] for h in range(RH)]
    tasks += [[m.h[:, t, OFF_QB + WD * h:OFF_QB + WD * h + WD] for t in range(T)] for h in range(WQ)]
    tasks += [[m.h[:, t, OFF_KB + WD * h:OFF_KB + WD * h + WD] for t in range(T)] for h in range(WKV)]
    return tasks


def rope_out(m):
    out = [(m.qaT[:, h, :], lambda b: b) for h in range(RH)] + [(m.kaT[:, h, :], lambda b: b) for h in range(RH)]
    out += [(m.qbT[:, h, :], lambda b: b[0:WD]) for h in range(WQ)] + [(m.kbT[:, h, :], lambda b: b[0:WD]) for h in range(WKV)]
    return [(d, f, "act") for d, f in out]


def pe_even(E):
    K, m, pe = E.K, E.K.even, E.eng
    pe.wait_ge(K.x_loaded, 16)
    pe.wait_ge(K.consts_loaded, 16 * K.CONSTS)
    n0 = E.n
    pe_transposes(E, xt_tasks(K.x))
    E.wait_evacuated(n0, E.n)
    pe_linear(E, K.xT, EVEN_WIDTHS)
    E.phase()
    tasks = rope_tasks(m)
    for i in range(2):
        pe.wait_ge(K.rope_done, i + 1)
        pe_transposes(E, tasks[RH * i:RH * i + RH])
    E.phase()
    for h in range(RH + 1):
        if h < RH:
            for i in range(T):
                n = E.take()
                E.wait_bank(n)
                E.filled(pe.matmul(E.bank(n), m.kaT[:, h, P * i:P * i + P], m.qaT[:, h, :], start=True, stop=True), n)
        if h >= 1:
            g = h - 1
            E.wait_evacuated(K.ret_scores[g], K.ret_scores[g] + T)
            n = E.take()
            E.wait_bank(n)
            for t in range(T):
                for i in range(T):
                    mm = pe.matmul(E.bank(n)[:, P * t:P * t + P], m.W[g % 2][:, i, P * t:P * t + P],
                                   m.h[:, i, OFF_VA + P * g:OFF_VA + P * g + P], start=(i == 0), stop=(i == T - 1))
            E.filled(mm, n)
    E.phase()
    n0 = E.n
    pe_transposes(E, tasks[2 * RH:])
    E.wait_evacuated(n0, E.n)
    pe_attention(E, K.window)
    E.phase()
    mixer_end_pe(E, m.mix, 1)


def mixer_end_pe(E, mix, norm):
    K = E.K
    n0 = E.n
    if mix is not None:
        pe_transposes(E, xt_tasks(mix))
        E.wait_evacuated(n0, E.n)
    pe_linear(E, K.xT, [512] * 2)
    turn_x_pe(E, norm)
    E.phase()


def turn_x_pe(E, norm):
    E.eng.wait_ge(E.K.norm_done, norm)
    n0 = E.n
    pe_transposes(E, xt_tasks(E.K.x))
    E.wait_evacuated(n0, E.n)


def act_even(E):
    K, m, s = E.K, E.K.even, E.eng
    copy_out(E, xt_out(K.xT))
    n0 = E.n
    s.wait_ge(K.rows_zero, 1)
    per = 8
    parts = NOV * SB // per
    s.dma_start(K.ys_dram[NE * SB:, :].rearrange("(p r) d -> p r d", r=per),
                m.zero[0:parts].unsqueeze(1).to_broadcast([parts, per, D])).then_inc(K.rows_stored, 16)
    per = (JOBS + 1) * SB // P
    s.dma_start(K.xs_dram.rearrange("(p r) d -> p r d", r=per), m.zero.unsqueeze(1).to_broadcast([P, per, D])).then_inc(K.rows_cleared, 16)
    copy_out(E, linear_out(m.h, EVEN_WIDTHS))
    E.wait_evacuated(n0, E.n)
    s.wait_ge(K.rows_stored, 16)
    s.wait_ge(K.rows_cleared, 16)
    E.phase()
    s.activation(m.ga, m.ga, ACT.Silu)
    s.wait_ge(K.small_dve, 1)
    s.activation(m.lg[:, 8:16], m.lg[:, 8:16], ACT.Exp, scale=-1.0).then_inc(K.small_act, 1)
    s.wait_ge(K.small_dve, 2)
    s.activation(m.lg[:, 24:32], m.lg[:, 16:24], ACT.Ln).then_inc(K.small_act, 1)
    copy_out(E, rope_out(m)[0:2 * RH])
    E.phase()
    for h in range(RH):
        s.wait_ge(K.decay_exponents, h + 1)
        s.activation(m.G[:, h, :], m.G[:, h, :], ACT.Exp).then_inc(K.decays_ready, 1)
    E.n += (T + 1) * RH
    E.phase()
    copy_out(E, rope_out(m)[2 * RH:])
    act_attention(E, K.window)
    E.phase()
    mixer_end_act(E, m.mix)


def mixer_end_act(E, mix):
    K = E.K
    if mix is not None:
        copy_out(E, xt_out(K.xT))
    residual_out(E, K.x, 2, ALPHA)
    copy_out(E, xt_out(K.xT))
    E.phase()


def dve_log1p_end(E, out, ln, u, e, t):
    v = E.eng
    E.link(v.scalar_tensor_tensor(t, u, -1.0, e, ALU.add, ALU.subtract))
    E.link(v.tensor_tensor(out, ln, t, ALU.subtract))


def dve_even(E):
    K, m, v = E.K, E.K.even, E.eng
    copy_out(E, xt_out(K.xT))
    n0 = E.n
    copy_out(E, linear_out(m.h, EVEN_WIDTHS))
    E.wait_evacuated(n0, E.n)
    E.phase()
    v.wait_ge(K.even_loaded, 16 * K.EVEN_DMAS)
    lg, e, u, ln = m.lg[:, 0:8], m.lg[:, 8:16], m.lg[:, 16:24], m.lg[:, 24:32]
    v.scalar_tensor_tensor(e, lg, -1.0, lg, ALU.mult, ALU.max).then_inc(K.small_dve, 1)
    for x, heads, half, cos, sin in ((m.h[:, :, OFF_QA:OFF_KA], RH, 64, m.cos128, m.sin128),
                                     (m.h[:, :, OFF_KA:OFF_VA], RH, 64, m.cos128, m.sin128),
                                     (m.h[:, :, OFF_QB:OFF_KB], WQ, 32, m.cos64, m.sin64),
                                     (m.h[:, :, OFF_KB:OFF_VB], WKV, 32, m.cos64, m.sin64)):
        K.rope_count += 1
        dve_rope(E, x, heads, half, cos, sin, m.ta, m.tb).then_inc(K.rope_done, 1)
        v.wait_ge(K.rope_done, K.rope_count)
    v.wait_ge(K.small_act, 1)
    v.tensor_scalar(u, e, 1.0, None, ALU.add).then_inc(K.small_dve, 1)
    v.wait_ge(K.small_dve, 2)
    v.wait_ge(K.small_act, 2)
    dve_log1p_end(E, ln, ln, u, e, e)
    E.link(v.scalar_tensor_tensor(lg, lg, 0.0, ln, ALU.min, ALU.subtract))
    copy_out(E, rope_out(m)[0:2 * RH])
    E.phase()
    for h in range(RH):
        E.link(v.tensor_scalar(m.G[:, h, :], m.dneg, lg[:, RH + h:RH + h + 1], None, ALU.mult))
        v.scalar_tensor_tensor(m.G[:, h, :], m.dpos, lg[:, h:h + 1], m.G[:, h, :], ALU.mult, ALU.add).then_inc(K.decay_exponents, 1)
    for h in range(RH + 1):
        if h < RH:
            v.wait_ge(K.decays_ready, h + 1)
            for i in range(T):
                n = E.take()
                E.wait_filled(n)
                E.evacuated(v.scalar_tensor_tensor(m.W[h % 2][:, i, :], E.bank(n), P ** -0.5,
                                                   m.G[:, h, P * (T - 1 - i):P * (T - 1 - i) + S], ALU.mult, ALU.mult), n)
        if h >= 1:
            n = E.take()
            E.wait_filled(n)
            E.evacuated(v.tensor_copy(m.mix[:, :, P * (h - 1):P * h], E.bank(n).rearrange("p (t d) -> p t d", t=T)), n)
    E.wait_evacuated(E.n - 8, E.n)
    ya = m.mix[:, :, 0:512].rearrange("p t (h d) -> p t h d", h=RH)
    sq = m.sq.rearrange("p (t h) d -> p t h d", t=T)
    mu, var, rs = (m.gst[:, i, :].rearrange("p (t h) -> p t h", t=T) for i in range(3))
    E.link(v.reduce_sum(mu, ya, AX))
    E.link(v.tensor_scalar(mu, mu, 1.0 / P, None, ALU.mult))
    for t in range(T):
        ins = v.tensor_tensor(ya[:, t], ya[:, t], mu[:, t].unsqueeze(2).to_broadcast([P, RH, P]), ALU.subtract)
    E.link(ins)
    for t in range(T):
        ins = v.tensor_tensor(sq[:, t], ya[:, t], ya[:, t], ALU.mult)
    E.link(ins)
    E.link(v.reduce_sum(var, sq, AX))
    E.link(v.tensor_scalar(var, var, 1.0 / P, EPS, ALU.mult, ALU.add))
    dve_rsqrt(E, rs, var, mu)
    for t in range(T):
        ins = v.tensor_tensor(ya[:, t], ya[:, t], rs[:, t].unsqueeze(2).to_broadcast([P, RH, P]), ALU.mult)
    E.link(ins)
    for t in range(T):
        ins = v.tensor_tensor(m.mix[:, t, 0:512], m.mix[:, t, 0:512], m.gn, ALU.mult)
    E.link(ins)
    E.link(v.tensor_tensor(m.mix[:, :, 0:512], m.mix[:, :, 0:512], m.ga, ALU.mult))
    E.phase()
    for b in range(2):
        v.memset(m.s[:, b, 0, 0:P], NEG)
        ins = v.memset(m.s[:, b, T - 1, 2 * P:3 * P], NEG)
    E.link(ins)
    v.wait_ge(K.mask_loaded, 16)
    copy_out(E, rope_out(m)[2 * RH:])
    dve_attention(E, K.window)
    E.phase()
    mixer_end_dve(E, m.mix, 0)


def mixer_end_dve(E, mix, layer):
    K = E.K
    if mix is not None:
        copy_out(E, xt_out(K.xT))
    n0 = E.n
    residual_out(E, K.x, 2, ALPHA)
    E.wait_evacuated(n0, E.n)
    E.eng.wait_ge(K.gains_loaded, 16 * 2 * (2 * layer + 1))
    dve_layer_norm(E, K.x, K.gains[:, 0, :], K.gains[:, 1, :], K.lnst)
    E.eng.drain().then_inc(K.norm_done, 1)
    copy_out(E, xt_out(K.xT))
    E.phase()



def fourier_views(K):
    A = K.carve(0)
    m = Names()
    m.feat = A(2, 512)
    m.cs, m.sn = A(T, S), A(T, S)
    m.z = A(T, 4, 512)
    return m


def pe_fourier(E):
    K, m, pe = E.K, E.K.fourier, E.eng
    pe.wait_ge(K.fourier_loaded, 16 * 3)
    n0 = E.n
    for t in range(T):
        for g in range(4):
            n = E.take()
            E.wait_bank(n)
            for k in range(2):
                mm = pe.matmul(E.bank(n), K.xT[:, 2 * g + k, P * t:P * t + P], m.feat[:, k, :], start=(k == 0), stop=(k == 1))
            E.filled(mm, n)
    E.wait_evacuated(n0, E.n)
    n0 = E.n
    for k in range(KD):
        g, c = k // 2, P * (k % 2)
        n = E.take()
        E.wait_bank(n)
        for t in range(T):
            pe.matmul(E.bank(n), m.z[:, t, g, c:c + P], m.cs[:, t, :], start=(t == 0), stop=False)
        for t in range(T):
            mm = pe.matmul(E.bank(n), m.z[:, t, g, 256 + c:256 + c + P], m.sn[:, t, :], start=False, stop=(t == T - 1))
        E.filled(mm, n)
    E.wait_evacuated(n0, E.n)
    mixer_end_pe(E, None, 3)


def fourier_out(E):
    K, m = E.K, E.K.fourier
    copy_out(E, [(m.z[:, t, g, :], lambda b: b, turn(g)) for t in range(T) for g in range(4)])
    copy_out(E, xt_out(K.xT))
    (mixer_end_act if E.name == "act" else lambda E, x: mixer_end_dve(E, x, 1))(E, None)



def moe_views(K):
    A = K.carve(0)
    m = Names()
    m.wr, m.br = A(KD, NG + NE), A(NG + NE)
    m.iota, m.iotag, m.iotaj = A(NE), A(NE), A(NOV, NE)
    m.lg, m.cp, m.mx, m.fm = A(T, NG + NE), A(T, 8), A(T, 8), A(T, NE)
    m.ix, m.mk = A(T, 8), A(T, NE)
    m.one = A(2, T, NE)
    m.A, m.rk, m.tmp = A(T, NE), A(5, NE), A(T, NE)
    m.ov, m.ovend, m.extra, m.zero = A(NE), A(NE), A(NE), A(NE)
    m.c = A(16, T)
    m.slot = A(2, T)
    m.jt, m.jx, m.ja = A(NOV + 2), A(NOV, NE), A(NOV, NE)
    m.xs, m.xsT = A(D)[0:SB], A(KD, SB)
    m.sg, m.hid, m.hidT = A(EH)[0:SB], A(EH)[0:SB], A(EH // P, SB)
    m.y = A(WT)[0:2 * SB]
    m.xs_blocks = m.xs.rearrange("s (p k) -> s k p", k=KD)
    m.hid_blocks = m.hid.rearrange("s (p k) -> s k p", k=EH // P)
    m.g = A(2, T, D)
    m.more = A(3, KD * WT)
    return m


def dve_skip(E, count):
    for _ in range(count):
        n = E.take()
        E.wait_filled(n)
        E.evacuated(E.eng.nop(), n)


def store_y(E, job, signal):
    K = E.K
    for h in range(2):
        E.eng.dma_start(K.ys_dram[bass.ds(job * SB, SB), WT * h:WT * h + WT], K.moe.y[SB * h:SB * h + SB, :]).then_inc(signal, 16)


def stored(layer, jobs):
    return 16 + 32 * (NE * layer + jobs)


def load_rows(E, job, signal):
    E.eng.dma_start(E.K.moe.xs, E.K.xs_dram[bass.ds(job * SB, SB), :]).then_inc(signal, 16)


def moe_rows(E, bank):
    m = E.K.moe
    for k in range(KD):
        tr = E.eng.matmul(bank[:, SB * k:SB * k + SB], m.xs_blocks[:, k, :], E.K.ident[0:SB, 0:SB], start=True, stop=True)
        if k == 0:
            first = tr
    return first, tr


def moe_gate_up(E, bank, gate, up):
    m = E.K.moe
    for k in range(KD):
        for i, w in enumerate((gate, up)):
            mm = E.eng.matmul(bank[SB * i:SB * i + SB, :], m.xsT[:, k, :], w[:, k, :], start=(k == 0), stop=(k == KD - 1))
    return mm


def moe_hidden(E, bank):
    m = E.K.moe
    for k in range(EH // P):
        tr = E.eng.matmul(bank[:, SB * k:SB * k + SB], m.hid_blocks[:, k, :], E.K.ident[0:SB, 0:SB], start=True, stop=True)
        if k == 0:
            first = tr
    return first, tr


def moe_down(E, bank, down):
    m = E.K.moe
    for k in range(EH // P):
        for i in range(2):
            mm = E.eng.matmul(bank[SB * i:SB * i + SB, :], m.hidT[:, k, :], down[:, k, WT * i:WT * i + WT],
                              start=(k == 0), stop=(k == EH // P - 1))
    return mm


def slot_weights(K, i):
    return lambda slot: K.ring[:, slot, :].rearrange("p (k n) -> p k n", k=KD if i < 2 else EH // P)


def job_weights(E, layer, w0, i, odd, j, c):
    K = E.K
    if odd:
        E.eng.wait_ge(K.more_loaded[i], j * 16 + 16 * (NE // 2 * layer + c + 1))
        return K.moe.more[:, i, :].rearrange("p (k n) -> p k n", k=KD if i < 2 else EH // P)
    w = w0 + i
    E.eng.wait_ge(K.w_loaded[w % RING], j * 16 + 16 * (w // RING + c + 1))
    return slot_weights(K, i)(w % RING)


def wait_before(E, n):
    if E.loop is not None and n < E.loop[3]:
        E.wait_bank(n + 8)
    else:
        E.wait_evacuated(n, n + 1)


def pe_moe(E, layer):
    K, m, pe = E.K, E.K.moe, E.eng
    pe.wait_ge(K.moe_loaded, 16 * K.MOE_DMAS * (layer + 1))
    n = E.take()
    E.wait_bank(n)
    for t in range(T):
        for k in range(KD):
            mm = pe.matmul(E.bank(n)[:, 36 * t:36 * t + 36], K.xT[:, k, P * t:P * t + P], m.wr[:, k, :],
                           start=(k == 0), stop=(k == KD - 1))
    E.filled(mm, n)
    pe.wait_ge(K.choices_ready, layer + 1)
    n = E.take()
    E.wait_bank(n)
    for t in range(T):
        for u in range(t + 1):
            pe.matmul(E.bank(n)[:, NE * t:NE * t + NE], K.before if u == t else K.ones, m.A[:, u, :],
                      start=(u == 0), stop=(u == t))
    for u in range(T):
        mm = pe.matmul(E.bank(n)[:, NE * T:NE * T + NE], K.ones, m.A[:, u, :], start=(u == 0), stop=(u == T - 1))
    E.filled(mm, n)

    xs0 = 16 * (NE + 1) * layer
    w0 = E.w
    used = (K.w_used, K.more_used)

    def rows(count, after_gate=False):
        n = E.take()
        pe.wait_ge(K.xs_loaded, count)
        E.wait_bank(n)
        first, last = moe_rows(E, E.bank(n))
        if after_gate:
            first.then_inc(K.w_used, 2)
        E.filled(last, n)

    def gate_up(odd, j, c):
        gate, up = (job_weights(E, layer, w0, i, odd, j, c) for i in range(2))
        n = E.take()
        E.wait_bank(n)
        E.filled(moe_gate_up(E, E.bank(n), gate, up), n)

    def hidden(odd=None):
        n = E.take()
        E.wait_bank(n)
        first, last = moe_hidden(E, E.bank(n))
        if odd is not None:
            first.then_inc(used[odd], 2)
        E.filled(last, n)

    def down(odd, j, c):
        mat = job_weights(E, layer, w0, 2, odd, j, c)
        n = E.take()
        E.wait_bank(n)
        E.filled(moe_down(E, E.bank(n), mat), n)
        pe.drain().then_inc(used[odd], 1)

    while E.n % 4 != 2:
        E.skip()
    rows(xs0 + 16)
    E.skip()
    E.wait_evacuated(E.n - 2, E.n - 1)
    gate_up(0, 0, 0)
    E.skip()
    rows(xs0 + 32, True)
    E.skip()
    with pe.Fori(0, NE // 2 - 1) as j:
        E.begin_loop(j, 8, 0)
        for u in range(2):
            n = E.n
            wait_before(E, n - 2)
            gate_up(1 - u, j, u)
            wait_before(E, n - 4)
            hidden(1 - u)
            rows(j * 32 + (xs0 + 16 * (u + 3)))
            E.wait_evacuated(n + 1, n + 2)
            down(u, j, 0)
        E.end_loop(NE // 2 - 1)
    n, c = E.n, NE // 2 - 1
    E.wait_evacuated(n - 2, n - 1)
    gate_up(1, 0, c)
    E.wait_evacuated(n - 4, n - 3)
    hidden(1)
    E.wait_evacuated(n + 1, n + 2)
    down(0, 0, c)
    E.wait_evacuated(n, n + 1)
    hidden()
    E.wait_evacuated(n + 3, n + 4)
    down(1, 0, c)
    E.w = w0 + 3 * NE // 2
    E.wait_evacuated(E.n - 8, E.n)
    V = K.beyond[layer]
    some = pe.value_load(K.moe.jt.bitcast(I32)[0:1, NOV + 1:NOV + 2], min_val=0, max_val=NOV)
    with pe.If(some > 0):
        with pe.Fori(0, NOV) as j:
            pe.wait_ge(V.xs, j * 16 + 16)
            moe_rows(E, K.ps[:, 0, :])[1].then_inc(V.pe, 1)
            pe.wait_ge(V.w, j * 48 + 48)
            pe.wait_ge(V.dve, j * 4 + 1)
            moe_gate_up(E, K.ps[:, 1, :], slot_weights(K, 0)(0), slot_weights(K, 1)(1)).then_inc(V.pe, 1)
            pe.wait_ge(V.dve, j * 4 + 2)
            moe_hidden(E, K.ps[:, 2, :])[1].then_inc(V.pe, 1)
            pe.wait_ge(V.dve, j * 4 + 3)
            moe_down(E, K.ps[:, 3, :], slot_weights(K, 2)(2)).then_inc(V.pe, 1)
    pe.drain()


def act_moe(E, layer):
    K, m, s = E.K, E.K.moe, E.eng
    E.n += 1
    s.wait_ge(K.router_dve, 2 * layer + 1)
    s.activation(m.cp[:, :, 0:4], m.cp[:, :, 0:4], ACT.Exp).then_inc(K.router_act, 1)
    s.wait_ge(K.router_dve, 2 * layer + 2)
    s.activation(m.c[:, 3, :], m.c[:, 3, :], ACT.Exp).then_inc(K.router_act, 1)
    E.n += 1

    while E.n % 4 != 2:
        E.n += 1
    s.wait_ge(K.x_scattered, 16 * 2 * T * (layer + 1))
    xs0 = 16 * (NE + 1) * layer

    def silu(n):
        E.wait_filled(n)
        s.activation(m.sg, E.bank(n)[0:SB, :], ACT.Silu).then_inc(K.silu_done, 1)

    def y(n, job, before):
        s.wait_ge(K.rows_stored, before)
        E.wait_filled(n)
        E.evacuated(s.activation(m.y, E.bank(n)[0:2 * SB, :], ACT.Copy), n)
        E.wait_evacuated(n, n + 1)
        store_y(E, job, K.rows_stored)

    load_rows(E, 0, K.xs_loaded)
    E.wait_filled(E.n)
    s.wait_ge(K.xs_loaded, xs0 + 16)
    load_rows(E, 1, K.xs_loaded)
    silu(E.n + 2)
    E.wait_filled(E.n + 4)
    s.wait_ge(K.xs_loaded, xs0 + 32)
    load_rows(E, 2, K.xs_loaded)
    E.n += 6
    with s.Fori(0, NE // 2 - 1) as j:
        E.begin_loop(j, 8, 0)
        for u in range(2):
            n = E.n
            wait_before(E, n - 4)
            silu(n)
            E.wait_filled(n + 2)
            load_rows(E, j * 2 + (u + 3), K.xs_loaded)
            y(n + 3, j * 2 + u, j * 64 + stored(layer, u))
            E.n += 4
        E.end_loop(NE // 2 - 1)
    n = E.n
    E.wait_evacuated(n - 4, n - 3)
    silu(n)
    y(n + 2, NE - 2, stored(layer, NE - 2))
    y(n + 4, NE - 1, stored(layer, NE - 1))
    E.n += 5
    s.wait_ge(K.rows_stored, stored(layer, NE))
    s.wait_ge(K.xs_loaded, 16 * (NE + 1) * (layer + 1))
    V = K.beyond[layer]
    some = s.value_load(m.jt.bitcast(I32)[0:1, NOV + 1:NOV + 2], min_val=0, max_val=NOV)
    with s.If(some > 0):
        load_rows(E, NE, V.xs)
        with s.Fori(0, NOV) as j:
            s.wait_ge(V.pe, j * 4 + 1)
            load_rows(E, j + (NE + 1), V.xs)
            s.wait_ge(V.pe, j * 4 + 2)
            s.activation(m.sg, K.ps[0:SB, 1, :], ACT.Silu).then_inc(V.act, 1)
            s.wait_ge(V.dve, j * 4 + 4)
            store_y(E, j + NE, V.rows)
        s.wait_ge(V.xs, 16 * (NOV + 1))
    s.drain()


def dve_moe(E, layer):
    K, m, v = E.K, E.K.moe, E.eng
    L = E.link
    c = lambda i: m.c[:, i, :]
    v.wait_ge(K.moe_loaded, 16 * K.MOE_DMAS * (layer + 1))
    v.memset(m.cp, NEG)
    L(v.memset(m.zero, 0.0))
    n = E.take()
    E.wait_filled(n)
    E.evacuated(v.tensor_tensor(m.lg, E.bank(n)[:, 0:T * 36].rearrange("p (t e) -> p t e", t=T),
                                m.br.unsqueeze(1).to_broadcast([P, T, 36]), ALU.add), n)
    E.wait_evacuated(n, n + 1)
    L(v.tensor_copy(m.cp[:, :, 0:NG], m.lg[:, :, 0:NG]))
    for t in range(T):
        ins = v.max(m.mx[:, t, :], m.cp[:, t, :])
    L(ins)
    for t in range(T):
        ins = v.max_index(m.ix.bitcast(U32)[:, t, :], m.mx[:, t, :], m.cp[:, t, :])
    L(ins)
    L(v.tensor_copy(c(0), m.ix.bitcast(U32)[:, :, 0]))
    v.tensor_tensor(m.cp[:, :, 0:NG], m.lg[:, :, 0:NG], m.mx[:, :, 0:1].to_broadcast([P, T, NG]),
                    ALU.subtract).then_inc(K.router_dve, 1)
    for t in range(T):
        ins = v.tensor_scalar(m.mk[:, t, :], m.iotag, m.c[:, 0, t:t + 1], None, ALU.is_equal)
    L(ins)
    v.wait_ge(K.router_act, 2 * layer + 1)
    L(v.reduce_sum(c(1), m.cp[:, :, 0:NG], AX))
    L(v.reciprocal(c(1), c(1)))
    L(v.tensor_tensor(m.fm, m.lg[:, :, NG:], m.mk, ALU.mult))
    L(v.tensor_scalar(m.mk, m.mk, -NEG, NEG, ALU.mult, ALU.add))
    L(v.tensor_tensor(m.fm, m.fm, m.mk, ALU.add))
    for t in range(T):
        ins = v.max(m.mx[:, t, :], m.fm[:, t, :])
    L(ins)
    for t in range(T):
        ins = v.max_index(m.ix.bitcast(U32)[:, t, :], m.mx[:, t, :], m.fm[:, t, :])
    L(ins)
    v.tensor_tensor(c(3), m.mx[:, :, 1], m.mx[:, :, 0], ALU.subtract).then_inc(K.router_dve, 1)
    for k in range(2):
        ins = v.tensor_copy(c(4 + k), m.ix.bitcast(U32)[:, :, k])
    L(ins)
    for k in range(2):
        for t in range(T):
            ins = v.tensor_scalar(m.one[:, k, t, :], m.iota, m.c[:, 4 + k, t:t + 1], None, ALU.is_equal)
    L(ins)
    v.tensor_tensor(m.A, m.one[:, 0], m.one[:, 1], ALU.add).then_inc(K.choices_ready, 1)
    v.wait_ge(K.router_act, 2 * layer + 2)
    L(v.tensor_scalar(c(6), c(3), 1.0, None, ALU.add))
    L(v.reciprocal(c(6), c(6)))
    L(v.tensor_tensor(c(6), c(6), c(1), ALU.mult))
    L(v.tensor_tensor(c(7), c(6), c(3), ALU.mult))
    n = E.take()
    E.wait_filled(n)
    E.evacuated(v.tensor_copy(m.rk, E.bank(n)[:, 0:5 * NE].rearrange("p (a e) -> p a e", a=5)), n)
    E.wait_evacuated(n, n + 1)
    cnt = m.rk[:, T, :]
    L(v.tensor_scalar(m.extra, cnt, SB + 0.5, None, ALU.is_gt))
    for q in range(2, S // SB):
        L(v.scalar_tensor_tensor(m.extra, cnt, SB * q + 0.5, m.extra, ALU.is_gt, ALU.add))
    L(v.tensor_tensor_scan(m.ovend, m.extra, m.zero, 0.0, ALU.add, ALU.add))
    L(v.tensor_tensor(m.ov, m.ovend, m.extra, ALU.subtract))
    for k in range(2):
        r, o, ch, nz, e = c(8), c(9), c(10), c(11), c(4 + k)
        L(v.tensor_tensor(m.tmp, m.rk[:, 0:T, :], m.one[:, k], ALU.mult))
        L(v.reduce_sum(r, m.tmp, AX))
        L(v.tensor_tensor(m.tmp, m.ov.unsqueeze(1).to_broadcast([P, T, NE]), m.one[:, k], ALU.mult))
        L(v.reduce_sum(o, m.tmp, AX))
        L(v.tensor_scalar(nz, r, SB - 0.5, None, ALU.is_gt))
        L(v.tensor_copy(ch, nz))
        for q in range(2, S // SB):
            L(v.scalar_tensor_tensor(ch, r, SB * q - 0.5, ch, ALU.is_gt, ALU.add))
        L(v.tensor_tensor(o, o, ch, ALU.add))
        L(v.tensor_tensor(o, o, e, ALU.subtract))
        L(v.scalar_tensor_tensor(o, o, NE - 1.0, nz, ALU.add, ALU.mult))
        L(v.tensor_tensor(o, o, e, ALU.add))
        L(v.tensor_tensor(o, o, ch, ALU.subtract))
        L(v.scalar_tensor_tensor(o, o, float(SB), r, ALU.mult, ALU.add))
        L(v.tensor_copy(m.slot.bitcast(I32)[:, k, :], o))
    ovb = m.ov.unsqueeze(1).to_broadcast([P, NOV, NE])
    oveb = m.ovend.unsqueeze(1).to_broadcast([P, NOV, NE])
    v.tensor_tensor(m.jx, m.iotaj, ovb, ALU.is_ge)
    L(v.tensor_tensor(m.ja, m.iotaj, oveb, ALU.is_lt))
    L(v.tensor_tensor(m.jx, m.jx, m.ja, ALU.mult))
    L(v.tensor_tensor(m.jx, m.jx, m.iota.unsqueeze(1).to_broadcast([P, NOV, NE]), ALU.mult))
    L(v.reduce_sum(m.ja[:, 0, 0:NOV], m.jx, AX))
    L(v.memset(m.jt, 0.0))
    L(v.tensor_copy(m.jt.bitcast(I32)[:, NOV + 1:NOV + 2], m.ovend[:, NE - 1:NE]))
    L(v.tensor_copy(m.jt.bitcast(I32)[:, 0:NOV], m.ja[:, 0, 0:NOV]))
    v.drain().then_inc(K.slots_ready, 1)

    while E.n % 4 != 2:
        dve_skip(E, 1)

    def rows(n):
        E.wait_filled(n)
        E.evacuated(v.tensor_copy(m.xsT.rearrange("p k t -> p (k t)"), E.bank(n)[:, 0:KD * SB]), n)

    def product(n, count):
        v.wait_ge(K.silu_done, count)
        E.evacuated(v.tensor_tensor(m.hid, m.sg, E.bank(n)[SB:2 * SB, :], ALU.mult), n)

    def hidden(n):
        E.wait_filled(n)
        E.evacuated(v.tensor_copy(m.hidT.rearrange("p k t -> p (k t)"), E.bank(n)[:, 0:SB * EH // P]), n)

    rows(E.n)
    E.n += 1
    dve_skip(E, 1)
    product(E.n, NE * layer + 1)
    E.n += 1
    dve_skip(E, 1)
    rows(E.n)
    E.n += 1
    dve_skip(E, 1)
    with v.Fori(0, NE // 2 - 1) as j:
        E.begin_loop(j, 8, 0)
        for u in range(2):
            n = E.n
            hidden(n + 1)
            rows(n + 2)
            product(n, j * 2 + (NE * layer + u + 2))
            E.n += 4
        E.end_loop(NE // 2 - 1)
    n = E.n
    hidden(n + 1)
    product(n, NE * layer + NE)
    hidden(n + 3)
    E.n += 5
    V = K.beyond[layer]
    some = v.value_load(m.jt.bitcast(I32)[0:1, NOV + 1:NOV + 2], min_val=0, max_val=NOV)
    with v.If(some > 0):
        v.wait_ge(K.rows_stored, stored(layer, NE))
        with v.Fori(0, NOV) as j:
            v.wait_ge(V.pe, j * 4 + 1)
            v.tensor_copy(m.xsT.rearrange("p k t -> p (k t)"), K.ps[:, 0, 0:KD * SB]).then_inc(V.dve, 1)
            v.wait_ge(V.pe, j * 4 + 2)
            v.wait_ge(V.act, j + 1)
            v.tensor_tensor(m.hid, m.sg, K.ps[SB:2 * SB, 1, :], ALU.mult).then_inc(V.dve, 1)
            v.wait_ge(V.pe, j * 4 + 3)
            v.tensor_copy(m.hidT.rearrange("p k t -> p (k t)"), K.ps[:, 2, 0:SB * EH // P]).then_inc(V.dve, 1)
            v.wait_ge(V.pe, j * 4 + 4)
            v.tensor_copy(m.y, K.ps[0:2 * SB, 3, :]).then_inc(V.dve, 1)
            v.wait_ge(V.rows, j * 32 + 32)
    v.drain()
    L(v.tensor_scalar(K.x, K.x, ALPHA, None, ALU.mult))
    for t in range(T):
        v.wait_ge(K.y_gathered[t], 32 * (layer + 1))
        for k in range(2):
            L(v.scalar_tensor_tensor(K.x[:, t, :], m.g[:, k, t, :], m.c[:, 6 + k, t:t + 1], K.x[:, t, :], ALU.mult, ALU.add))
    v.wait_ge(K.gains_loaded, 16 * 2 * (2 * layer + 2))
    dve_layer_norm(E, K.x, K.gains[:, 0, :], K.gains[:, 1, :], K.lnst)
    v.drain().then_inc(K.norm_done, 1)


def pool_moe(E, layer):
    K, m, g = E.K, E.K.moe, E.eng
    g.dma_start(m.wr[:, :, NG:], K.d.router_fine_w[layer].rearrange("(k p) e -> p k e", p=P)).then_inc(K.moe_loaded, 16)
    g.dma_start(m.wr[:, :, 0:NG], K.d.router_coarse_w[layer].rearrange("(k p) e -> p k e", p=P)).then_inc(K.moe_loaded, 16)
    g.dma_start(m.br[:, 0:NG], K.d.router_coarse_b[layer:layer + 1, :].to_broadcast([P, NG])).then_inc(K.moe_loaded, 16)
    g.dma_start(m.br[:, NG:], K.d.router_fine_b[layer:layer + 1, :].to_broadcast([P, NE])).then_inc(K.moe_loaded, 16)
    g.dma_start(m.iota, K.d.c_iota).then_inc(K.moe_loaded, 16)
    g.dma_start(m.iotag, K.d.c_iotag).then_inc(K.moe_loaded, 16)
    g.dma_start(m.iotaj, K.d.c_iotaj).then_inc(K.moe_loaded, 16)
    g.wait_ge(K.norm_done, 2 * layer + 1)
    load_gains(E, K.d.ln2_gain[layer:layer + 1, :], K.d.ln2_bias[layer:layer + 1, :])
    g.wait_ge(K.rows_cleared, 16)
    g.wait_ge(K.slots_ready, layer + 1)
    for k in range(2):
        for t in range(T):
            g.indirect_dma_start(out=K.xs_dram, out_offset=bass.IndirectOffsetOnAxis(ap=m.slot.bitcast(U32)[:, k, t:t + 1], axis=0),
                                 in_=K.x[:, t, :], in_offset=None).then_inc(K.x_scattered, 16)
    E.n += 2
    while E.n % 4 != 2:
        E.n += 1
    E.n += 6 + 4 * (NE - 2) + 5
    g.wait_ge(K.x_scattered, 16 * 2 * T * (layer + 1))
    g.wait_ge(K.rows_stored, stored(layer, NE))
    V = K.beyond[layer]
    some = g.value_load(m.jt.bitcast(I32)[0:1, NOV + 1:NOV + 2], min_val=0, max_val=NOV)
    with g.If(some > 0):
        g.wait_ge(V.rows, 32 * NOV)
    g.drain()
    g.wait_ge(K.jobs_read, layer + 1)
    for t in range(T):
        for k in range(2):
            g.indirect_dma_start(out=m.g[:, k, t, :], out_offset=None, in_=K.ys_dram,
                                 in_offset=bass.IndirectOffsetOnAxis(ap=m.slot.bitcast(U32)[:, k, t:t + 1], axis=0)).then_inc(K.y_gathered[t], 16)


def load_gains(E, *rows):
    for i, row in enumerate(rows):
        E.eng.dma_start(E.K.gains[:, i, :], row.to_broadcast([P, D])).then_inc(E.K.gains_loaded, 16)


def pool_even(E):
    K, m, g, d = E.K, E.K.even, E.eng, E.K.d
    g.dma_start(K.x, d.x[0].rearrange("(t p) d -> p t d", p=P)).then_inc(K.x_loaded, 16)
    g.memset(m.zero, 0.0).then_inc(K.rows_zero, 1)
    for dst, src in ((K.ident, d.c_ident), (K.ones, d.c_ones), (K.before, d.c_before), (K.upto, d.c_upto), (K.since, d.c_since)):
        g.dma_start(dst, src).then_inc(K.consts_loaded, 16)
    loads = [(m.cos128, d.c_cos128), (m.sin128, d.c_sin128), (m.cos64, d.c_cos64), (m.sin64, d.c_sin64),
             (m.dpos, d.c_dpos), (m.dneg, d.c_dneg),
             (m.gn, d.ret_gn_gain.to_broadcast([P, RH * P])),
             (m.lg[:, 0:8], d.ret_decay_logit.rearrange("a b h -> a (b h)").to_broadcast([P, 8])),
             (m.sink, d.sink_logit.to_broadcast([P, WQ]))]
    assert len(loads) == K.EVEN_DMAS
    for dst, src in loads:
        g.dma_start(dst, src).then_inc(K.even_loaded, 16)
    load_gains(E, d.ln1_gain[0:1, :], d.ln1_bias[0:1, :])
    for _ in range(3):
        E.phase()
    g.dma_start(m.mask, d.c_mask).then_inc(K.mask_loaded, 16)
    E.phase()
    E.phase()
    E.n = K.after_even


def pool_fourier(E):
    K, m, g, d = E.K, E.K.fourier, E.eng, E.K.d
    g.dma_start(m.feat, d.c_feat).then_inc(K.fourier_loaded, 16)
    g.dma_start(m.cs, d.c_cs).then_inc(K.fourier_loaded, 16)
    g.dma_start(m.sn, d.c_sn).then_inc(K.fourier_loaded, 16)
    load_gains(E, d.ln1_gain[1:2, :], d.ln1_bias[1:2, :])
    E.phase()
    E.n += 16 + KD + 2 * T + KD



def second_views(K):
    A = K.carve(0)
    m = Names()
    m.mix = A(T, D)
    m.gates = A(36, T)
    m.small = A(13, T, 12)
    m.par = A(2 * MLH * 2 + 2 * GDH * 2)
    m.nw = K.gains[:, 1, 512:512 + GDH * HD]
    base = A.at
    m.h = A(T, W2_ML)
    m.bias, m.near, m.far = A(NAH, 14, HD), A(HD), A(HD)
    m.nqT, m.nkT = A(NAH, S)[0:HD], A(NAH, S)[0:HD]
    m.s, m.pT, m.st = A(2, T, S), A(2, 16, P), A(2, 5, T)
    A.at = base
    m.hm = A(T, C2_MLE)
    m.mqT, m.mkT = A(MLH, S)[0:HD], A(MLH, S)[0:HD]
    m.ST, m.W, m.Dm = A(T, S), A(2, T, S), A(2, T, S)
    m.v1 = A(T, MLH, HD + 1)
    m.hs, m.ex = A(T, 256), A(T, 256)
    m.hsq = m.Dm[:, 0].rearrange("p a c -> p (a c)")[:, 0:T * 256].rearrange("p (t c) -> p t c", t=T)
    m.rows, m.zrow = A(2, S), A(S)
    m.norm = A(2, T, HD + 1)
    A.at = base
    m.hz = A(T, C2_ZE)
    m.tm = A(T, GDC)
    m.levels = A(2, LEVELS, P)
    base = A.at
    m.cin, m.cout = A(GCT, S + 4), A(GCT, S)
    m.cw = A(GCT, 5)
    m.gtmp = A(T, 2 * GDH * HD)
    A.at = base
    m.gqT, m.gkT = A(GDH, S)[0:HD], A(GDH, S)[0:HD]
    U = (4, 3, P)
    V = (4, 3, HD)
    m.E, m.AT, m.X = A(*U), A(*U), A(*U)
    m.at = m.E
    m.qd, m.nw_T = A(*U)[0:HD], A(*U)[0:HD]
    m.vb, m.kbe, m.ks, m.vn = A(*V), A(*V), A(*V), A(*V)
    spare = K.xT.rearrange("p k s -> p (k s)")
    size = 12 * P
    m.Ti, m.TiT = (spare[:, size * i:size * i + size].rearrange("p (g u l) -> p g u l", g=4, u=3) for i in range(2))
    m.state = spare[0:HD, 2 * size:2 * size + 2 * GDH * HD].rearrange("p (h d) -> p h d", h=2 * GDH)
    m.o = K.gains.rearrange("p a d -> p (a d)")[:, 0:T * GDH * HD].rearrange("p (t c) -> p t c", t=T)
    flat = lambda ap: ap.rearrange("p g u l -> p (g u l)").rearrange("p (t c) -> p t c", t=T)
    m.osq, m.ez = flat(m.AT), flat(m.Ti)
    return m


def cross_views(K):
    A = K.carve(0)
    m = Names()
    m.hn, m.mem = A(T, D), A(2, D)
    m.memT = A(KD, MEMN)
    m.qT, m.kT, m.v = A(KD, S), A(KD, MEMN), A(2, D)
    m.s, m.pT, m.st = A(2, T, MEMN), A(2, 8, P), A(2, 5, T)
    m.mix = m.hn
    m.tmp, m.nst = A(D), A(T, 4)
    m.gain = A(D)
    return m


def ffn_views(K):
    A = K.carve(0)
    m = Names()
    m.hT = A(FFT, S)
    m.hn = A(T, D)
    m.tmp, m.nst = A(D), A(T, 4)
    m.r = A(2, S)
    return m


NEAR_WIDTHS = [512, 512, W2_ML - 1024]
ML_WIDTHS = [512, 512, C2_MLE - 1024]


def near_attention(K):
    m = K.second
    a = Names()
    a.name = "near"
    a.heads = NAH
    a.scale = HD ** -0.5
    a.dv = HD
    a.s = m.s
    a.pT = m.pT
    a.st = m.st
    a.blocks = [list(range(T))] * T
    a.cols = lambda n: (0, S)
    a.scores = lambda h, n: [(m.nqT[:, h, P * n:P * n + P], m.nkT[:, h, :])]
    a.addend = lambda h, n: m.bias[:, h, 6 - 2 * n:14 - 2 * n, :].rearrange("p r c -> p (r c)")
    a.sink = lambda h: None
    a.value = lambda h, j: m.h[:, j, C2_NAV + HD * h:C2_NAV + HD * h + HD]
    a.out = lambda h, lo, hi: m.mix[:, lo:hi, HD * h:HD * h + HD]
    return att_plan(a)


def cross_attention(K):
    m = K.cross
    a = Names()
    a.name = "memory"
    a.heads = XH
    a.scale = XD ** -0.5
    a.dv = XD
    a.s = m.s
    a.pT = m.pT
    a.st = m.st
    a.blocks = [[0, 1]] * T
    a.cols = lambda n: (0, MEMN)
    a.scores = lambda h, n: [(m.qT[:, 2 * h + i, P * n:P * n + P], m.kT[:, 2 * h + i, :]) for i in range(2)]
    a.addend = lambda h, n: None
    a.sink = lambda h: None
    a.value = lambda h, j: m.v[:, j, XD * h:XD * h + XD]
    a.out = lambda h, lo, hi: m.mix[:, lo:hi, XD * h:XD * h + XD]
    return att_plan(a)


def head_tasks(src, heads, dst, who=None):
    tasks = [[src[:, t, HD * h:HD * h + HD] for t in range(T)] for h in range(heads)]
    return tasks, [(dst[:, h, :], lambda b: b[0:HD], who or turn(h)) for h in range(heads)]


def second_head_tasks(m):
    a = head_tasks(m.h[:, :, C2_NAQ:C2_NAK], NAH, m.nqT)
    b = head_tasks(m.h[:, :, C2_NAK:C2_NAV], NAH, m.nkT)
    return a[0] + b[0], a[1] + b[1]


def ml_head_tasks(m):
    a = head_tasks(m.hm[:, :, C2_MLQ:C2_MLK], MLH, m.mqT)
    b = head_tasks(m.hm[:, :, C2_MLK:C2_MLV], MLH, m.mkT)
    return a[0] + b[0], a[1] + b[1]


def ml_tiles(dir, i):
    return (i, T) if dir == 0 else (0, i + 1)


def pe_mlstm(E):
    K, m, pe = E.K, E.K.second, E.eng
    n0 = E.n
    pe_transposes(E, ml_head_tasks(m)[0])
    pe.wait_ge(K.ml_gates, 1)
    n = E.take()
    E.wait_bank(n)
    lf = m.small[:, 0]
    for t in range(T):
        for dir in range(2):
            others = [u for u in range(T) if (u < t if dir == 0 else u > t)]
            for i, u in enumerate([t] + others):
                mm = pe.matmul(E.bank(n)[:, 8 * t + 4 * dir:8 * t + 4 * dir + 4], (K.upto, K.since)[dir] if u == t else K.ones,
                               lf[:, u, 4 * dir:4 * dir + 4], start=(i == 0), stop=(i == len(others)))
    E.filled(mm, n)
    pe.wait_ge(K.ml_gates, 2)
    a = m.small[:, 3]
    pe_transposes(E, [[a[:, t, 4 * dir:4 * dir + 4] for t in range(T)] for dir in range(2)])
    pe.wait_ge(K.ml_gates, 3)
    n = E.take()
    E.wait_bank(n)
    for dir in range(2):
        for t in range(T):
            tr = pe.transpose(E.bank(n)[:, 16 * dir + 4 * t:16 * dir + 4 * t + 4], m.rows[0:4, dir, P * t:P * t + P], K.ident[0:4, 0:4])
    E.filled(tr, n)
    E.wait_evacuated(n0, n0 + 2 * MLH)
    for h in range(MLH):
        for i in range(T):
            n = E.take()
            E.wait_bank(n)
            E.filled(pe.matmul(E.bank(n), m.mkT[:, h, P * i:P * i + P], m.mqT[:, h, :], start=True, stop=True), n)
        for dir in range(2):
            n = E.take()
            E.wait_bank(n)
            E.filled(pe.matmul(E.bank(n), K.ident[0:4, h:h + 1].to_broadcast([4, P]), m.rows[0:4, dir, :],
                               start=True, stop=True), n)
        for dir in range(2):
            pe.wait_ge(K.ml_weights, 2 * h + dir + 1)
            n = E.take()
            E.wait_bank(n)
            for t in range(T):
                keys = [i for i in range(T) if ml_tiles(dir, i)[0] <= t < ml_tiles(dir, i)[1]]
                for i in keys:
                    mm = pe.matmul(E.bank(n)[:, (HD + 1) * t:(HD + 1) * (t + 1)], m.W[:, dir, i, P * t:P * t + P], m.v1[:, i, h, :],
                                   start=(i == keys[0]), stop=(i == keys[-1]))
            E.filled(mm, n)


def act_mlstm(E):
    K, m, s = E.K, E.K.second, E.eng
    copy_out(E, ml_head_tasks(m)[1])
    sm = lambda i: m.small[:, i, :, 0:8]
    s.wait_ge(K.ml_dve, 1)
    s.activation(sm(1), sm(1), ACT.Exp, scale=-1.0).then_inc(K.ml_act, 1)
    s.wait_ge(K.ml_dve, 2)
    s.activation(sm(5), sm(2), ACT.Ln).then_inc(K.ml_act, 1)
    s.wait_ge(K.ml_dve, 3)
    s.activation(sm(6), sm(6), ACT.Exp, scale=-1.0).then_inc(K.ml_act, 1)
    s.activation(m.ex, m.hm[:, :, C2_MLO:C2_MLI], ACT.Exp, scale=-1.0).then_inc(K.ml_act, 1)
    E.n += 4
    for h in range(MLH):
        if h:
            E.wait_filled(E.n - 1)
        for i in range(T):
            n = E.take()
            E.wait_filled(n)
            if h and i == 0:
                s.wait_ge(K.ml_weights, 2 * h)
            E.evacuated(s.activation(m.ST[:, i, :], E.bank(n), ACT.Copy, scale=HD ** -0.5), n)
        E.n += 2
        for dir in range(2):
            s.wait_ge(K.ml_exponents, 2 * h + dir + 1)
            for i in range(T):
                lo, hi = ml_tiles(dir, i)
                ins = s.activation(m.W[:, dir, i, P * lo:P * hi], m.Dm[:, dir, i, P * lo:P * hi], ACT.Exp, scale=-1.0)
            ins.then_inc(K.ml_exps, 1)
        E.n += 2


def dve_mlstm(E):
    K, m, v = E.K, E.K.second, E.eng
    L = E.link
    copy_out(E, ml_head_tasks(m)[1])
    sm = lambda i: m.small[:, i, :, 0:8]
    pi, pf = m.par[:, 0:8], m.par[:, 8:16]
    lf, e, u, a, F, ln, fl, igc = (sm(i) for i in range(8))
    for t in range(T):
        v.tensor_tensor(igc[:, t], m.hm[:, t, C2_MLI:C2_MLF], pi, ALU.add)
        ins = v.tensor_tensor(lf[:, t], m.hm[:, t, C2_MLF:C2_MLE], pf, ALU.add)
    L(ins)
    v.scalar_tensor_tensor(e, lf, -1.0, lf, ALU.mult, ALU.max).then_inc(K.ml_dve, 1)
    v.wait_ge(K.ml_act, 1)
    v.tensor_scalar(u, e, 1.0, None, ALU.add).then_inc(K.ml_dve, 1)
    v.wait_ge(K.ml_dve, 2)
    v.wait_ge(K.ml_act, 2)
    dve_log1p_end(E, ln, ln, u, e, e)
    v.scalar_tensor_tensor(lf, lf, 0.0, ln, ALU.min, ALU.subtract).then_inc(K.ml_gates, 1)
    L(v.memset(m.v1, 1.0))
    for h in range(MLH):
        v.tensor_copy(m.v1[:, :, h, 0:HD], m.hm[:, :, C2_MLV + HD * h:C2_MLV + HD * h + HD])
    L(v.memset(m.zrow, 0.0))
    n = E.take()
    E.wait_filled(n)
    E.evacuated(v.tensor_copy(F, E.bank(n)[:, 0:32].rearrange("p (t c) -> p t c", t=T)), n)
    E.wait_evacuated(n, n + 1)
    v.tensor_tensor(a, igc, F, ALU.subtract).then_inc(K.ml_gates, 1)
    v.wait_ge(K.ml_gates, 2)
    for dir in range(2):
        n = E.take()
        E.wait_filled(n)
        E.evacuated(v.tensor_copy(m.rows[0:4, dir, :], E.bank(n)[0:4, :]), n)
    E.wait_evacuated(n - 1, n + 1)
    L(v.tensor_tensor_scan(m.rows[0:4, 0, :], m.rows[0:4, 0, :], m.zrow[0:4, :], 0.0, ALU.max, ALU.max))
    v.tensor_tensor_scan(m.rows[0:4, 1, ::-1], m.rows[0:4, 1, ::-1], m.zrow[0:4, :], 0.0, ALU.max, ALU.max).then_inc(K.ml_gates, 1)
    n = E.take()
    E.wait_filled(n)
    for dir in range(2):
        ins = v.tensor_tensor(fl[:, :, 4 * dir:4 * dir + 4], F[:, :, 4 * dir:4 * dir + 4],
                              E.bank(n)[:, 16 * dir:16 * dir + 16].rearrange("p (t c) -> p t c", t=T), ALU.add)
    E.evacuated(ins, n)
    E.wait_evacuated(n, n + 1)
    v.nop().then_inc(K.ml_dve, 1)
    for h in range(MLH):
        n0 = E.n
        E.n += T
        for dir in range(2):
            n = E.take()
            E.wait_filled(n)
            for i in range(T):
                lo, hi = ml_tiles(dir, i)
                ins = v.tensor_scalar(m.Dm[:, dir, i, P * lo:P * hi], E.bank(n)[:, P * lo:P * hi],
                                      m.small[:, 3, i, 4 * dir + h:4 * dir + h + 1], 0.0, ALU.subtract, ALU.max)
                if i == T - 1:
                    E.evacuated(ins, n)
            E.wait_evacuated(n, n + 1)
            v.nop().then_inc(K.ml_exponents, 1)
        E.wait_evacuated(n0, n0 + T)
        for dir in range(2):
            v.wait_ge(K.ml_exps, 2 * h + dir + 1)
            for i in range(T):
                d = m.W[:, dir, i, P * i:P * i + P]
                ins = v.tensor_tensor(d, d, (K.upto, K.since)[dir], ALU.mult)
            L(ins)
            for i in range(T):
                lo, hi = ml_tiles(dir, i)
                w = m.W[:, dir, i, P * lo:P * hi]
                ins = v.tensor_tensor(w, w, m.ST[:, i, P * lo:P * hi], ALU.mult)
            ins.then_inc(K.ml_weights, 1)
        if h == 0:
            v.wait_ge(K.ml_act, 4)
        for dir in range(2):
            n = E.take()
            E.wait_filled(n)
            b = E.bank(n)[:, 0:T * (HD + 1)].rearrange("p (t d) -> p t d", t=T)
            dn = m.gates[:, 2 * dir, :]
            rn = m.gates[:, 2 * dir + 1, :]
            L(v.tensor_copy(dn, b[:, :, HD]))
            L(v.scalar_tensor_tensor(dn, dn, -1.0, dn, ALU.mult, ALU.max))
            L(v.tensor_tensor(dn, dn, m.small[:, 6, :, 4 * dir + h], ALU.max))
            L(v.reciprocal(rn, dn))
            out = m.hs[:, :, HD * h:HD * h + HD] if dir == 0 else m.norm[:, 0, :, 0:HD]
            E.evacuated(v.tensor_tensor(out, b[:, :, 0:HD], rn.unsqueeze(2).to_broadcast([P, T, HD]), ALU.mult), n)
        E.wait_evacuated(n - 1, n + 1)
        L(v.tensor_tensor(m.hs[:, :, HD * h:HD * h + HD], m.hs[:, :, HD * h:HD * h + HD], m.norm[:, 0, :, 0:HD], ALU.add))
    dve_head_norm(E, m.hs, m.hsq, m.gates, MLH)
    v.wait_ge(K.nw_loaded, 16)
    L(v.tensor_scalar(m.ex, m.ex, 1.0, None, ALU.add))
    L(v.reciprocal(m.ex, m.ex))
    for t in range(T):
        ins = v.tensor_tensor(m.hs[:, t], m.hs[:, t], m.nw[:, 0:256], ALU.mult)
    L(ins)
    L(v.tensor_tensor(m.mix[:, :, NAH * HD:NAH * HD + 256], m.hs, m.ex, ALU.mult))


def dve_head_norm(E, x, sq, cols, heads):
    v = E.eng
    x4 = x.rearrange("p t (h d) -> p t h d", h=heads)
    c = cols[:, 4:4 + heads, :].rearrange("p h t -> p t h")
    E.link(v.tensor_tensor(sq, x, x, ALU.mult))
    for h in range(heads):
        ins = v.reduce_sum(cols[:, 4 + h, :], sq[:, :, HD * h:HD * h + HD], AX)
    E.link(ins)
    E.link(v.tensor_scalar(cols[:, 10:10 + heads, :], cols[:, 4:4 + heads, :], 1.0 / HD, EPS, ALU.mult, ALU.add))
    dve_rsqrt(E, cols[:, 4:4 + heads, :], cols[:, 10:10 + heads, :], cols[:, 16:16 + heads, :])
    for t in range(T):
        ins = v.tensor_tensor(x4[:, t], x4[:, t], c[:, t].unsqueeze(2).to_broadcast([P, heads, HD]), ALU.mult)
    E.link(ins)



GROUPS = [(dir, half) for dir in range(2) for half in range(2)]


def chunk(dir, step):
    return step if dir == 0 else T - 1 - step


def pe_gdn(E):
    K, m, pe = E.K, E.K.second, E.eng
    pe_linear(E, K.xT, [C2_ZE])
    for width in (512, 512, 128):
        w = pe_weights(E).rearrange("p (k n) -> p k n", k=KD)
        for c in range(width // P):
            n = E.take()
            E.wait_bank(n)
            for k in range(KD):
                mm = pe.matmul(E.bank(n), w[:, k, P * c:P * c + P], K.xT[:, k, :], start=(k == 0), stop=(k == KD - 1))
            E.filled(mm, n)
        pe.drain().then_inc(K.w_used, 1)
    for c in range(GCT):
        pe.wait_ge(K.conv_done, c + 1)
        pe_transposes(E, [[m.cout[:, c, P * t:P * t + P] for t in range(T)]])
    pe.wait_ge(K.gd_gates, 1)
    n = E.take()
    E.wait_bank(n)
    g = m.small[:, 0]
    for dir in range(2):
        for t in range(T):
            pe.matmul(E.bank(n)[:, 12 * t + 6 * dir:12 * t + 6 * dir + 6], (K.upto, K.since)[dir], g[:, t, 6 * dir:6 * dir + 6],
                      start=True, stop=True)
    for t in range(T):
        mm = pe.matmul(E.bank(n)[:, 48 + 12 * t:60 + 12 * t], K.ones, g[:, t, :], start=True, stop=True)
    E.filled(mm, n)
    E.phase()
    n0 = E.n
    pe.wait_ge(K.gd_normed, 1)
    pe_transposes(E, head_tasks(m.tm[:, :, 0:384], GDH, m.gqT)[0])
    pe_transposes(E, head_tasks(m.tm[:, :, 384:768], GDH, m.gkT)[0])
    E.wait_evacuated(n0, E.n)

    def each(body):
        for gi, (dir, half) in enumerate(GROUPS):
            n = E.take()
            E.wait_bank(n)
            for u in range(3):
                mm = body(E.bank(n), gi, dir, 3 * half + u, u)
            E.filled(mm, n)

    cols = lambda u: slice(P * u, P * u + P)
    for step in range(T):
        tk = lambda dir: slice(P * chunk(dir, step), P * chunk(dir, step) + P)
        g = lambda dir, h: m.small[:, 0, chunk(dir, step), 6 * dir + h:6 * dir + h + 1].to_broadcast([P, P])
        b = lambda dir, h: m.small[:, 1, chunk(dir, step), 6 * dir + h:6 * dir + h + 1].to_broadcast([P, P])
        each(lambda ps, gi, dir, h, u: pe.matmul(ps[:, cols(u)], g(dir, h), (K.upto, K.since)[dir], start=True, stop=True))
        each(lambda ps, gi, dir, h, u: pe.matmul(ps[:, cols(u)], m.gkT[:, h, tk(dir)], m.gkT[:, h, tk(dir)], start=True, stop=True))
        each(lambda ps, gi, dir, h, u: pe.matmul(ps[:, cols(u)], b(dir, h), K.ident, start=True, stop=True))
        each(lambda ps, gi, dir, h, u: pe.matmul(ps[:, cols(u)], m.gkT[:, h, tk(dir)], m.gqT[:, h, tk(dir)], start=True, stop=True))
        for level in range(LEVELS):
            for gi in range(4):
                n = E.take()
                E.wait_bank(n)
                pe.wait_ge(K.level_masked, (step * LEVELS + level) * 4 + gi + 1)
                for u in range(3):
                    if level == 0:
                        mm = pe.transpose(E.bank(n)[:, cols(u)], m.X[:, gi, u, :], K.ident)
                    else:
                        mm = pe.matmul(E.bank(n)[:, cols(u)], m.X[:, gi, u, :], m.Ti[:, gi, u, :], start=True, stop=True)
                E.filled(mm, n)
            if level == 0:
                E.wait_evacuated(E.n - 4, E.n)
                continue
            for gi in range(4):
                E.wait_evacuated(E.n - 4 - gi * (1 if level == LEVELS - 1 else 2) + gi, E.n - 3 - gi * (1 if level == LEVELS - 1 else 2) + gi)
                for turned in ((True,) if level == LEVELS - 1 else (True, False)):
                    n = E.take()
                    E.wait_bank(n)
                    for u in range(3):
                        if turned:
                            mm = pe.matmul(E.bank(n)[:, cols(u)], m.X[:, gi, u, :], m.TiT[:, gi, u, :], start=True, stop=True)
                        else:
                            mm = pe.matmul(E.bank(n)[:, cols(u)], m.TiT[:, gi, u, :], m.X[:, gi, u, :], start=True, stop=True)
                    E.filled(mm, n)
            E.wait_evacuated(E.n - (4 if level == LEVELS - 1 else 8), E.n)
        pe.wait_ge(K.gd_operands, step + 1)
        each(lambda ps, gi, dir, h, u: pe.matmul(ps[0:HD, cols(u)], m.kbe[:, gi, u, :], m.TiT[:, gi, u, :], start=True, stop=True))
        E.wait_evacuated(E.n - 4, E.n)

        def new_values(ps, gi, dir, h, u):
            mm = pe.matmul(ps[:, HD * u:HD * u + HD], m.TiT[:, gi, u, :], m.vb[:, gi, u, :], start=True, stop=(step == 0))
            if step:
                mm = pe.matmul(ps[:, HD * u:HD * u + HD], m.nw_T[:, gi, u, :], m.state[:, 6 * dir + h, :], start=False, stop=True)
            return mm
        each(new_values)
        E.wait_evacuated(E.n - 4, E.n)

        def outputs(ps, gi, dir, h, u):
            mm = pe.matmul(ps[:, HD * u:HD * u + HD], m.at[:, gi, u, :], m.vn[:, gi, u, :], start=True, stop=(step == 0))
            if step:
                mm = pe.matmul(ps[:, HD * u:HD * u + HD], m.qd[:, gi, u, :], m.state[:, 6 * dir + h, :], start=False, stop=True)
            return mm
        each(outputs)
        if step < T - 1:
            each(lambda ps, gi, dir, h, u: pe.matmul(ps[0:HD, HD * u:HD * u + HD], m.ks[:, gi, u, :], m.vn[:, gi, u, :], start=True, stop=True))
            E.wait_evacuated(E.n - 8, E.n)


def act_gdn(E):
    K, m, s = E.K, E.K.second, E.eng
    n0 = E.n
    copy_out(E, linear_out(m.hz, [C2_ZE]))
    E.wait_evacuated(n0, E.n)
    for c in range(GCT):
        copy_out(E, [(m.cin[:, c, 2:S + 2], lambda b: b, "act")])
    sm = lambda i: m.small[:, i]
    s.wait_ge(K.gd_dve, 1)
    s.activation(sm(2), sm(2), ACT.Exp, scale=-1.0)
    s.activation(sm(1), m.hz[:, :, C2_B:C2_A], ACT.Exp, scale=-1.0)
    s.activation(m.par[:, 16:28], m.par[:, 16:28], ACT.Exp).then_inc(K.gd_act, 1)
    for c in range(GCT):
        s.wait_ge(K.conv_sums, c + 1)
        s.activation(m.cout[:, c, :], m.cout[:, c, :], ACT.Silu).then_inc(K.conv_done, 1)
    s.wait_ge(K.gd_dve, 2)
    s.activation(sm(4), sm(3), ACT.Ln).then_inc(K.gd_act, 1)
    copy_out(E, [(m.tm[:, :, P * c:P * c + P], lambda b: b.rearrange("p (t c) -> p t c", t=T), turn(c)) for c in range(GCT)])
    E.n += 1
    s.wait_ge(K.gd_dve, 3)
    s.activation(sm(6), sm(5), ACT.Exp)
    s.activation(sm(8), sm(7), ACT.Exp)
    s.activation(sm(10), sm(9), ACT.Exp).then_inc(K.gd_act, 1)
    E.phase()
    copy_out(E, head_tasks(m.tm[:, :, 0:384], GDH, m.gqT)[1])
    copy_out(E, head_tasks(m.tm[:, :, 384:768], GDH, m.gkT)[1])
    for step in range(T):
        for gi in range(4):
            n = E.take()
            s.wait_ge(K.gd_exponents, 4 * step + gi + 1)
            s.activation(m.qd[:, gi].rearrange("p u l -> p (u l)"), E.bank(n)[0:HD, 0:3 * P], ACT.Exp)
            E.evacuated(s.activation(m.E[:, gi], m.E[:, gi], ACT.Exp), n)
        E.n += 12
        for level in range(LEVELS):
            if level == 0:
                E.n += 4
                continue
            for gi in range(4):
                n = E.take()
                E.wait_filled(n)
                E.evacuated(s.activation(m.X[:, gi].rearrange("p u l -> p (u l)"), E.bank(n)[:, 0:3 * P], ACT.Copy), n)
            E.n += 4 if level == LEVELS - 1 else 8
        for gi in range(4):
            n = E.take()
            E.wait_filled(n)
            E.evacuated(s.activation(m.nw_T[:, gi].rearrange("p u l -> p (u l)"), E.bank(n)[0:HD, 0:3 * P], ACT.Copy, scale=-1.0), n)
        E.n += 8 if step == T - 1 else 12
    E.wait_evacuated(E.n - 4, E.n)
    s.activation(m.ez, m.hz[:, :, 0:384], ACT.Silu).then_inc(K.z_gate, 1)


def dve_gdn(E):
    K, m, v = E.K, E.K.second, E.eng
    L = E.link
    n0 = E.n
    copy_out(E, linear_out(m.hz, [C2_ZE]))
    E.wait_evacuated(n0, E.n)
    v.wait_ge(K.gd_loaded, 16 * K.GD_DMAS)
    v.memset(m.cin[:, :, 0:2], 0.0)
    L(v.memset(m.cin[:, :, S + 2:S + 4], 0.0))
    n0 = E.n
    E.n += GCT
    sm = lambda i: m.small[:, i]
    al = m.hz[:, :, C2_A:C2_ZE]
    for t in range(T):
        ins = v.tensor_tensor(sm(11)[:, t], al[:, t], m.par[:, 28:40], ALU.add)
    L(ins)
    v.scalar_tensor_tensor(sm(2), sm(11), -1.0, sm(11), ALU.mult, ALU.max).then_inc(K.gd_dve, 1)
    for c in range(GCT):
        E.wait_evacuated(n0 + c, n0 + c + 1)
        L(v.tensor_scalar(m.cout[:, c, :], m.cin[:, c, 0:S], m.cw[:, c, 0:1], None, ALU.mult))
        for k in range(1, 5):
            L(v.scalar_tensor_tensor(m.cout[:, c, :], m.cin[:, c, k:S + k], m.cw[:, c, k:k + 1], m.cout[:, c, :], ALU.mult, ALU.add))
        v.nop().then_inc(K.conv_sums, 1)
    v.wait_ge(K.gd_act, 1)
    L(v.tensor_scalar(sm(1), sm(1), 1.0, None, ALU.add))
    L(v.reciprocal(sm(1), sm(1)))
    v.tensor_scalar(sm(3), sm(2), 1.0, None, ALU.add).then_inc(K.gd_dve, 1)
    v.wait_ge(K.gd_dve, 2)
    v.wait_ge(K.gd_act, 2)
    dve_log1p_end(E, sm(4), sm(4), sm(3), sm(2), sm(2))
    L(v.scalar_tensor_tensor(sm(4), sm(11), 0.0, sm(4), ALU.max, ALU.add))
    for t in range(T):
        ins = v.scalar_tensor_tensor(sm(0)[:, t], sm(4)[:, t], -1.0, m.par[:, 16:28], ALU.mult, ALU.mult)
    L(ins)
    v.nop().then_inc(K.gd_gates, 1)
    n1 = E.n
    copy_out(E, [(m.tm[:, :, P * c:P * c + P], lambda b: b.rearrange("p (t c) -> p t c", t=T), turn(c)) for c in range(GCT)])
    n = E.take()
    E.wait_filled(n)
    v.tensor_copy(sm(9), E.bank(n)[:, 48:96].rearrange("p (t c) -> p t c", t=T))
    E.evacuated(v.tensor_copy(sm(5), E.bank(n)[:, 0:48].rearrange("p (t c) -> p t c", t=T)), n)
    E.wait_evacuated(n, n + 1)
    L(v.tensor_tensor(sm(7), sm(9), sm(5), ALU.subtract))
    v.nop().then_inc(K.gd_dve, 1)
    E.wait_evacuated(n1, E.n)
    L(v.tensor_tensor(m.gtmp[:, :, 0:768], m.tm[:, :, 0:768], m.tm[:, :, 0:768], ALU.mult))
    for i in range(12):
        ins = v.reduce_sum(m.gates[:, i, :], m.gtmp[:, :, HD * i:HD * i + HD], AX)
    L(ins)
    L(v.tensor_scalar(m.gates[:, 12:24, :], m.gates[:, 0:12, :], EPS, None, ALU.add))
    dve_rsqrt(E, m.gates[:, 0:12, :], m.gates[:, 12:24, :], m.gates[:, 24:36, :])
    L(v.tensor_scalar(m.gates[:, 0:6, :], m.gates[:, 0:6, :], HD ** -0.5, None, ALU.mult))
    c = m.gates[:, 0:12, :].rearrange("p h t -> p t h")
    for t in range(T):
        x4 = m.tm[:, t, 0:768].rearrange("p (h d) -> p h d", h=12)
        ins = v.tensor_tensor(x4, x4, c[:, t].unsqueeze(2).to_broadcast([P, 12, HD]), ALU.mult)
    L(ins)
    v.wait_ge(K.gd_act, 3)
    L(v.tensor_tensor(sm(12), sm(1), sm(6), ALU.mult))
    E.phase()
    v.nop().then_inc(K.gd_normed, 1)
    L(v.memset(m.o, 0.0))
    copy_out(E, head_tasks(m.tm[:, :, 0:384], GDH, m.gqT)[1])
    copy_out(E, head_tasks(m.tm[:, :, 384:768], GDH, m.gkT)[1])
    E.wait_evacuated(E.n - 12, E.n)
    incl = (K.upto, K.since)
    bc3 = lambda ap: ap.unsqueeze(1).to_broadcast([P, 3, P])
    v3 = lambda b: b[:, 0:3 * P].rearrange("p (u l) -> p u l", u=3)
    for step in range(T):
        rows = E.n
        for gi, (dir, half) in enumerate(GROUPS):
            n = E.take()
            E.wait_filled(n)
            for u in range(3):
                col = m.small[:, 5, chunk(dir, step), 6 * dir + 3 * half + u:6 * dir + 3 * half + u + 1]
                ins = v.tensor_scalar(m.E[:, gi, u, :], E.bank(n)[:, P * u:P * u + P], col, 0.0, ALU.subtract, ALU.min)
            ins.then_inc(K.gd_exponents, 1)
        for gi, (dir, half) in enumerate(GROUPS):
            E.wait_evacuated(rows + gi, rows + gi + 1)
            c = chunk(dir, step)
            h0 = 3 * half
            wide = lambda i: m.small[:, i, c, 6 * dir + h0:6 * dir + h0 + 3].unsqueeze(2).to_broadcast([P, 3, HD])
            k3 = m.tm[:, c, 384 + HD * h0:384 + HD * h0 + 192].rearrange("p (u d) -> p u d", u=3)
            x3 = m.tm[:, c, 768 + HD * h0:768 + HD * h0 + 192].rearrange("p (u d) -> p u d", u=3)
            v.tensor_tensor(m.vb[:, gi], x3, wide(1), ALU.mult)
            v.tensor_tensor(m.kbe[:, gi], k3, wide(12), ALU.mult)
            v.tensor_tensor(m.ks[:, gi], k3, wide(8), ALU.mult)
            q3 = m.gqT[:, h0:h0 + 3, P * c:P * c + P]
            v.tensor_tensor(m.qd[:, gi], m.qd[:, gi], q3, ALU.mult)
            ins = v.tensor_tensor(m.E[:, gi], m.E[:, gi], bc3(incl[dir]), ALU.mult)
        L(ins)
        v.nop().then_inc(K.gd_operands, 1)
        n0 = E.n
        for gi in range(4):
            n = E.take()
            E.wait_filled(n)
            E.evacuated(v.tensor_tensor(m.AT[:, gi], v3(E.bank(n)), m.E[:, gi], ALU.mult), n)
        E.wait_evacuated(n0, E.n)
        n0 = E.n
        for gi in range(4):
            n = E.take()
            E.wait_filled(n)
            E.evacuated(v.tensor_tensor(m.AT[:, gi], v3(E.bank(n)), m.AT[:, gi], ALU.mult), n)
        E.wait_evacuated(n0, E.n)
        for gi in range(4):
            n = E.take()
            E.wait_filled(n)
            E.evacuated(v.tensor_tensor(m.at[:, gi], v3(E.bank(n)), m.E[:, gi], ALU.mult), n)
        for level in range(LEVELS):
            for gi, (dir, half) in enumerate(GROUPS):
                v.tensor_tensor(m.X[:, gi], m.AT[:, gi], bc3(m.levels[:, dir, level, :]), ALU.mult).then_inc(K.level_masked, 1)
            if level == 0:
                v.wait_ge(K.level_masked, (step * LEVELS + level) * 4 + 4)
                for gi in range(4):
                    ins = v.scalar_tensor_tensor(m.TiT[:, gi], m.X[:, gi], -1.0, bc3(K.ident), ALU.mult, ALU.add)
                L(ins)
                for gi in range(4):
                    n = E.take()
                    E.wait_filled(n)
                    E.evacuated(v.scalar_tensor_tensor(m.Ti[:, gi], v3(E.bank(n)), -1.0, bc3(K.ident), ALU.mult, ALU.add), n)
                E.wait_evacuated(E.n - 4, E.n)
                continue
            E.n += 4
            last = level == LEVELS - 1
            n0 = E.n
            for gi in range(4):
                n = E.take()
                if not last:
                    E.wait_filled(n + 1)
                else:
                    E.wait_filled(n)
                E.evacuated(v.tensor_tensor(m.TiT[:, gi], m.TiT[:, gi], v3(E.bank(n)), ALU.subtract), n)
                if not last:
                    n = E.take()
                    E.evacuated(v.tensor_tensor(m.Ti[:, gi], m.Ti[:, gi], v3(E.bank(n)), ALU.subtract), n)
            E.wait_evacuated(n0, E.n)
        E.n += 4
        w3 = lambda b: b[:, 0:3 * HD].rearrange("p (u d) -> p u d", u=3)
        for gi in range(4):
            n = E.take()
            E.wait_filled(n)
            E.evacuated(v.tensor_copy(m.vn[:, gi], w3(E.bank(n))), n)
        for gi, (dir, half) in enumerate(GROUPS):
            n = E.take()
            E.wait_filled(n)
            o3 = m.o[:, chunk(dir, step), 192 * half:192 * half + 192].rearrange("p (u d) -> p u d", u=3)
            E.evacuated(v.tensor_tensor(o3, o3, w3(E.bank(n)), ALU.add), n)
        E.wait_evacuated(E.n - 4, E.n)
        if step < T - 1:
            for gi, (dir, half) in enumerate(GROUPS):
                n = E.take()
                E.wait_filled(n)
                for u in range(3):
                    h = 6 * dir + 3 * half + u
                    src, st = E.bank(n)[0:HD, HD * u:HD * u + HD], m.state[:, h, :]
                    if step == 0:
                        ins = v.tensor_copy(st, src)
                    else:
                        ins = v.scalar_tensor_tensor(st, st, m.small[0:HD, 10, chunk(dir, step), h:h + 1], src, ALU.mult, ALU.add)
                E.evacuated(ins, n)
            E.wait_evacuated(E.n - 4, E.n)
    dve_head_norm(E, m.o, m.osq, m.gates, GDH)
    v.wait_ge(K.nw_loaded, 32)
    for t in range(T):
        ins = v.tensor_tensor(m.o[:, t], m.o[:, t], m.nw, ALU.mult)
    L(ins)
    v.wait_ge(K.z_gate, 1)
    L(v.tensor_tensor(m.mix[:, :, 640:1024], m.o, m.ez, ALU.mult))


def pe_second(E):
    K, m, pe = E.K, E.K.second, E.eng
    pe.wait_ge(K.norm_done, 5)
    n0 = E.n
    pe_transposes(E, xt_tasks(m.mix))
    E.wait_evacuated(n0, E.n)
    pe_linear(E, K.xT, NEAR_WIDTHS)
    E.phase()
    n0 = E.n
    pe_transposes(E, second_head_tasks(m)[0])
    E.wait_evacuated(n0, E.n)
    pe_attention(E, K.near)
    E.phase()
    pe_linear(E, K.xT, ML_WIDTHS)
    E.phase()
    pe_mlstm(E)
    E.phase()
    pe_gdn(E)
    E.phase()
    n0 = E.n
    pe_transposes(E, xt_tasks(m.mix))
    E.wait_evacuated(n0, E.n)
    pe_linear(E, K.xT, [512] * 2)
    E.phase()


def act_second(E):
    K, m = E.K, E.K.second
    copy_out(E, xt_out(K.xT))
    copy_out(E, linear_out(m.h, NEAR_WIDTHS))
    E.wait_evacuated(E.n - 8, E.n)
    E.phase()
    copy_out(E, second_head_tasks(m)[1])
    act_attention(E, K.near)
    E.phase()
    copy_out(E, linear_out(m.hm, ML_WIDTHS))
    E.wait_evacuated(E.n - 8, E.n)
    E.phase()
    act_mlstm(E)
    E.phase()
    act_gdn(E)
    E.phase()
    copy_out(E, xt_out(K.xT))
    residual_out(E, K.x, 2, 1.0)
    E.phase()


def dve_second(E):
    K, m, v = E.K, E.K.second, E.eng
    v.wait_ge(K.gains_loaded, 16 * 9)
    dve_rms_norm(E, m.mix, K.x, K.gains[:, 0, :], T)
    v.drain().then_inc(K.norm_done, 1)
    copy_out(E, xt_out(K.xT))
    v.wait_ge(K.bias_loaded, 16 * (2 * NAH + 1))
    E.link(v.tensor_scalar(m.far, m.near, -NEG, NEG, ALU.mult, ALU.add))
    b = m.bias.rearrange("p h r c -> p (h r) c")
    wide = lambda ap: ap.unsqueeze(1).to_broadcast([P, NAH * 14, HD])
    E.link(v.tensor_tensor(b, b, wide(m.near), ALU.mult))
    E.link(v.tensor_tensor(b, b, wide(m.far), ALU.add))
    copy_out(E, linear_out(m.h, NEAR_WIDTHS))
    E.wait_evacuated(E.n - 8, E.n)
    E.phase()
    copy_out(E, second_head_tasks(m)[1])
    dve_attention(E, K.near)
    E.phase()
    copy_out(E, linear_out(m.hm, ML_WIDTHS))
    E.wait_evacuated(E.n - 8, E.n)
    E.phase()
    dve_mlstm(E)
    E.phase()
    dve_gdn(E)
    E.phase()
    copy_out(E, xt_out(K.xT))
    residual_out(E, K.x, 2, 1.0)
    E.wait_evacuated(E.n - 8, E.n)
    E.phase()


def pool_second(E):
    K, m, g, d = E.K, E.K.second, E.eng, E.K.d
    load_gains(E, d.norm_mix_w_2)
    g.dma_start(m.near, d.c_near).then_inc(K.bias_loaded, 16)
    for lo, src in ((0, d.ml_i_bias_2), (8, d.ml_f_bias_2), (16, d.gdn_a_log_2), (28, d.gdn_dt_bias_2)):
        n = src.shape[1] * src.shape[2]
        g.dma_start(m.par[:, lo:lo + n], src.rearrange("a b h -> a (b h)").to_broadcast([P, n])).then_inc(K.par_loaded, 16)
    rows, pad = NAH * 15, 2 * HD - 1
    stage = m.s.rearrange("p a t c -> p (a t c)")[0:rows, 0:pad]
    g.memset(stage, 0.0).then_inc(K.stage_zero, 1)
    g.wait_ge(K.stage_zero, 1)
    g.dma_start(stage[:, HD - 16:HD + 15], d.na_rel_bias_2.rearrange("a h r c -> (a h r) c")).then_inc(K.stage_filled, 16)
    g.wait_ge(K.stage_filled, 16)
    g.dma_start(K.bias_dram, stage.unsqueeze(1).to_broadcast([rows, HD, pad])).then_inc(K.stage_stored, 16)
    g.wait_ge(K.stage_stored, 16)
    for h in range(NAH):
        for a in range(2):
            src = bass.AP(tensor=K.bias_dram.tensor, offset=(15 * h + 1 - a) * HD * pad + HD - 1,
                          ap=[[pad - 1, HD], [HD * pad, 14], [1, HD]])
            g.dma_start(m.bias[HD * a:HD * a + HD, h], src).then_inc(K.bias_loaded, 16)
    g.wait_ge(K.par_loaded, 16 * 4)
    E.phase()
    E.phase()
    E.phase()
    g.dma_start(m.nw[:, 0:MLH * HD], d.ml_norm_w_2.to_broadcast([P, MLH * HD])).then_inc(K.nw_loaded, 16)
    E.phase()
    g.dma_start(m.nw, d.gdn_norm_w_2.to_broadcast([P, GDH * HD])).then_inc(K.nw_loaded, 16)
    for dir in range(2):
        g.dma_start(m.levels[:, dir], (d.c_levels_up, d.c_levels_down)[dir]).then_inc(K.gd_loaded, 16)
    for c in range(GCT):
        g.dma_start(m.cw[:, c, :], d.gdn_conv_w_2[0, :, P * c:P * c + P].rearrange("k p -> p k"),
                    allow_slow_non_contiguous=True).then_inc(K.gd_loaded, 16)
    E.phase()
    E.phase()
    E.phase()


def pe_feature_major(E, xT, tokens, tiles):
    for _ in range(tiles):
        w = pe_weights(E).rearrange("p (k n) -> p k n", k=KD)
        for c in range(WT // P):
            n = E.take()
            E.wait_bank(n)
            for k in range(KD):
                mm = E.eng.matmul(E.bank(n)[:, 0:tokens], w[:, k, P * c:P * c + P], xT[:, k, :], start=(k == 0), stop=(k == KD - 1))
            E.filled(mm, n)
        E.eng.drain().then_inc(E.K.w_used, 1)


def cross_copies(m):
    kT = [(m.kT[:, c, :], lambda b: b[:, 0:MEMN], turn(c)) for c in range(KD)]
    v = [(m.v[:, t, WT * h:WT * h + WT], lambda b: b, turn(t)) for h in range(2) for t in range(2)]
    qT = [(m.qT[:, c, :], lambda b: b, turn(c)) for c in range(KD)]
    return kT, v, qT


def mem_tasks(m):
    return [[m.mem[:, t, P * k:P * k + P] for t in range(2)] for k in range(KD)]


def mem_out(m):
    return [(m.memT[:, k, :], lambda b: b[:, 0:MEMN], turn(k)) for k in range(KD)]


def pe_cross(E):
    K, m, pe = E.K, E.K.cross, E.eng
    pe.wait_ge(K.norm_done, 6)
    n0 = E.n
    pe_transposes(E, mem_tasks(m))
    E.wait_evacuated(n0, E.n)
    pe_feature_major(E, m.memT, MEMN, 2)
    pe_linear(E, m.memT, [512] * 2, tiles=2)
    pe.wait_ge(K.norm_done, 7)
    n0 = E.n
    pe_transposes(E, xt_tasks(m.hn))
    E.wait_evacuated(n0, E.n)
    pe_feature_major(E, K.xT, S, 2)
    E.wait_evacuated(E.n - 8, E.n)
    pe_attention(E, K.memory)
    E.phase()
    n0 = E.n
    pe_transposes(E, xt_tasks(m.mix))
    E.wait_evacuated(n0, E.n)
    pe_linear(E, K.xT, [512] * 2)
    E.phase()


def act_cross(E):
    K, m = E.K, E.K.cross
    kT, v, qT = cross_copies(m)
    copy_out(E, mem_out(m))
    copy_out(E, kT)
    copy_out(E, v)
    copy_out(E, xt_out(K.xT))
    copy_out(E, qT)
    act_attention(E, K.memory)
    E.phase()
    copy_out(E, xt_out(K.xT))
    residual_out(E, K.x, 2, 1.0)
    E.phase()


def dve_cross(E):
    K, m, v = E.K, E.K.cross, E.eng
    kT, vv, qT = cross_copies(m)
    v.wait_ge(K.mem_loaded, 32)
    dve_rms_norm(E, m.mem, m.mem, m.gain, MEMN // P)
    v.drain().then_inc(K.norm_done, 1)
    v.wait_ge(K.gains_loaded, 16 * 10)
    dve_rms_norm(E, m.hn, K.x, K.gains[:, 1, :], T)
    v.drain().then_inc(K.norm_done, 1)
    copy_out(E, mem_out(m))
    copy_out(E, kT)
    copy_out(E, vv)
    copy_out(E, xt_out(K.xT))
    copy_out(E, qT)
    E.wait_evacuated(E.n - 8, E.n)
    dve_attention(E, K.memory)
    E.phase()
    copy_out(E, xt_out(K.xT))
    residual_out(E, K.x, 2, 1.0)
    E.wait_evacuated(E.n - 8, E.n)
    E.phase()


def pool_cross(E):
    K, m, g, d = E.K, E.K.cross, E.eng, E.K.d
    g.dma_start(m.mem, d.mem_2[0].rearrange("(t p) d -> p t d", p=P)).then_inc(K.mem_loaded, 16)
    g.dma_start(m.gain, d.norm_mem_w_2.to_broadcast([P, D])).then_inc(K.mem_loaded, 16)
    g.dma_start(K.gains[:, 1, :], d.norm_xa_w_2.to_broadcast([P, D])).then_inc(K.gains_loaded, 16)
    E.phase()
    E.phase()


def pe_ffn(E):
    K, m, pe = E.K, E.K.ffn, E.eng
    pe.wait_ge(K.norm_done, 8)
    n0 = E.n
    pe_transposes(E, xt_tasks(m.hn))
    E.wait_evacuated(n0, E.n)
    pe_feature_major(E, K.xT, S, FF // WT)
    E.wait_evacuated(E.n - 8, E.n)
    n0 = E.n
    for i in range(8):
        E.wait_bank(E.take())
    for f in range(FF // WT):
        w = pe_weights(E).rearrange("p (k n) -> p k n", k=WT // P)
        for t in range(T):
            for half in range(2):
                for k in range(WT // P):
                    mm = pe.matmul(E.bank(n0 + 4 * half + t), m.hT[:, 4 * f + k, P * t:P * t + P], w[:, k, WT * half:WT * half + WT],
                                   start=(f == 0 and k == 0), stop=(f == FF // WT - 1 and k == WT // P - 1))
                if f == FF // WT - 1:
                    E.filled(mm, n0 + 4 * half + t)
        pe.drain().then_inc(K.w_used, 1)
    E.phase()


def act_ffn(E):
    K, m, s = E.K, E.K.ffn, E.eng
    copy_out(E, xt_out(K.xT))
    for f in range(FFT):
        n = E.take()
        if f % 2 == 0:
            E.wait_filled(n)
            E.link(s.activation(m.r[:, 0, :], E.bank(n), ACT.Relu))
            E.evacuated(s.activation(m.hT[:, f, :], m.r[:, 0, :], ACT.Square), n)
            E.wait_evacuated(n, n + 1)
    residual_out(E, K.x, 2, 1.0)
    E.phase()


def dve_ffn(E):
    K, m, v = E.K, E.K.ffn, E.eng
    v.wait_ge(K.gains_loaded, 16 * 12)
    dve_rms_norm(E, m.hn, K.x, K.gains[:, 0, :], T)
    v.drain().then_inc(K.norm_done, 1)
    copy_out(E, xt_out(K.xT))
    for f in range(FFT):
        n = E.take()
        if f % 2 == 1:
            E.wait_filled(n)
            E.link(v.tensor_scalar(m.r[:, 1, :], E.bank(n), 0.0, None, ALU.max))
            E.evacuated(v.tensor_tensor(m.hT[:, f, :], m.r[:, 1, :], m.r[:, 1, :], ALU.mult), n)
            E.wait_evacuated(n, n + 1)
    n0 = E.n
    residual_out(E, K.x, 2, 1.0)
    E.wait_evacuated(n0, E.n)
    E.phase()
    dve_rms_norm(E, m.hn, K.x, K.gains[:, 1, :], T)
    v.drain().then_inc(K.norm_done, 1)


def pool_ffn(E):
    K, m, g, d = E.K, E.K.ffn, E.eng, E.K.d
    load_gains(E, d.norm_ffn_w_2, d.norm_out_w_2.rearrange("(a n) -> a n", a=1))
    E.phase()
    g.wait_ge(K.norm_done, 9)
    g.dma_start(K.out[0].rearrange("(t p) d -> p t d", p=P), m.hn).then_inc(K.out_stored, 16)
    g.wait_ge(K.out_stored, 16)



def sp_weights(E):
    K, sp, d = E.K, E.eng, E.K.d

    def load(src, rows):
        w = E.w
        E.w += 1
        if w >= RING:
            sp.wait_ge(K.w_used, w - RING + 1)
        cols = src.shape[1]
        wide = WT if rows == KD else D
        dst = K.ring[:, w % RING, :].rearrange("p (k n) -> p k n", n=wide)[:, :, 0:cols]
        sp.dma_start(dst, src.rearrange("(k p) n -> p k n", p=P)).then_inc(K.w_loaded[w % RING], 16)

    def load_wide(mat, lo, hi):
        for c in range(lo, hi, WT):
            load(mat[:, c:min(c + WT, hi)], KD)

    def expert(layer, i, e, slot, signal):
        mat, rows = ((K.gate_rows, D), (K.up_rows, D), (K.down_rows, EH))[i]
        src = mat[layer][bass.ds(e * rows, rows), :].rearrange("(p k) n -> p (k n)", p=P)
        sp.dma_start(K.ring[:, slot, :], src).then_inc(signal, 16)

    def more(layer, i, e, ready, j=None):
        if j is not None or ready > 0:
            sp.wait_ge(K.more_used, ready if j is None else j * 3 + ready)
        mat, rows = ((K.gate_rows, D), (K.up_rows, D), (K.down_rows, EH))[i]
        src = mat[layer][bass.ds(e * rows, rows), :].rearrange("(p k) n -> p (k n)", p=P)
        sp.dma_start(K.moe.more[:, i, :], src).then_inc(K.more_loaded[i], 16)

    def experts(layer):
        w0, o0 = E.w, 3 * (NE // 2) * layer

        def even(i, c, j=None):
            w = w0 + 3 * c + i
            sp.wait_ge(K.w_used, w - RING + 1 if j is None else j * 3 + (w - RING + 1))
            expert(layer, i, 2 * c if j is None else j * 2 + 2 * c, w % RING, K.w_loaded[w % RING])

        for i in range(3):
            even(i, 0)
        sp.wait_ge(K.phase_done, 4 * (5 + 2 * layer))
        for i in range(3):
            more(layer, i, 1, o0 + i - 2)
        even(0, 1)
        even(1, 1)
        more(layer, 0, 3, o0 + 1)
        more(layer, 1, 3, o0 + 2)
        even(2, 1)
        with sp.Fori(0, NE // 2 - 2) as j:
            even(0, 2, j)
            even(1, 2, j)
            more(layer, 2, j * 2 + 3, o0 + 3, j)
            more(layer, 0, j * 2 + 5, o0 + 4, j)
            more(layer, 1, j * 2 + 5, o0 + 5, j)
            even(2, 2, j)
        more(layer, 2, NE - 1, o0 + 3 * (NE // 2 - 1))
        E.w = w0 + 3 * NE // 2
        sp.wait_ge(K.slots_ready, layer + 1)
        V = K.beyond[layer]
        jt = K.moe.jt.bitcast(I32)
        some = sp.value_load(jt[0:1, NOV + 1:NOV + 2], min_val=0, max_val=NOV)
        with sp.If(some > 0):
            sp.wait_ge(K.w_used, E.w)
            sp.wait_ge(K.more_used, 3 * NE // 2 * (layer + 1))
            first = sp.value_load(jt[0:1, 0:1], min_val=0, max_val=NE - 1)
            for i in range(3):
                expert(layer, i, first, i, V.w)
            with sp.Fori(0, NOV) as j:
                sp.wait_ge(V.pe, j * 4 + 4)
                e = sp.value_load(jt[0:1, bass.ds(j + 1, 1)], min_val=0, max_val=NE - 1)
                for i in range(3):
                    expert(layer, i, e, i, V.w)
            sp.wait_ge(V.w, 48 * (NOV + 1))
        sp.drain().then_inc(K.jobs_read, 1)

    load_wide(d.w_in_even[0], 0, IN_EVEN)
    load_wide(d.w_out_even[0], 0, D)
    for layer in range(2):
        if layer == 1:
            load_wide(d.w_out_fourier[0], 0, D)
        experts(layer)
    w = d.w_in_2[0]
    load_wide(w, 0, W2_ML)
    load_wide(w, W2_ML, W2_GD)
    load(w[:, W2_Z:], KD)
    load_wide(w, W2_GD, W2_Z)
    load_wide(d.w_out_2[0], 0, D)
    load_wide(d.w_xkv_2[0], 0, 2 * D)
    load_wide(d.w_xq_2[0], 0, D)
    load_wide(d.w_xo_2[0], 0, D)
    load_wide(d.w_ff1_2[0], 0, FF)
    for f in range(FF // WT):
        load(d.w_ff2_2[0][WT * f:WT * f + WT, :], WT // P)


def bass_two_block_kernel(nc, args, out):
    d = Names()
    (d.x, d.w_in_even, d.ret_decay_logit, d.ret_gn_gain, d.sink_logit, d.w_out_even, d.w_out_fourier, d.ln1_gain,
     d.ln1_bias, d.ln2_gain, d.ln2_bias, d.router_coarse_w, d.router_coarse_b, d.router_fine_w, d.router_fine_b,
     d.expert_w_gate, d.expert_w_up, d.expert_w_down, d.mem_2, d.norm_mix_w_2, d.w_in_2, d.na_rel_bias_2,
     d.ml_i_bias_2, d.ml_f_bias_2, d.ml_norm_w_2, d.gdn_conv_w_2, d.gdn_a_log_2, d.gdn_dt_bias_2, d.gdn_norm_w_2,
     d.w_out_2, d.norm_xa_w_2, d.norm_mem_w_2, d.w_xq_2, d.w_xkv_2, d.w_xo_2, d.norm_ffn_w_2, d.w_ff1_2, d.w_ff2_2,
     d.norm_out_w_2, d.c_ident, d.c_ones, d.c_before, d.c_upto, d.c_since, d.c_cos128, d.c_sin128, d.c_cos64,
     d.c_sin64, d.c_dpos, d.c_dneg, d.c_mask, d.c_feat, d.c_cs, d.c_sn, d.c_iota, d.c_iotag, d.c_iotaj,
     d.c_near, d.c_levels_up, d.c_levels_down) = args
    K = Names()
    K.d, K.out, K.rope_count = d, out, 0
    K.CONSTS, K.EVEN_DMAS, K.MOE_DMAS, K.GD_DMAS = 5, 9, 7, 2 + GCT
    K.phases = dict(pe=0, act=0, dve=0, pool=0)
    with ExitStack() as ctx:
        ring = ctx.enter_context(nc.sbuf_tensor("ring", [P, RING, KD * WT], F32))
        K.ring = ring[:, :, :]
        K.x = ctx.enter_context(nc.sbuf_tensor("x", [P, T, D], F32))[:, :, :]
        K.xT = ctx.enter_context(nc.sbuf_tensor("xT", [P, KD, S], F32))[:, :, :]
        K.gains = ctx.enter_context(nc.sbuf_tensor("gains", [P, 2, D], F32))[:, :, :]
        K.ident, K.ones, K.before, K.upto, K.since = (
            ctx.enter_context(nc.sbuf_tensor(name, [P, P], F32))[:, :] for name in ("ident", "ones", "before", "upto", "since"))
        K.lnst = ctx.enter_context(nc.sbuf_tensor("lnst", [P, T, 16], F32))[:, :, :]
        words = ARENA
        arena = ctx.enter_context(nc.sbuf_tensor("arena", [P, words], F32))
        K.ps = ctx.enter_context(nc.psum_tensor("products", [P, 8, WT], F32))[:, :, :]
        K.xs_dram = nc.dram_tensor("slot_rows", ((JOBS + 1) * SB, D), F32).ap()
        K.ys_dram = nc.dram_tensor("expert_rows", (JOBS * SB, D), F32).ap()
        K.bias_dram = nc.dram_tensor("bias_rows", (NAH * 15, HD, 2 * HD - 1), F32).ap()
        K.gate_rows = [d.expert_w_gate[l].rearrange("e k n -> (e k) n") for l in range(2)]
        K.up_rows = [d.expert_w_up[l].rearrange("e k n -> (e k) n") for l in range(2)]
        K.down_rows = [d.expert_w_down[l].rearrange("e k n -> (e k) n") for l in range(2)]

        def carve(at):
            def take(*shape):
                size = int(np.prod(shape))
                ap = arena[:, c.at:c.at + size]
                c.at += size
                assert c.at <= words, (c.at, words)
                names = "abcd"[:len(shape)]
                if len(shape) > 1:
                    ap = ap.rearrange(f"p ({' '.join(names)}) -> p {' '.join(names)}", **dict(zip(names[1:], shape[1:])))
                return ap
            c = take
            c.at = at
            return take
        K.carve = carve
        K.even, K.fourier, K.moe = even_views(K), fourier_views(K), moe_views(K)
        K.second, K.cross, K.ffn = second_views(K), cross_views(K), ffn_views(K)
        K.window, K.near, K.memory = even_attention(K), near_attention(K), cross_attention(K)
        K.probs_base = dict(window=0, near=WQ, memory=WQ + NAH)

        sem = lambda name: ctx.enter_context(nc.semaphore(name))
        K.bank_filled = [sem(f"bank_filled_{i}") for i in range(8)]
        K.bank_evacuated = [sem(f"bank_evacuated_{i}") for i in range(8)]
        K.w_loaded = [sem(f"w_loaded_{i}") for i in range(RING)]
        K.vector_step = sem("vector_step")
        K.scalar_step = sem("scalar_step")
        K.phase_done = sem("phase_done")
        K.w_used = sem("w_used")
        K.more_loaded = [sem(f"more_loaded_{i}") for i in range(3)]
        K.more_used = sem("more_used")
        K.x_loaded = sem("x_loaded")
        K.consts_loaded = sem("consts_loaded")
        K.even_loaded = sem("even_loaded")
        K.mask_loaded = sem("mask_loaded")
        K.gains_loaded = sem("gains_loaded")
        K.norm_done = sem("norm_done")
        K.rope_done = sem("rope_done")
        K.small_dve = sem("small_dve")
        K.small_act = sem("small_act")
        K.decay_exponents = sem("decay_exponents")
        K.decays_ready = sem("decays_ready")
        K.scores_ready = sem("scores_ready")
        K.probs_ready = sem("probs_ready")
        K.fourier_loaded = sem("fourier_loaded")
        K.moe_loaded = sem("moe_loaded")
        K.router_dve = sem("router_dve")
        K.router_act = sem("router_act")
        K.choices_ready = sem("choices_ready")
        K.slots_ready = sem("slots_ready")
        K.rows_stored = sem("rows_stored")
        K.xs_loaded = sem("xs_loaded")
        K.x_scattered = sem("x_scattered")
        K.y_gathered = [sem(f"y_gathered_{t}") for t in range(T)]
        K.bias_loaded = sem("bias_loaded")
        K.par_loaded = sem("par_loaded")
        K.stage_zero = sem("stage_zero")
        K.stage_filled = sem("stage_filled")
        K.stage_stored = sem("stage_stored")
        K.nw_loaded = sem("nw_loaded")
        K.ml_gates = sem("ml_gates")
        K.ml_dve = sem("ml_dve")
        K.ml_act = sem("ml_act")
        K.ml_exponents = sem("ml_exponents")
        K.ml_exps = sem("ml_exps")
        K.ml_weights = sem("ml_weights")
        K.gd_loaded = sem("gd_loaded")
        K.conv_sums = sem("conv_sums")
        K.conv_done = sem("conv_done")
        K.gd_gates = sem("gd_gates")
        K.gd_dve = sem("gd_dve")
        K.gd_act = sem("gd_act")
        K.gd_normed = sem("gd_normed")
        K.gd_exponents = sem("gd_exponents")
        K.gd_operands = sem("gd_operands")
        K.level_masked = sem("level_masked")
        K.z_gate = sem("z_gate")
        K.mem_loaded = sem("mem_loaded")
        K.out_stored = sem("out_stored")

        K.silu_done = sem("silu_done")
        K.jobs_read = sem("jobs_read")
        K.rows_zero = sem("rows_zero")
        K.rows_cleared = sem("rows_cleared")
        K.beyond = []
        for layer in range(2):
            V = Names()
            V.w, V.xs = sem(f"beyond{layer}_weights_loaded"), sem(f"beyond{layer}_rows_loaded")
            V.pe, V.act, V.dve, V.rows = (sem(f"beyond{layer}_{x}") for x in ("tensor", "scalar", "vector", "rows_stored"))
            K.beyond.append(V)

        n = KD + T * len(EVEN_WIDTHS) + 2 * RH
        K.ret_scores = {}
        for h in range(RH + 1):
            if h < RH:
                K.ret_scores[h] = n
                n += T
            if h >= 1:
                n += 1
        K.after_even = n + WQ + WKV + WQ * K.window.per + KD + 2 * T + KD

        block = ctx.enter_context(nc.Block())

        @block.sync
        def _(eng):
            sp_weights(Engine(K, eng, "sp", None))

        @block.tensor
        def _(eng):
            E = Engine(K, eng, "pe", None)
            pe_even(E)
            pe_moe(E, 0)
            E.phase()
            turn_x_pe(E, 2)
            pe_fourier(E)
            pe_moe(E, 1)
            E.phase()
            pe_second(E)
            pe_cross(E)
            pe_ffn(E)

        @block.scalar
        def _(eng):
            E = Engine(K, eng, "act", K.scalar_step)
            act_even(E)
            act_moe(E, 0)
            E.phase()
            copy_out(E, xt_out(K.xT))
            fourier_out(E)
            act_moe(E, 1)
            E.phase()
            act_second(E)
            act_cross(E)
            act_ffn(E)

        @block.vector
        def _(eng):
            E = Engine(K, eng, "dve", K.vector_step)
            dve_even(E)
            dve_moe(E, 0)
            E.phase()
            copy_out(E, xt_out(K.xT))
            fourier_out(E)
            dve_moe(E, 1)
            E.phase()
            dve_second(E)
            dve_cross(E)
            dve_ffn(E)

        @block.gpsimd
        def _(eng):
            E = Engine(K, eng, "pool", None)
            pool_even(E)
            pool_moe(E, 0)
            E.phase()
            E.n += KD
            pool_fourier(E)
            pool_moe(E, 1)
            E.phase()
            pool_second(E)
            pool_cross(E)
            pool_ffn(E)


ARENA = 29976

def shape_tables():
    f = np.float32
    r = np.arange(P)
    c = {}
    c["ident"] = np.eye(P, dtype=f)
    c["ones"] = np.ones((P, P), f)
    c["before"] = (r[:, None] < r[None, :]).astype(f)
    c["upto"] = (r[:, None] <= r[None, :]).astype(f)
    c["since"] = (r[:, None] >= r[None, :]).astype(f)
    for half in (64, 32):
        inv = (f(10000.0) ** (-np.arange(half, dtype=f) / f(half))).astype(f)
        ang = (np.arange(S, dtype=f)[:, None] * inv[None, :]).astype(f).astype(np.float64)
        rows = lambda a: np.ascontiguousarray(a.reshape(T, P, half).transpose(1, 0, 2)).astype(f)
        c[f"cos{2 * half}"], c[f"sin{2 * half}"] = rows(np.cos(ang)), rows(np.sin(ang))
    diff = np.arange(TOEP)[None, :] - (T - 1) * P - r[:, None]
    c["dpos"], c["dneg"] = np.maximum(diff, 0).astype(f), np.maximum(-diff, 0).astype(f)
    rel = np.arange(3 * P)[None, :] - P - r[:, None]
    c["mask"] = np.where(np.abs(rel) <= P, 0.0, NEG).astype(f)
    a = 2 * np.pi * np.outer(np.arange(256), np.arange(256)) / 256
    feat = np.concatenate([np.cos(a), np.sin(a)], 1)
    c["feat"] = feat.reshape(2, P, 512).transpose(1, 0, 2).astype(f)
    a = 2 * np.pi * np.outer(np.arange(S), np.arange(S)) / S
    norm = 1.0 / np.sqrt(S * 256.0)
    c["cs"] = (np.cos(a) * norm).reshape(T, P, S).transpose(1, 0, 2).astype(f)
    c["sn"] = (-np.sin(a) * norm).reshape(T, P, S).transpose(1, 0, 2).astype(f)
    c["iota"] = np.tile(np.arange(NE, dtype=f), (P, 1))
    c["iotag"] = np.tile((np.arange(NE) // (NE // NG)).astype(f), (P, 1))
    c["iotaj"] = np.tile(np.arange(NOV, dtype=f)[None, :, None], (P, 1, NE))
    col = np.arange(HD)
    start = np.clip(col - 8, 0, HD - 16)
    ok = (col[None, :] >= start[:, None]) & (col[None, :] < start[:, None] + 16)
    c["near"] = np.tile(ok.astype(f), (2, 1))
    up = np.zeros((P, LEVELS, P), f)
    for l in range(LEVELS):
        b = 1 << l
        up[:, l, :] = (r[:, None] // (2 * b) == r[None, :] // (2 * b)) & (r[:, None] // b % 2 == 0) & (r[None, :] // b % 2 == 1)
    c["levels_up"] = up
    c["levels_down"] = np.ascontiguousarray(up.transpose(2, 1, 0))
    return {"c_" + k: np.ascontiguousarray(v) for k, v in c.items()}


_INS = ['x', 'w_in_even', 'ret_decay_logit', 'ret_gn_gain', 'sink_logit', 'w_out_even', 'w_out_fourier', 'ln1_gain',
        'ln1_bias', 'ln2_gain', 'ln2_bias', 'router_coarse_w', 'router_coarse_b', 'router_fine_w', 'router_fine_b',
        'expert_w_gate', 'expert_w_up', 'expert_w_down', 'mem_2', 'norm_mix_w_2', 'w_in_2', 'na_rel_bias_2',
        'ml_i_bias_2', 'ml_f_bias_2', 'ml_norm_w_2', 'gdn_conv_w_2', 'gdn_a_log_2', 'gdn_dt_bias_2', 'gdn_norm_w_2',
        'w_out_2', 'norm_xa_w_2', 'norm_mem_w_2', 'w_xq_2', 'w_xkv_2', 'w_xo_2', 'norm_ffn_w_2', 'w_ff1_2', 'w_ff2_2',
        'norm_out_w_2']


def kernel(**inputs):
    import concourse.bacc as _bacc
    from concourse.bass_utils import run_bass_kernel_spmd as _run

    nc = _bacc.Bacc("TRN2", target_bir_lowering=False, num_devices=1)
    arrays, args = {}, []
    for name, a in [(name, inputs[name]) for name in _INS] + list(shape_tables().items()):
        a = np.ascontiguousarray(a)
        arrays[f"in_{name}_dram"] = a
        args.append(nc.dram_tensor(f"in_{name}_dram", a.shape, mybir.dt.from_np(a.dtype), kind="ExternalInput").ap())
    out = nc.dram_tensor("out_0_dram", (1, S, D), F32, kind="ExternalOutput").ap()
    bass_two_block_kernel(nc, args, out)
    r = _run(nc, [arrays], core_ids=[0])
    return r.results[0]["out_0_dram"]
```
